# Optimizing a Trainium2 kernel written in Bass

```python
import jax, jax.numpy as jnp
from jax import lax
import numpy as np
import math

D_MODEL = 1024
BATCH = 1
SEQ = 256
DEPTH = 2

CHUNK = 64
N_MIXERS = 2
N_GLA_LAYERS = (DEPTH + 1) // 2
N_LRU_LAYERS = DEPTH // 2
EPS = 1e-6

GLA_HEADS = 4
GLA_DK = D_MODEL // 2 // GLA_HEADS
GLA_DV = D_MODEL // GLA_HEADS
GLA_QK = GLA_HEADS * GLA_DK
GLA_VD = GLA_HEADS * GLA_DV
GLA_GATE_RANK = 16
GLA_GATE_TAU = 16.0
GLA_IN = 2 * GLA_QK + 2 * GLA_VD + GLA_GATE_RANK

LRU_WIDTH = D_MODEL
LRU_BLOCKS = 4
LRU_BLOCK_W = LRU_WIDTH // LRU_BLOCKS
CONV_W = 4
LRU_C = 8.0

N_EXPERTS = 16
N_GROUPS = 4
EXPERTS_PER_GROUP = N_EXPERTS // N_GROUPS
TOP_K = 2
D_EXPERT = 512


def rmsnorm(x, g):
    x32 = x.astype(jnp.float32)
    inv = lax.rsqrt(jnp.mean(x32 * x32, axis=-1, keepdims=True) + EPS)
    return (x32 * inv).astype(x.dtype) * g

def modulate(h, shift, scale):
    return h * (1 + scale[:, None]) + shift[:, None]

def gla_mixer(h, w_in, w_gate_up, b_gate, norm_g, w_out):
    B, S, _ = h.shape
    N = S // CHUNK
    proj = h @ w_in
    q, k, v, g, a_lr = jnp.split(
        proj, [GLA_QK, 2 * GLA_QK, 2 * GLA_QK + GLA_VD, 2 * GLA_QK + 2 * GLA_VD], axis=-1)
    log_a = jax.nn.log_sigmoid((a_lr @ w_gate_up + b_gate).astype(jnp.float32)) / GLA_GATE_TAU

    def chunked(t, d):
        return t.reshape(B, N, CHUNK, GLA_HEADS, d)

    q = chunked(q, GLA_DK) * (GLA_DK ** -0.5)
    k = chunked(k, GLA_DK)
    v = chunked(v, GLA_DV)
    cum = jnp.cumsum(chunked(log_a, GLA_DK), axis=2)
    total = cum[:, :, -1]
    k_dec = k * jnp.exp(total[:, :, None] - cum).astype(k.dtype)
    gamma = jnp.exp(total).astype(h.dtype)

    def step(s_prev, xs):
        qn, kn, vn, gn = xs
        inter = jnp.einsum('bchk,bhkv->bchv', qn * gn[:, None], s_prev)
        scores = jnp.einsum('bchk,bshk->bhcs', qn, kn)
        intra = jnp.einsum('bhcs,bshv->bchv', scores, vn)
        s_new = gn[..., None] * s_prev + jnp.einsum('bshk,bshv->bhkv', kn, vn)
        return s_new, inter + intra

    s0 = jnp.zeros((B, GLA_HEADS, GLA_DK, GLA_DV), h.dtype)
    xs = (jnp.moveaxis(q, 1, 0), jnp.moveaxis(k_dec, 1, 0),
          jnp.moveaxis(v, 1, 0), jnp.moveaxis(gamma, 1, 0))
    _, o = lax.scan(step, s0, xs)
    o = jnp.moveaxis(o, 0, 1).reshape(B, S, GLA_HEADS, GLA_DV)
    o = rmsnorm(o, norm_g) * jax.nn.silu(g).reshape(B, S, GLA_HEADS, GLA_DV)
    return o.reshape(B, S, GLA_VD) @ w_out

def lru_mixer(h, w_in, conv_w, conv_b, w_r, b_r, w_i, b_i, lam, w_out):
    B, S, _ = h.shape
    proj = h @ w_in
    gate_br, xb = jnp.split(proj, 2, axis=-1)
    xp = jnp.pad(xb, ((0, 0), (CONV_W - 1, 0), (0, 0)))
    xc = conv_b + sum(xp[:, j:j + S] * conv_w[j] for j in range(CONV_W))
    xg = xc.reshape(B, S, LRU_BLOCKS, LRU_BLOCK_W)
    r = jax.nn.sigmoid(jnp.einsum('bshi,hij->bshj', xg, w_r) + b_r).reshape(B, S, LRU_WIDTH)
    i = jax.nn.sigmoid(jnp.einsum('bshi,hij->bshj', xg, w_i) + b_i).reshape(B, S, LRU_WIDTH)
    log_a = (-LRU_C * r.astype(jnp.float32)) * jax.nn.softplus(-lam.astype(jnp.float32))
    a = jnp.exp(log_a)
    mult = jnp.sqrt(-jnp.expm1(2.0 * log_a))
    b = (xc * i).astype(jnp.float32) * mult

    def combine(left, right):
        a1, b1 = left
        a2, b2 = right
        return a1 * a2, a2 * b1 + b2

    _, hs = lax.associative_scan(combine, (a, b), axis=1)
    y = hs.astype(h.dtype) * jax.nn.gelu(gate_br)
    return y @ w_out

def grouped_moe(h, router_w, router_bias, w_gate, w_up, w_down):
    B, S, D = h.shape
    t = h.reshape(-1, D)
    scores = jax.nn.sigmoid((t @ router_w).astype(jnp.float32))
    sel = scores + router_bias.astype(jnp.float32)
    grouped = sel.reshape(-1, N_GROUPS, EXPERTS_PER_GROUP)
    group_score = lax.top_k(grouped, TOP_K)[0].sum(-1)
    grp = jnp.argmax(group_score, axis=-1)
    in_group = jnp.take_along_axis(grouped, grp[:, None, None], axis=1)[:, 0]
    _, local = lax.top_k(in_group, TOP_K)
    expert_idx = grp[:, None] * EXPERTS_PER_GROUP + local
    w = jnp.take_along_axis(scores, expert_idx, axis=1)
    w = w / jnp.sum(w, axis=-1, keepdims=True)
    combine = jnp.sum(jax.nn.one_hot(expert_idx, N_EXPERTS, dtype=jnp.float32) * w[..., None], axis=1)
    combine = combine.astype(t.dtype)
    out = jnp.zeros_like(t)
    for e in range(N_EXPERTS):
        he = jax.nn.silu(t @ w_gate[e]) * (t @ w_up[e])
        out = out + combine[:, e:e + 1] * (he @ w_down[e])
    return out.reshape(B, S, D)

def first_inputs(seed: int = 0) -> dict:
    key = jax.random.key(seed)
    ks = iter(jax.random.split(key, 40))
    f32 = jnp.float32

    def nrm(shape, scale):
        return jax.random.normal(next(ks), shape, f32) * scale

    def gain(shape):
        return 1.0 + nrm(shape, 0.05)

    D = D_MODEL
    p = {}
    p["x"] = nrm((BATCH, SEQ, D), 1.0)
    p["c"] = nrm((BATCH, D), 1.0)
    p["gla_w_in"] = nrm((N_GLA_LAYERS, D, GLA_IN), D ** -0.5)
    p["gla_w_gate_up"] = nrm((N_GLA_LAYERS, GLA_GATE_RANK, GLA_QK), GLA_GATE_RANK ** -0.5)
    p["gla_b_gate"] = nrm((N_GLA_LAYERS, GLA_QK), 0.1)
    p["gla_norm_g"] = gain((N_GLA_LAYERS, GLA_DV))
    p["gla_w_out"] = nrm((N_GLA_LAYERS, GLA_VD, D), GLA_VD ** -0.5)
    p["lru_w_in"] = nrm((N_LRU_LAYERS, D, 2 * LRU_WIDTH), D ** -0.5)
    p["lru_conv_w"] = nrm((N_LRU_LAYERS, CONV_W, LRU_WIDTH), CONV_W ** -0.5)
    p["lru_conv_b"] = nrm((N_LRU_LAYERS, LRU_WIDTH), 0.02)
    p["lru_w_r"] = nrm((N_LRU_LAYERS, LRU_BLOCKS, LRU_BLOCK_W, LRU_BLOCK_W), LRU_BLOCK_W ** -0.5)
    p["lru_b_r"] = nrm((N_LRU_LAYERS, LRU_BLOCKS, LRU_BLOCK_W), 0.02)
    p["lru_w_i"] = nrm((N_LRU_LAYERS, LRU_BLOCKS, LRU_BLOCK_W, LRU_BLOCK_W), LRU_BLOCK_W ** -0.5)
    p["lru_b_i"] = nrm((N_LRU_LAYERS, LRU_BLOCKS, LRU_BLOCK_W), 0.02)
    u = jax.random.uniform(next(ks), (N_LRU_LAYERS, LRU_WIDTH), f32, 0.9, 0.999)
    a_base = u ** (1.0 / LRU_C)
    p["lru_lambda"] = jnp.log(a_base) - jnp.log1p(-a_base)
    p["lru_w_out"] = nrm((N_LRU_LAYERS, LRU_WIDTH, D), LRU_WIDTH ** -0.5)
    p["router_w"] = nrm((D, N_EXPERTS), D ** -0.5)
    p["router_bias"] = nrm((N_EXPERTS,), 0.01)
    p["moe_w_gate"] = nrm((DEPTH, N_EXPERTS, D, D_EXPERT), D ** -0.5)
    p["moe_w_up"] = nrm((DEPTH, N_EXPERTS, D, D_EXPERT), D ** -0.5)
    p["moe_w_down"] = nrm((DEPTH, N_EXPERTS, D_EXPERT, D), D_EXPERT ** -0.5)
    p["norm_mix_g"] = gain((DEPTH, D))
    p["norm_ffn_g"] = gain((DEPTH, D))
    p["ada_w"] = nrm((DEPTH, D, 6 * D), 0.5 * D ** -0.5)
    p["ada_b"] = nrm((DEPTH, 6 * D), 0.02)
    p["final_norm_g"] = gain((D,))
    return p

def first_block(x, c, gla_w_in, gla_w_gate_up, gla_b_gate, gla_norm_g, gla_w_out,
              lru_w_in, lru_conv_w, lru_conv_b, lru_w_r, lru_b_r, lru_w_i, lru_b_i,
              lru_lambda, lru_w_out, router_w, router_bias, moe_w_gate, moe_w_up,
              moe_w_down, norm_mix_g, norm_ffn_g, ada_w, ada_b, final_norm_g):
    cond = jax.nn.silu(c)
    for i in range(DEPTH):
        sh1, sc1, g1, sh2, sc2, g2 = jnp.split(cond @ ada_w[i] + ada_b[i], 6, axis=-1)
        h = modulate(rmsnorm(x, norm_mix_g[i]), sh1, sc1)
        j = i // N_MIXERS
        if i % N_MIXERS == 0:
            mix = gla_mixer(h, gla_w_in[j], gla_w_gate_up[j], gla_b_gate[j],
                            gla_norm_g[j], gla_w_out[j])
        else:
            mix = lru_mixer(h, lru_w_in[j], lru_conv_w[j], lru_conv_b[j], lru_w_r[j],
                            lru_b_r[j], lru_w_i[j], lru_b_i[j], lru_lambda[j], lru_w_out[j])
        x = x + g1[:, None] * mix
        h = modulate(rmsnorm(x, norm_ffn_g[i]), sh2, sc2)
        x = x + g2[:, None] * grouped_moe(h, router_w, router_bias,
                                          moe_w_gate[i], moe_w_up[i], moe_w_down[i])
    return rmsnorm(x, final_norm_g)


DEPTH_2 = 1

GRID_W = 64
CTX_LEN = 256
CONV_W_2 = 3
M_HEADS = 4
M_HEAD_DIM = 128
M_WIDTH = M_HEADS * M_HEAD_DIM
M_CHUNK = 64
A_HEADS = 4
A_SUB_DIM = 64
A_V_DIM = 2 * A_SUB_DIM
A_WIDTH = A_HEADS * A_V_DIM
Q_BLOCK = 128
ROPE_BASE = 10000.0
ROPE_FREQS = A_SUB_DIM // 4
S_HEADS = 8
S_HEAD_DIM = 64
S_WIDTH = S_HEADS * S_HEAD_DIM
S_GROUPS = 2
S_STATE = 128
S_CHUNK = 64
S_CONV_DIM = S_WIDTH + 2 * S_GROUPS * S_STATE
D_FF = 2816
N_BRANCH = 3
N_MOD = 6
IN_SPLITS = (2 * M_WIDTH, M_WIDTH, M_WIDTH, 4 * M_HEADS, A_WIDTH, A_WIDTH, A_WIDTH, S_WIDTH, S_CONV_DIM, 2 * S_HEADS, N_BRANCH * D_MODEL)
D_IN = sum(IN_SPLITS)
NORM_EPS = 1e-6


def rmsnorm_2(x, g):
    xf = x.astype(jnp.float32)
    y = xf * lax.rsqrt(jnp.mean(xf * xf, axis=-1, keepdims=True) + NORM_EPS)
    return (y * g.astype(jnp.float32)).astype(x.dtype)

def modulate_2(h, shift, scale):
    return h * (1.0 + scale) + shift

def dwconv(x, w, b=None):
    k = w.shape[0]
    y = lax.conv_general_dilated(x, w[:, None, :].astype(x.dtype), window_strides=(1,),
                                 padding=[(k // 2, k // 2)], dimension_numbers=('NWC', 'WIO', 'NWC'),
                                 feature_group_count=x.shape[-1])
    if b is not None:
        y = y + b.astype(x.dtype)
    return y

def to_chunks(a, axis, size):
    shp = a.shape
    a = a.reshape(shp[:axis] + (shp[axis] // size, size) + shp[axis + 1:])
    return jnp.moveaxis(a, axis, 0)

def from_chunks(a, axis):
    a = jnp.moveaxis(a, 0, axis)
    shp = a.shape
    return a.reshape(shp[:axis] + (shp[axis] * shp[axis + 1],) + shp[axis + 2:])

def rev(a, axis, on):
    return jnp.flip(a, axis=axis) if on else a

def mlstm_scan(q, k, v, ig, lf, state, emit):
    L = M_CHUNK
    causal = jnp.tril(jnp.ones((L, L), dtype=bool))

    def step(carry, inp):
        C, n, m = carry
        qc, kc, vc, ic, fc = inp
        b = jnp.cumsum(fc, axis=-1)
        g_prev = b + m[..., None]
        d_mat = jnp.where(causal, b[..., :, None] - b[..., None, :] + ic[..., None, :], -jnp.inf)
        m_t = jnp.maximum(g_prev, jnp.max(d_mat, axis=-1))
        m_new = m_t[..., -1]
        w_s = jnp.exp(b[..., -1:] - b + ic - m_new[..., None])
        decay = jnp.exp(b[..., -1] + m - m_new)
        C_new = decay[..., None, None] * C + jnp.einsum('bhs,bhsk,bhsv->bhkv', w_s, kc, vc)
        n_new = decay[..., None] * n + jnp.einsum('bhs,bhsk->bhk', w_s, kc)
        if not emit:
            return (C_new, n_new, m_new), None
        w_prev = jnp.exp(g_prev - m_t)
        w = jnp.exp(d_mat - m_t[..., None]) * jnp.einsum('bhtk,bhsk->bhts', qc, kc)
        num = w_prev[..., None] * jnp.einsum('bhtk,bhkv->bhtv', qc, C) + jnp.einsum('bhts,bhsv->bhtv', w, vc)
        den = w_prev * jnp.einsum('bhtk,bhk->bht', qc, n) + jnp.sum(w, axis=-1)
        h = num / jnp.maximum(jnp.abs(den), jnp.exp(-m_t))[..., None]
        return (C_new, n_new, m_new), h

    xs = (to_chunks(q, 2, L), to_chunks(k, 2, L), to_chunks(v, 2, L), to_chunks(ig, 2, L), to_chunks(lf, 2, L))
    state, h = lax.scan(step, state, xs)
    return (from_chunks(h, 2) if emit else None), state

def mlstm_prep(qk_pre, v_pre, gate_pre, conv_w, conv_b, ig_b, fg_b):
    bsz, t = v_pre.shape[:2]
    qk = jax.nn.silu(dwconv(qk_pre, conv_w, conv_b)).astype(jnp.float32)
    q, k = jnp.split(qk, 2, axis=-1)

    def heads(a):
        return a.astype(jnp.float32).reshape(bsz, t, M_HEADS, M_HEAD_DIM).transpose(0, 2, 1, 3)

    g = gate_pre.astype(jnp.float32).reshape(bsz, t, 2, 2, M_HEADS)
    ig = (g[:, :, :, 0] + ig_b).transpose(2, 0, 3, 1)
    lf = jax.nn.log_sigmoid(g[:, :, :, 1] + fg_b).transpose(2, 0, 3, 1)
    return heads(q), heads(k) * M_HEAD_DIM ** -0.5, heads(v_pre), ig, lf

def mlstm_out(h, o_pre, norm_g):
    bsz, t = o_pre.shape[:2]
    h = rmsnorm_2(h.transpose(0, 2, 1, 3), norm_g.reshape(M_HEADS, M_HEAD_DIM)).reshape(bsz, t, M_WIDTH)
    return (jax.nn.sigmoid(o_pre.astype(jnp.float32)) * h).astype(o_pre.dtype)

def mlstm_mixer(lat, ctx, conv_w, conv_b, ig_b, fg_b, norm_g, emit_ctx):
    q, k, v, ig, lf = mlstm_prep(lat[0], lat[1], lat[3], conv_w, conv_b, ig_b, fg_b)
    qc, kc, vc, igc, lfc = mlstm_prep(ctx[0], ctx[1], ctx[3], conv_w, conv_b, ig_b, fg_b)
    bsz = q.shape[0]
    zeros = (jnp.zeros((bsz, M_HEADS, M_HEAD_DIM, M_HEAD_DIM), jnp.float32),
             jnp.zeros((bsz, M_HEADS, M_HEAD_DIM), jnp.float32),
             jnp.zeros((bsz, M_HEADS), jnp.float32))
    h_lat, h_ctx = 0.0, 0.0
    for d in range(2):
        hc, st = mlstm_scan(rev(qc, 2, d), rev(kc, 2, d), rev(vc, 2, d), rev(igc[d], 2, d), rev(lfc[d], 2, d), zeros, emit_ctx)
        hl, _ = mlstm_scan(rev(q, 2, d), rev(k, 2, d), rev(v, 2, d), rev(ig[d], 2, d), rev(lf[d], 2, d), st, True)
        h_lat = h_lat + rev(hl, 2, d)
        if emit_ctx:
            h_ctx = h_ctx + rev(hc, 2, d)
    out_l = mlstm_out(h_lat, lat[2], norm_g)
    out_c = mlstm_out(h_ctx, ctx[2], norm_g) if emit_ctx else None
    return out_l, out_c

def rope_2d(x, cos, sin):
    shp = x.shape
    xr = x.reshape(shp[:-1] + (2, 2, ROPE_FREQS))
    x1, x2 = xr[..., 0, :], xr[..., 1, :]
    cb, sb = cos[None, :, None, None], sin[None, :, None, None]
    return jnp.stack([x1 * cb - x2 * sb, x2 * cb + x1 * sb], axis=-2).reshape(shp)

def diff_attention(q, k, v, qc, kc, vc, qn_g, kn_g, lam_p, subln_g, lam_init, cos, sin, emit_ctx):
    def heads_qk(a, g, rot):
        bsz, t = a.shape[:2]
        a = rmsnorm_2(a.reshape(bsz, t, A_HEADS, 2, A_SUB_DIM), g).astype(jnp.float32)
        if rot:
            a = rope_2d(a, cos, sin)
        return a.transpose(0, 2, 3, 1, 4)

    def heads_v(a):
        bsz, t = a.shape[:2]
        return a.reshape(bsz, t, A_HEADS, A_V_DIM).transpose(0, 2, 1, 3).astype(jnp.float32)

    lam_p = lam_p.astype(jnp.float32)
    lam = jnp.exp(jnp.sum(lam_p[0] * lam_p[1])) - jnp.exp(jnp.sum(lam_p[2] * lam_p[3])) + lam_init
    scale = A_SUB_DIM ** -0.5

    def attend(qb, kk, vv):
        s = jnp.einsum('bhjqd,bhjkd->bhjqk', qb, kk) * scale
        p = jax.nn.softmax(s, axis=-1)
        return jnp.einsum('bhqk,bhkv->bhqv', p[:, :, 0] - lam * p[:, :, 1], vv)

    k_ctx, v_ctx = heads_qk(kc, kn_g, False), heads_v(vc)
    k_all = jnp.concatenate([heads_qk(k, kn_g, True), k_ctx], axis=3)
    v_all = jnp.concatenate([heads_v(v), v_ctx], axis=2)
    q_blocks = to_chunks(heads_qk(q, qn_g, True), 3, Q_BLOCK)
    o_lat = from_chunks(lax.map(lambda qb: attend(qb, k_all, v_all), q_blocks), 2)

    def post(o):
        o = rmsnorm_2(o.transpose(0, 2, 1, 3), subln_g) * (1.0 - lam_init)
        return o.reshape(o.shape[0], o.shape[1], A_WIDTH).astype(q.dtype)

    out_c = post(attend(heads_qk(qc, qn_g, False), k_ctx, v_ctx)) if emit_ctx else None
    return post(o_lat), out_c

def ssd_scan(x, dt, a_coef, bm, cm, state, emit):
    L = S_CHUNK
    rep = S_HEADS // S_GROUPS
    causal = jnp.tril(jnp.ones((L, L), dtype=bool))[None, :, :, None]

    def step(h, inp):
        xk, dtk, bk, ck = inp
        s = jnp.cumsum(dtk * a_coef, axis=1)
        bh = jnp.repeat(bk, rep, axis=2)
        xdt = xk * dtk[..., None]
        h_new = (jnp.exp(s[:, -1])[..., None, None] * h
                 + jnp.einsum('bsh,bshp,bshn->bhpn', jnp.exp(s[:, -1:] - s), xdt, bh))
        if not emit:
            return h_new, None
        ch = jnp.repeat(ck, rep, axis=2)
        seg = jnp.exp(jnp.where(causal, s[:, :, None] - s[:, None], -jnp.inf))
        y = (jnp.einsum('btsh,bshp->bthp', jnp.einsum('bthn,bshn->btsh', ch, bh) * seg, xdt)
             + jnp.exp(s)[..., None] * jnp.einsum('bthn,bhpn->bthp', ch, h))
        return h_new, y

    xs = (to_chunks(x, 1, L), to_chunks(dt, 1, L), to_chunks(bm, 1, L), to_chunks(cm, 1, L))
    state, y = lax.scan(step, state, xs)
    return (from_chunks(y, 1) if emit else None), state

def ssd_prep(xbc_pre, dt_pre, conv_w, conv_b, dt_bias):
    bsz, t = xbc_pre.shape[:2]
    xbc = jax.nn.silu(dwconv(xbc_pre, conv_w, conv_b)).astype(jnp.float32)
    xs, bm, cm = jnp.split(xbc, [S_WIDTH, S_WIDTH + S_GROUPS * S_STATE], axis=-1)
    dt = jax.nn.softplus(dt_pre.astype(jnp.float32).reshape(bsz, t, 2, S_HEADS) + dt_bias)
    return (xs.reshape(bsz, t, S_HEADS, S_HEAD_DIM), bm.reshape(bsz, t, S_GROUPS, S_STATE),
            cm.reshape(bsz, t, S_GROUPS, S_STATE), dt)

def ssd_out(y, xs, z, d_skip, norm_g):
    bsz, t = z.shape[:2]
    y = (y + d_skip.astype(jnp.float32)[:, None] * xs).reshape(bsz, t, S_WIDTH) * jax.nn.silu(z.astype(jnp.float32))
    y = rmsnorm_2(y.reshape(bsz, t, S_GROUPS, S_WIDTH // S_GROUPS), norm_g.reshape(S_GROUPS, S_WIDTH // S_GROUPS))
    return y.reshape(bsz, t, S_WIDTH).astype(z.dtype)

def ssd_mixer(z, xbc_pre, dt_pre, zc, xbcc_pre, dtc_pre, conv_w, conv_b, dt_bias, a_log, d_skip, norm_g, emit_ctx):
    a_coef = -jnp.exp(a_log.astype(jnp.float32))
    x, bm, cm, dt = ssd_prep(xbc_pre, dt_pre, conv_w, conv_b, dt_bias)
    xc, bc, cc, dtc = ssd_prep(xbcc_pre, dtc_pre, conv_w, conv_b, dt_bias)
    zeros = jnp.zeros((x.shape[0], S_HEADS, S_HEAD_DIM, S_STATE), jnp.float32)
    y_lat, y_ctx = 0.0, 0.0
    for d in range(2):
        yc, st = ssd_scan(rev(xc, 1, d), rev(dtc[:, :, d], 1, d), a_coef[d], rev(bc, 1, d), rev(cc, 1, d), zeros, emit_ctx)
        yl, _ = ssd_scan(rev(x, 1, d), rev(dt[:, :, d], 1, d), a_coef[d], rev(bm, 1, d), rev(cm, 1, d), st, True)
        y_lat = y_lat + rev(yl, 1, d)
        if emit_ctx:
            y_ctx = y_ctx + rev(yc, 1, d)
    out_l = ssd_out(y_lat, x, z, d_skip, norm_g)
    out_c = ssd_out(y_ctx, xc, zc, d_skip, norm_g) if emit_ctx else None
    return out_l, out_c

def gated_merge(y_m, y_a, y_s, gate_pre, w_m, w_a, w_s, w_o):
    g_m, g_a, g_s = jnp.split(jax.nn.sigmoid(gate_pre), N_BRANCH, axis=-1)
    return (g_m * (y_m @ w_m) + g_a * (y_a @ w_a) + g_s * (y_s @ w_s)) @ w_o

def conv_ffn(h, w_up, conv_w, w_down):
    a, g = jnp.split(dwconv(h @ w_up, conv_w), 2, axis=-1)
    return (jax.nn.silu(g) * a) @ w_down

def second_inputs(seed: int = 0) -> dict:
    key = jax.random.key(seed)
    ks = jax.random.split(key, 32)
    f32 = jnp.float32

    def nrm(i, shape, scale):
        return scale * jax.random.normal(ks[i], shape, f32)

    def gain(i, shape):
        return 1.0 + nrm(i, shape, 0.05)

    dt0 = jnp.exp(jax.random.uniform(ks[20], (DEPTH_2, 2, S_HEADS), f32, math.log(1e-3), math.log(1e-1)))
    return {
        "x": nrm(0, (BATCH, SEQ, D_MODEL), 1.0),
        "c": nrm(1, (BATCH, D_MODEL), 1.0),
        "ctx": nrm(2, (BATCH, CTX_LEN, D_MODEL), 1.0),
        "c_ctx": nrm(3, (D_MODEL,), 1.0),
        "w_mod": nrm(4, (DEPTH_2, D_MODEL, N_MOD * D_MODEL), 0.5 * D_MODEL ** -0.5),
        "b_mod": nrm(5, (DEPTH_2, N_MOD * D_MODEL), 0.02),
        "norm1_g": gain(6, (DEPTH_2, D_MODEL)),
        "norm2_g": gain(7, (DEPTH_2, D_MODEL)),
        "w_in": nrm(8, (DEPTH_2, D_MODEL, D_IN), D_MODEL ** -0.5),
        "m_conv_w": nrm(9, (DEPTH_2, CONV_W_2, 2 * M_WIDTH), CONV_W_2 ** -0.5),
        "m_conv_b": nrm(10, (DEPTH_2, 2 * M_WIDTH), 0.02),
        "m_igate_b": nrm(11, (DEPTH_2, 2, M_HEADS), 0.1),
        "m_fgate_b": jnp.linspace(3.0, 6.0, M_HEADS, dtype=f32) + nrm(12, (DEPTH_2, 2, M_HEADS), 0.1),
        "m_norm_g": gain(13, (DEPTH_2, M_WIDTH)),
        "a_qnorm_g": gain(14, (DEPTH_2, A_SUB_DIM)),
        "a_knorm_g": gain(15, (DEPTH_2, A_SUB_DIM)),
        "a_lambda": nrm(16, (DEPTH_2, 4, A_SUB_DIM), 0.1),
        "a_subln_g": gain(17, (DEPTH_2, A_V_DIM)),
        "s_conv_w": nrm(18, (DEPTH_2, CONV_W_2, S_CONV_DIM), CONV_W_2 ** -0.5),
        "s_conv_b": nrm(19, (DEPTH_2, S_CONV_DIM), 0.02),
        "s_dt_bias": dt0 + jnp.log(-jnp.expm1(-dt0)),
        "s_a_log": jnp.log(jax.random.uniform(ks[21], (DEPTH_2, 2, S_HEADS), f32, 1.0, 16.0)),
        "s_d": gain(22, (DEPTH_2, S_HEADS)),
        "s_norm_g": gain(23, (DEPTH_2, S_WIDTH)),
        "w_branch_m": nrm(24, (DEPTH_2, M_WIDTH, D_MODEL), M_WIDTH ** -0.5),
        "w_branch_a": nrm(25, (DEPTH_2, A_WIDTH, D_MODEL), A_WIDTH ** -0.5),
        "w_branch_s": nrm(26, (DEPTH_2, S_WIDTH, D_MODEL), S_WIDTH ** -0.5),
        "w_out": nrm(27, (DEPTH_2, D_MODEL, D_MODEL), D_MODEL ** -0.5),
        "w_up": nrm(28, (DEPTH_2, D_MODEL, 2 * D_FF), D_MODEL ** -0.5),
        "ffn_conv_w": nrm(29, (DEPTH_2, CONV_W_2, 2 * D_FF), CONV_W_2 ** -0.5),
        "w_down": nrm(30, (DEPTH_2, D_FF, D_MODEL), D_FF ** -0.5),
    }

def second_block(x, c, ctx, c_ctx, w_mod, b_mod, norm1_g, norm2_g, w_in, m_conv_w, m_conv_b, m_igate_b, m_fgate_b,
              m_norm_g, a_qnorm_g, a_knorm_g, a_lambda, a_subln_g, s_conv_w, s_conv_b, s_dt_bias, s_a_log, s_d,
              s_norm_g, w_branch_m, w_branch_a, w_branch_s, w_out, w_up, ffn_conv_w, w_down):
    t = x.shape[1]
    rows = t // GRID_W
    row = jnp.repeat(jnp.arange(rows), GRID_W)
    col = jnp.tile(jnp.arange(GRID_W), rows)
    inv_freq = ROPE_BASE ** (-jnp.arange(ROPE_FREQS, dtype=jnp.float32) / ROPE_FREQS)
    ang = jnp.stack([row, col], axis=-1).astype(jnp.float32)[..., None] * inv_freq
    cos, sin = jnp.cos(ang), jnp.sin(ang)
    split_pts = [int(p) for p in np.cumsum(IN_SPLITS)[:-1]]

    xc = ctx
    for l in range(DEPTH_2):
        emit = l < DEPTH_2 - 1
        lam_init = 0.8 - 0.6 * math.exp(-0.3 * l)
        mod = jnp.split(jax.nn.silu(c) @ w_mod[l] + b_mod[l], N_MOD, axis=-1)
        modc = jnp.split(jax.nn.silu(c_ctx) @ w_mod[l] + b_mod[l], N_MOD, axis=-1)

        h = modulate_2(rmsnorm_2(x, norm1_g[l]), mod[0][:, None], mod[1][:, None])
        hc = modulate_2(rmsnorm_2(xc, norm1_g[l]), modc[0], modc[1])
        u = jnp.split(h @ w_in[l], split_pts, axis=-1)
        uc = jnp.split(hc @ w_in[l], split_pts, axis=-1)
        y_m, y_mc = mlstm_mixer(u[0:4], uc[0:4], m_conv_w[l], m_conv_b[l], m_igate_b[l], m_fgate_b[l], m_norm_g[l], emit)
        y_a, y_ac = diff_attention(u[4], u[5], u[6], uc[4], uc[5], uc[6], a_qnorm_g[l], a_knorm_g[l], a_lambda[l],
                                   a_subln_g[l], lam_init, cos, sin, emit)
        y_s, y_sc = ssd_mixer(u[7], u[8], u[9], uc[7], uc[8], uc[9], s_conv_w[l], s_conv_b[l], s_dt_bias[l],
                              s_a_log[l], s_d[l], s_norm_g[l], emit)
        x = x + mod[2][:, None] * gated_merge(y_m, y_a, y_s, u[10], w_branch_m[l], w_branch_a[l], w_branch_s[l], w_out[l])

        h2 = modulate_2(rmsnorm_2(x, norm2_g[l]), mod[3][:, None], mod[4][:, None])
        x = x + mod[5][:, None] * conv_ffn(h2, w_up[l], ffn_conv_w[l], w_down[l])

        if emit:
            xc = xc + modc[2] * gated_merge(y_mc, y_ac, y_sc, uc[10], w_branch_m[l], w_branch_a[l], w_branch_s[l], w_out[l])
            hc2 = modulate_2(rmsnorm_2(xc, norm2_g[l]), modc[3], modc[4])
            xc = xc + modc[5] * conv_ffn(hc2, w_up[l], ffn_conv_w[l], w_down[l])
    return x


def setup_inputs(seed=0):
    out = dict(first_inputs(seed))
    for name, value in second_inputs(seed + 1).items():
        if name != "x":
            out[name + "_2"] = value
    return out


def reference(
    x, c, gla_w_in, gla_w_gate_up, gla_b_gate, gla_norm_g, gla_w_out, lru_w_in, lru_conv_w,
    lru_conv_b, lru_w_r, lru_b_r, lru_w_i, lru_b_i, lru_lambda, lru_w_out, router_w,
    router_bias, moe_w_gate, moe_w_up, moe_w_down, norm_mix_g, norm_ffn_g, ada_w, ada_b,
    final_norm_g, c_2, ctx_2, c_ctx_2, w_mod_2, b_mod_2, norm1_g_2, norm2_g_2, w_in_2,
    m_conv_w_2, m_conv_b_2, m_igate_b_2, m_fgate_b_2, m_norm_g_2, a_qnorm_g_2, a_knorm_g_2,
    a_lambda_2, a_subln_g_2, s_conv_w_2, s_conv_b_2, s_dt_bias_2, s_a_log_2, s_d_2, s_norm_g_2,
    w_branch_m_2, w_branch_a_2, w_branch_s_2, w_out_2, w_up_2, ffn_conv_w_2, w_down_2,
):
    x = first_block(
        x, c, gla_w_in, gla_w_gate_up, gla_b_gate, gla_norm_g, gla_w_out, lru_w_in, lru_conv_w,
        lru_conv_b, lru_w_r, lru_b_r, lru_w_i, lru_b_i, lru_lambda, lru_w_out, router_w,
        router_bias, moe_w_gate, moe_w_up, moe_w_down, norm_mix_g, norm_ffn_g, ada_w, ada_b,
        final_norm_g,
    )
    return second_block(
        x, c_2, ctx_2, c_ctx_2, w_mod_2, b_mod_2, norm1_g_2, norm2_g_2, w_in_2, m_conv_w_2,
        m_conv_b_2, m_igate_b_2, m_fgate_b_2, m_norm_g_2, a_qnorm_g_2, a_knorm_g_2, a_lambda_2,
        a_subln_g_2, s_conv_w_2, s_conv_b_2, s_dt_bias_2, s_a_log_2, s_d_2, s_norm_g_2,
        w_branch_m_2, w_branch_a_2, w_branch_s_2, w_out_2, w_up_2, ffn_conv_w_2, w_down_2,
    )


_drawn_inputs = setup_inputs


def setup_inputs(seed=0):
    import zlib

    import numpy as np

    out = dict(_drawn_inputs(seed))
    spreads = {}
    factors = {'lru_b_r': 8.0,
     'lru_b_i': 8.0,
     'norm1_g_2': 3.977,
     'norm2_g_2': 3.55,
     'm_conv_b_2': 64.0,
     'm_igate_b_2': 48.711,
     'm_norm_g_2': 8.0,
     'a_qnorm_g_2': 8.0,
     'a_knorm_g_2': 8.0,
     'a_lambda_2': 8.0,
     'a_subln_g_2': 8.0,
     's_conv_b_2': 8.0,
     's_d_2': 64.0,
     's_norm_g_2': 6.748}
    for name, (base, spread) in spreads.items():
        noise = np.random.default_rng([zlib.crc32(name.encode()), seed]).standard_normal(out[name].shape)
        drawn = base * np.exp(spread * noise) if base else spread * noise
        out[name] = __import__('jax').numpy.asarray(drawn.astype(out[name].dtype))
    for name, factor in factors.items():
        out[name] = (out[name] * factor).astype(out[name].dtype)
    return out
```

```python
import math
from contextlib import ExitStack

import numpy as np

import concourse.bass as bass
from concourse import mybir

F32 = mybir.dt.float32
ALU = mybir.AluOpType
ACT = mybir.ActivationFunctionType
AX = mybir.AxisListType.X

P = 128
D = 1024
KT = D // P
T = 256
TT = T // P
TC = 512
EPS = 1e-6
EXPERTS, GROUPS, D_EXPERT = 16, 4, 512
FT = D_EXPERT // P
GLA_H, GLA_CHUNK, GLA_DV = 4, 64, 256
CHUNKS = T // GLA_CHUNK
M_H, A_H, S_H, SUB = 4, 4, 8, 64
D_FF = 2816
FF_PAIRS = D_FF // 256
LAM_INIT = 0.8 - 0.6 * math.exp(0.0)
U_QK, U_V, U_O, U_G, U_AQ, U_AK, U_AV, U_Z, U_XBC, U_DT, U_MERGE = np.cumsum(
    [0, 1024, 512, 512, 16, 512, 512, 512, 512, 1024, 16]).tolist()

RING = 6
SLOT = 2048

C_ID, C_ONE, C_BLK, C_ROT, C_COS, C_SIN, C_FWD, C_BWD, C_SGN, C_EPS, C_IOTA, C_TRI, C_END = np.cumsum(
    [0, 128, 128, 128, 128, 256, 256, 128, 128, 1, 1, 4, 16]).tolist()


def constants():
    c = np.zeros((P, C_END), np.float32)
    c[:, C_ID:C_ID + P] = np.eye(P)
    c[:, C_ONE:C_ONE + P] = 1.0
    half = np.arange(P) // SUB
    c[:, C_BLK:C_BLK + P] = half[:, None] == half[None, :]
    inv_freq = np.float32(10000.0) ** (-np.arange(16, dtype=np.float32) / np.float32(16))
    t = np.arange(T)
    for p in range(P):
        f = p % SUB
        pos = (t // 64 if f < 32 else t % 64).astype(np.float32)
        ang = pos * inv_freq[f % 16]
        c[p, C_COS:C_COS + T] = np.cos(ang)
        c[p, C_SIN:C_SIN + T] = np.sin(ang)
        if f % 32 < 16:
            c[p + 16, C_ROT + p] = -1.0
        else:
            c[p - 16, C_ROT + p] = 1.0
    s = np.arange(P)
    c[:, C_FWD:C_FWD + P] = s[:, None] <= s[None, :]
    c[:, C_BWD:C_BWD + P] = s[:, None] >= s[None, :]
    c[:, C_SGN] = np.where(s < 64, -1.0, 1.0)
    c[:, C_EPS] = EPS
    c[:, C_IOTA:C_IOTA + 4] = [4, 3, 2, 1]
    c[:, C_TRI:C_TRI + 16] = (np.arange(4)[None, :] < np.arange(4)[:, None]).reshape(-1)
    return c


VECTORS = [("c", 8), ("c_2", 8), ("c_ctx_2", 8), ("ada_b", 96), ("b_mod_2", 48), ("norm_mix_g", 16),
           ("norm_ffn_g", 16), ("final_norm_g", 8), ("gla_b_gate", 4), ("gla_norm_g", 2), ("lru_conv_w", 32),
           ("lru_conv_b", 8), ("lru_b_r", 8), ("lru_b_i", 8), ("lru_lambda", 8), ("norm1_g_2", 8),
           ("norm2_g_2", 8), ("m_conv_w_2", 24), ("m_conv_b_2", 8), ("m_norm_g_2", 4), ("a_qnorm_g_2", 1),
           ("a_knorm_g_2", 1), ("a_subln_g_2", 1), ("s_conv_w_2", 24), ("s_conv_b_2", 8), ("s_norm_g_2", 4),
           ("ffn_conv_w_2", 132)]
COL, N_ROWS = {}, 0
for _name, _rows in VECTORS:
    COL[_name] = N_ROWS
    N_ROWS += _rows
ROW_TILES = -(-N_ROWS // P)


class Count:

    def __init__(self):
        self.at = {}

    def __call__(self, sem, by=1):
        self.at[sem.name] = self.at.get(sem.name, 0) + by
        return self.at[sem.name]

    def now(self, sem):
        return self.at.get(sem.name, 0)


class Banks:

    def __init__(self, banks, ready, taken):
        self.banks, self.ready, self.taken, self.n = banks, ready, taken, 0

    def fill(self, pe):
        if self.n >= len(self.banks):
            pe.wait_ge(self.taken, self.n - len(self.banks) + 1)
        return self.banks[self.n % len(self.banks)]

    def read(self, eng):
        eng.wait_ge(self.ready, self.n + 1)
        return self.banks[self.n % len(self.banks)]

    def step(self):
        self.n += 1


def build(nc, A, out):
    f_rows = "(k p) n -> p k n"

    def wide(w, col, kt=KT):
        n = SLOT // kt
        return w[:, col:col + n].rearrange(f_rows, p=P), kt, n

    def tall(w, row):
        return w[row:row + 256, :].rearrange(f_rows, p=P), 2, D

    ada, w_mod, gin, lin_w = A["ada_w"], A["w_mod_2"][0], A["gla_w_in"][0], A["lru_w_in"][0]
    win, w_up, w_down = A["w_in_2"][0], A["w_up_2"][0], A["w_down_2"][0]

    def plan():
        for j in range(24):
            yield "mod", wide(ada[0], 256 * j)
        for j in range(12):
            yield "gla_in", wide(gin, 256 * j)
        for j in range(4):
            yield "gla_out", wide(A["gla_w_out"][0], 256 * j)
        yield "moe", 0
        for j in (4, 5, 6, 7, 0, 1, 2, 3):
            yield "lru_in", wide(lin_w, 256 * j)
        for w in ("lru_w_r", "lru_w_i"):
            yield "lru_gate", (A[w][0].rearrange("b (k p) j -> p (b k) j", p=P), 8, 256)
        for j in range(4):
            yield "lru_out", wide(A["lru_w_out"][0], 256 * j)
        yield "moe", 1
        for col, n in ((U_QK, 4), (U_V, 2), (U_O, 2), (U_AQ, 2), (U_AK, 2), (U_AV, 2), (U_XBC, 4), (U_Z, 2),
                       (U_MERGE, 12)):
            for j in range(n):
                yield "u", wide(win, col + 256 * j)
        for half in range(2):
            for w in ("w_branch_m_2", "w_branch_a_2", "w_branch_s_2"):
                yield "branch", wide(A[w][0], 512 * half, 4)
        for j in range(4):
            yield "w_out", wide(A["w_out_2"][0], 256 * j)
        for j in range(FF_PAIRS):
            yield "ff_a", wide(w_up, 256 * j)
            yield "ff_g", wide(w_up, D_FF + 256 * j)
            yield "ff_down", tall(w_down, 256 * j)

    SLOTS = []
    for what, load in plan():
        SLOTS += [(what, load)] if what != "moe" else [("moe", load)] * (6 * EXPERTS)
    freed = {}

    with ExitStack() as ctx:
        def sb(name, shape):
            return ctx.enter_context(nc.sbuf_tensor(name, shape, F32))

        sems = {}

        def sem(name):
            if name not in sems:
                sems[name] = ctx.enter_context(nc.semaphore(name))
            return sems[name]

        ring = sb("ring", [P, RING, SLOT])
        con = sb("con", [P, C_END])
        cols = sb("cols", [P, ROW_TILES * P])
        x = sb("x", [P, KT, T])
        hh = sb("hh", [P, KT, TC])
        mods = sb("mods", [P, 4, 48])
        gains = sb("gains", [P, 6, KT])
        cond = sb("cond", [P, 24])
        cond_t = sb("cond_t", [P, 24])
        lnt = sb("lnt", [P, TC])
        inv = sb("inv", [P, 4, TC])
        w_lr = sb("w_lr", [P, KT, 16])
        w_gate_up = sb("w_gate_up", [16, 512])
        w_router = sb("w_router", [P, KT, 16])
        router_b = sb("router_b", [P, 16])
        w_small = sb("w_small", [P, 2, KT, 16])
        bias_i = sb("bias_i", [64, 1])
        bias_f = sb("bias_f", [P, 1])
        decay = sb("decay", [P, 2])
        lam_p = sb("lam_p", [P, 256])
        d_skip = sb("d_skip", [P, 4])
        misc = sb("misc", [P, 64])
        ROOM = 28200
        work = sb("work", [P, ROOM])

        used = [0, 0]

        def room(*shape):
            n = int(np.prod(shape))
            a = work[:, used[0]:used[0] + n]
            used[0] += n
            assert used[0] <= ROOM, (used, shape)
            if len(shape) == 1:
                return a
            names = "abcd"[:len(shape)]
            return a.rearrange(f"p ({' '.join(names)}) -> p {' '.join(names)}",
                               **{k: v for k, v in zip(names, shape)})

        def again(at=0):
            used[0] = at

        ident, ones = con[:, C_ID:C_ID + P], con[:, C_ONE:C_ONE + P]
        blk, rot = con[:, C_BLK:C_BLK + P], con[:, C_ROT:C_ROT + P]
        cos, sin = con[:, C_COS:C_COS + T], con[:, C_SIN:C_SIN + T]
        fwd, bwd = con[:, C_FWD:C_FWD + P], con[:, C_BWD:C_BWD + P]
        one = con[:, C_ONE:C_ONE + 1]
        sgn, eps = con[:, C_SGN:C_SGN + 1], con[:, C_EPS:C_EPS + 1]

        def col(name, j=0, n=1):
            return cols[:, COL[name] + j:COL[name] + j + n]

        banks = [ctx.enter_context(nc.psum_tensor(f"bank{i}", [P, 512], F32))[:, :] for i in range(8)]

        def act_banks():
            return Banks(banks[:4], sem("act_tile_ready"), sem("act_tile_taken"))

        def dve_banks():
            return Banks(banks[4:], sem("dve_tile_ready"), sem("dve_tile_taken"))

        again()
        prow, x_in, c_in = room(ROW_TILES, P), room(TT, D), room(TT, D)
        again()
        sq = room(KT, TC)
        base = used[0]
        g_q, g_k, g_v, g_g = room(4, T), room(4, T), room(TT, D), room(8, T)
        g_z, g_l, g_kt, g_lr = room(4, T), room(4, T), room(TT, 512), room(T)
        g_s, g_o = room(CHUNKS, GLA_H, GLA_DV), room(8, T)
        g_gam = room(4, CHUNKS)
        again(base)
        e_cb, e_th, e_t1, e_he, e_ct = room(EXPERTS, T), room(2, T), room(T), room(FT, T), room(T)
        e_zero = room(512)
        r_s, r_sel, r_pair, r_gs, r_gm, r_key, r_km, r_oh = (room(32), room(32), room(8, 6), room(8), room(2), room(8),
                                                             room(2), room(8))
        r_a, r_b, r_rank, r_w, r_den, r_comb = room(8, 16), room(8, 16), room(32), room(32), room(2), room(32)
        side, side_acc, side_raw = room(2, KT, 384), room(9, P), room(EXPERTS + 1, 9)
        again(base)
        mod_acc = room(2, 2, P)
        again(0)
        l_g, l_xb, l_x, l_r, l_i, l_a, l_m, l_h = (room(8, T), room(8, T + 3), room(8, T), room(8, T), room(8, T),
                                                   room(8, T), room(8, T), room(8, T))
        again(0)
        y_m, y_a, y_s = room(4, T), room(4, T), room(4, T)
        row_r, row_m, col_c, col_dt = room(T), room(T), room(4, P), room(4, P)
        base2 = used[0]
        sq2 = room(KT, TC)
        again(base2)
        m_pad, m_x, m_v, m_o, m_h = room(8, 2, 258), room(8, TC), room(4, 512), room(4, T), room(4, T)
        m_qm, m_e, m_rc = room(2, 4, T), room(2, 4, T), room(3, T)
        upper = used[0]
        z_i, z_f, z_sp, z_e, z_inc, z_ir, z_fs, z_ms, z_one = [room(TC) for _ in range(9)]
        wp_i, wp_f = room(KT, 64), room(KT, P)
        again(upper)
        a_q, a_k, a_v = room(4, T), room(4, TC), room(4, 512)
        again(base2)
        a_t, a_u, a_p0, a_p1, a_pt, a_o, a_st = (room(TC), room(TC), room(TC), room(TC), room(2, 4, T), room(4, T),
                                                 room(8))
        s_pad, s_z, s_x, s_xt = room(8, 2, 258), room(4, T), room(8, TC), room(4, 512)
        assert used[0] <= upper
        again(base2)
        s_y, s_qm, s_e = room(4, T), room(2, 4, T), room(4, T)
        sq_s = s_qm[:, 1]
        again(base2)
        g_acc, g_tmp = room(8, T), room(T)
        again(upper)
        g_th = room(24, T)
        again(base2)
        f_pad, f_c, f_th, f_he, f_zero = room(4, 258), room(4, T), room(2, T), room(2, 2, T), room(512)
        o_tok = room(TT, D)
        f_sq = room(KT, T)

        s = {n: sem(n) for n in (
            "params", "dve_step", "act_step", "pool_step", "columns", "cond", "norm_sq", "norm_inv", "normed",
            "mod_used", "x_in")}
        landed = [sem(f"slot_landed{i}") for i in range(RING)]
        marks = {}

        loads = [(con[:, :], A["consts"])]
        for name, rows in VECTORS:
            v = A[name]
            dims = len(v.shape)
            flat = v if dims == 1 else v.rearrange(" ".join("abcd"[:dims]) + " -> (" + " ".join("abcd"[:dims]) + ")")
            if name in ("a_qnorm_g_2", "a_knorm_g_2"):
                r = COL[name]
                for half in range(2):
                    loads.append((prow[r % P:r % P + 1, r // P, half * SUB:(half + 1) * SUB],
                                  flat.rearrange("(o n) -> o n", o=1)))
                continue
            m = flat.rearrange("(r n) -> r n", n=P)
            r, done = COL[name], 0
            while done < rows:
                k = min(rows - done, P - (r + done) % P)
                at = (r + done) % P
                loads.append((prow[at:at + k, (r + done) // P, :], m[done:done + k, :]))
                done += k
        loads.append((x_in, A["x"][0].rearrange("(t p) n -> p t n", p=P)))
        loads.append((c_in, A["ctx_2"][0].rearrange("(t p) n -> p t n", p=P)))
        loads.append((w_lr[:, :, :], gin[:, 3072:3088].rearrange(f_rows, p=P)))
        loads.append((w_gate_up[:, :], A["gla_w_gate_up"][0]))
        loads.append((w_router[:, :, :], A["router_w"].rearrange(f_rows, p=P)))
        loads.append((router_b[:, :], A["router_bias"].rearrange("(o n) -> o n", o=1).to_broadcast([P, 16])))
        loads.append((w_small[:, 0, :, :], win[:, U_G:U_G + 16].rearrange(f_rows, p=P)))
        loads.append((w_small[:, 1, :, :], win[:, U_DT:U_DT + 16].rearrange(f_rows, p=P)))
        loads.append((lam_p[:, :], A["a_lambda_2"][0].rearrange("(o a) b -> o (a b)", o=1).to_broadcast([P, 256])))
        column = lambda v, n: v.rearrange("(n o) -> n o", o=1)
        later = []
        for d in range(2):
            later.append((bias_i[32 * d:32 * d + 4, :], column(A["m_igate_b_2"][0, d], 4)))
            later.append((bias_f[32 * d:32 * d + 4, :], column(A["m_fgate_b_2"][0, d], 4)))
            later.append((bias_f[64 + 32 * d:64 + 32 * d + 8, :], column(A["s_dt_bias_2"][0, d], 8)))
            later.append((decay[64 + 32 * d:64 + 32 * d + 8, 0:1], column(A["s_a_log_2"][0, d], 8)))
        for hd in range(S_H):
            loads.append((d_skip[64 * (hd % 2):64 * (hd % 2) + 64, hd // 2:hd // 2 + 1],
                          A["s_d_2"][0, hd:hd + 1].rearrange("(n o) -> n o", o=1).to_broadcast([64, 1])))
        early, loads = loads[:4], loads[4:]
        n_params = 16 * (len(loads) + len(later))

        block = ctx.enter_context(nc.Block())

        @block.tensor
        def _(pe):
            c = Count()
            to_act, to_dve = act_banks(), dve_banks()
            slot = [0]

            def weights(what, kt):
                g = slot[0]
                assert SLOTS[g][0] == what, (g, SLOTS[g][0], what)
                pe.wait_ge(landed[g % RING], 16 * (g // RING + 1))
                slot[0] += 1
                return ring[:, g % RING, :].rearrange("p (k n) -> p k n", k=kt)

            def free_slot(sem_, value, back=1):
                freed[slot[0] - back] = (sem_, value)

            def close(banks_, ins):
                ins.then_inc(banks_.ready, 1)
                banks_.step()

            def linear(what, to, rhs, n, kt=KT, tiles=2, width=None):
                w = weights(what, kt)
                for m in range(tiles):
                    ps = to.fill(pe)
                    for k in range(kt):
                        ins = pe.matmul(ps[:, 0:n], w[:, k, m * P:(m + 1) * P], rhs(k), start=k == 0, stop=k == kt - 1)
                    close(to, ins)
                free_slot(to.ready, to.n)

            def by_token(what, to, src, tiles):
                w = weights(what, KT)
                for t in range(tiles):
                    ps = to.fill(pe)
                    for k in range(KT):
                        ins = pe.matmul(ps[:, 0:256], src(k, t), w[:, k, :], start=k == 0, stop=k == KT - 1)
                    close(to, ins)
                free_slot(to.ready, to.n)

            def norm_sum(parts, n, lhs=ones):
                pe.wait_ge(s["norm_sq"], c(s["norm_sq"]))
                ps = to_act.fill(pe)
                for k, part in enumerate(parts):
                    ins = pe.matmul(ps[:, 0:n], lhs, part, start=k == 0, stop=k == len(parts) - 1)
                close(to_act, ins)

            pe.wait_ge(sem("conditions"), 16 * len(early))
            ps = to_dve.fill(pe)
            close(to_dve, pe.transpose(ps[:, 0:24], prow[0:24, 0, :], ident[0:24, 0:24]))
            pe.wait_ge(s["params"], n_params)
            ps = to_dve.fill(pe)
            for i in range(ROW_TILES):
                n = min(P, N_ROWS - i * P)
                ins = pe.transpose(ps[:, i * P:i * P + n], prow[0:n, i, :], ident[0:n, 0:n])
            close(to_dve, ins)
            for src in (x_in, c_in):
                for pair in range(4):
                    ps = to_dve.fill(pe)
                    for k in range(2):
                        for t in range(TT):
                            ins = pe.transpose(ps[:, (2 * k + t) * P:(2 * k + t + 1) * P],
                                               src[:, t, (2 * pair + k) * P:(2 * pair + k + 1) * P], ident)
                    close(to_dve, ins)
            for j in range(24):
                pe.wait_ge(sem("mod_part"), j + 1)
                ps = to_dve.fill(pe)
                for m in range(2):
                    ins = pe.transpose(ps[:, m * P:(m + 1) * P], mod_acc[:, j % 2, m, :], ident)
                close(to_dve, ins)
                slot[0] += 1
                freed[j] = (to_dve.ready, to_dve.n)

            h = lambda k: hh[:, k, T:TC]
            token = lambda k, t: hh[:, k, t * P:(t + 1) * P]
            hb = lambda k: hh[:, k, :]

            def norm(n=T):
                norm_sum([sq[:, k, 0:n] for k in range(KT)], n)
                pe.wait_ge(s["normed"], c(s["normed"]))

            norm()
            for j in range(4):
                linear("gla_in", to_act, h, T)
            for j in range(4):
                by_token("gla_in", to_act, lambda k, t: hh[:, k, T + t * P:T + (t + 1) * P], TT)
            for j in range(4):
                linear("gla_in", to_act, h, T)
            ps = to_act.fill(pe)
            for k in range(KT):
                ins = pe.matmul(ps[0:16, 0:T], w_lr[:, k, :], h(k), start=k == 0, stop=k == KT - 1)
            close(to_act, ins)
            pe.wait_ge(to_act.taken, to_act.n)
            for j in range(4):
                ps = to_dve.fill(pe)
                close(to_dve, pe.matmul(ps[:, 0:T], w_gate_up[:, j * P:(j + 1) * P], g_lr[0:16, :],
                                        start=True, stop=True))
            pe.wait_ge(sem("gla_kdec"), 1)
            for t in range(TT):
                ps = to_dve.fill(pe)
                for hd in range(GLA_H):
                    ins = pe.transpose(ps[:, hd * P:(hd + 1) * P], g_z[:, hd, t * P:(t + 1) * P], ident)
                close(to_dve, ins)
            pe.wait_ge(to_dve.taken, to_dve.n)
            for n in range(CHUNKS):
                rows = slice(64 * (n % 2), 64 * (n % 2) + 64)
                for pair in range(2):
                    ps = to_dve.fill(pe)
                    for q in range(2):
                        hd = 2 * pair + q
                        ins = pe.matmul(ps[:, q * 256:(q + 1) * 256], g_kt[rows, n // 2, hd * P:(hd + 1) * P],
                                        g_v[rows, n // 2, hd * 256:(hd + 1) * 256], start=True, stop=True)
                    close(to_dve, ins)
            pe.wait_ge(to_dve.taken, to_dve.n)
            for hd in range(GLA_H):
                ps = to_dve.fill(pe)
                for j in range(2):
                    for n in range(CHUNKS):
                        ins = pe.matmul(ps[:, j * T + n * 64:j * T + (n + 1) * 64], g_s[:, n, hd, j * P:(j + 1) * P],
                                        g_q[:, hd, n * 64:(n + 1) * 64], start=True, stop=True)
                close(to_dve, ins)
            for hd in range(GLA_H):
                norm_sum([sq[:, j, 0:T] for j in (2 * hd, 2 * hd + 1)], T)
            pe.wait_ge(sem("gla_y"), 1)
            for j in range(4):
                linear("gla_out", to_dve, lambda k: g_o[:, k, :], T)

            def side_sums(e):
                pe.wait_ge(sem("side_part"), e + 1)
                pe.wait_ge(sem("hidden_ready"), 4 * e + 3)
                for b in range(3):
                    for i in range(4 * b, min(4 * b + 4, 9)):
                        ins = pe.transpose(banks[b][:, (i - 4 * b) * P:(i - 4 * b + 1) * P], side_acc[:, i, :], ident)
                ins.then_inc(sem("side_turned"), 1)

            def experts(layer):
                norm()
                ps = to_act.fill(pe)
                for t in range(TT):
                    for k in range(KT):
                        ins = pe.matmul(ps[:, t * 16:(t + 1) * 16], hh[:, k, T + t * P:T + (t + 1) * P],
                                        w_router[:, k, :], start=k == 0, stop=k == KT - 1)
                close(to_act, ins)
                marks["logits", layer] = to_act.n
                pe.wait_ge(sem("combine"), layer + 1)
                ps = to_dve.fill(pe)
                for t in range(TT):
                    ins = pe.matmul(ps[0:16, t * P:(t + 1) * P], r_comb[:, t * 16:(t + 1) * 16], ident,
                                    start=True, stop=True)
                close(to_dve, ins)
                pe.wait_ge(to_dve.taken, to_dve.n)
                for e in range(0, EXPERTS, 2):
                    ps = to_dve.fill(pe)
                    for q in range(2):
                        ins = pe.matmul(ps[:, q * T:(q + 1) * T],
                                        ident[0:16, e + q:e + q + 1].to_broadcast([16, P]), e_ct[0:16, :],
                                        start=True, stop=True)
                    close(to_dve, ins)
                pe.wait_ge(to_dve.taken, to_dve.n)
                pe.wait_ge(to_act.taken, to_act.n)
                for b in range(4):
                    pe.matmul(banks[4 + b][:, :], e_zero[:, 0:P], e_zero[:, :], start=True, stop=False,
                              skip_group_check=True)
                g0, first = slot[0], layer * EXPERTS
                gate_used, gu_ready, down_used = sem("gate_used"), sem("gate_up_ready"), sem("down_used")
                gu_taken, he_ready = sem("gate_up_taken"), sem("hidden_ready")

                def landed_at(j, e):
                    g = g0 + j
                    assert SLOTS[g][0] == "moe"
                    pe.wait_ge(landed[g % RING], 16 * (g // RING + 1) + 16 * e)
                    return ring[:, g % RING, :]

                with pe.Fori(0, EXPERTS) as e:
                    for pair in range(2):
                        for up in range(2):
                            w = landed_at(2 * pair + up, e).rearrange("p (k n) -> p k n", k=KT)
                            for q in range(2):
                                f = 2 * pair + q
                                if not up:
                                    pe.wait_ge(gu_taken, 4 * (e + first) + f + 1)
                                    if layer == 0 and f < 3:
                                        pe.wait_ge(sem("side_read"), 3 * e + f + 1)
                                for k in range(KT):
                                    ins = pe.matmul(banks[f][:, up * T:(up + 1) * T], w[:, k, q * P:(q + 1) * P],
                                                    h(k), start=k == 0, stop=k == KT - 1)
                                if up:
                                    ins.then_inc(gu_ready, 1)
                            if not up:
                                ins.then_inc(gate_used, 1)
                    for pair in range(2):
                        w = landed_at(4 + pair, e).rearrange("p (k n) -> p k n", k=2)
                        for q in range(2):
                            f = 2 * pair + q
                            pe.wait_ge(he_ready, 4 * (e + first) + f + 1)
                            for m in range(KT):
                                ins = pe.matmul(banks[4 + m // 2][:, (m % 2) * T:(m % 2 + 1) * T],
                                                w[:, q, m * P:(m + 1) * P], e_he[:, f, :], start=False, stop=False,
                                                skip_group_check=True)
                        ins.then_inc(down_used, 1)
                        if layer == 0 and pair == 0:
                            side_sums(e)
                if layer == 0:
                    pe.wait_ge(gu_taken, 4 * EXPERTS + 4)
                    pe.wait_ge(sem("side_part"), EXPERTS + 1)
                    pe.wait_ge(sem("side_read"), 3 * EXPERTS + 3)
                    for b in range(3):
                        for i in range(4 * b, min(4 * b + 4, 9)):
                            ins = pe.transpose(banks[b][:, (i - 4 * b) * P:(i - 4 * b + 1) * P], side_acc[:, i, :],
                                               ident)
                    ins.then_inc(sem("side_turned"), 1)
                for b in range(4):
                    ins = pe.matmul(banks[4 + b][:, :], e_zero[:, 0:P], e_zero[:, :], start=False, stop=True,
                                    skip_group_check=True)
                ins.then_inc(sem("experts_done"), 1)
                slot[0] += 6 * EXPERTS
                last = first + EXPERTS
                for j, (sm, v) in enumerate(((gate_used, 2 * last - 1), (gu_ready, 4 * last - 2),
                                             (gate_used, 2 * last), (gu_ready, 4 * last),
                                             (down_used, 2 * last - 1), (down_used, 2 * last))):
                    freed[slot[0] - 6 + j] = (sm, v)

            experts(0)

            norm()
            for j in range(8):
                if j == 0:
                    marks["lru_xb"] = to_act.n
                linear("lru_in", to_act, h, T)
            pe.wait_ge(sem("lru_conv"), 8)
            for gate in range(2):
                w = weights("lru_gate", 8)
                for m in range(8):
                    ps = to_act.fill(pe)
                    for k in range(2):
                        b = m // 2
                        ins = pe.matmul(ps[:, 0:T], w[:, 2 * b + k, (m % 2) * P:(m % 2 + 1) * P],
                                        l_x[:, 2 * b + k, :], start=k == 0, stop=k == 1)
                    close(to_act, ins)
                free_slot(to_act.ready, to_act.n)
            marks["lru_gates"] = to_act.n
            pe.wait_ge(sem("lru_y"), 1)
            for j in range(4):
                linear("lru_out", to_dve, lambda k: l_h[:, k, :], T)
            experts(1)
            norm_sum([sq[:, k, 0:T] for k in range(KT)], T)

            norm_sum([sq2[:, k, 0:T] for k in range(KT)], T)
            norm_sum([sq2[:, k, T:TC] for k in range(KT)], T)
            pe.wait_ge(s["normed"], c(s["normed"]))
            pe.wait_ge(sem("small_w"), 1)
            for w, n in ((wp_i, 64), (wp_f, P)):
                ps = to_act.fill(pe)
                for k in range(KT):
                    ins = pe.matmul(ps[0:n, :], w[:, k, :], hb(k), start=k == 0, stop=k == KT - 1)
                close(to_act, ins)
            for j in range(2):
                linear("u", to_act, h, T)
            for j in range(2):
                linear("u", to_act, hb, TC)
            marks["m_qk_in"] = to_act.n
            pe.wait_ge(sem("gate_rows"), 1)
            for src in (z_inc, z_sp):
                ps = to_dve.fill(pe)
                for t in range(4):
                    ins = pe.transpose(ps[:, t * P:(t + 1) * P], src[:, t * P:(t + 1) * P], ident)
                close(to_dve, ins)
            for j in range(2):
                by_token("u", to_act, token, 4)
            for j in range(2):
                linear("u", to_act, h, T)
            values_in = to_act.n
            spare = ([lambda: linear("u", to_act, h, T)] * 2 + [lambda: linear("u", to_act, hb, TC)] * 2
                     + [lambda: by_token("u", to_act, token, 4)] * 2)
            for _ in range(4):
                spare.pop(0)()
            pe.wait_ge(to_act.taken, values_in)
            pe.wait_ge(sem("m_qk"), 8)

            def products(k_of, q_of):
                for half in range(2):
                    ps = to_dve.fill(pe)
                    for q in range(2):
                        ins = pe.matmul(ps[:, q * T:(q + 1) * T], k_of(2 * half + q), q_of, start=True, stop=True)
                    close(to_dve, ins)

            def spread(to, *rows):
                ps = to.fill(pe)
                for i, (tile, n, r) in enumerate(rows):
                    ins = pe.matmul(ps[:, i * T:(i + 1) * T], ident[0:n, r:r + 1].to_broadcast([n, P]), tile[0:n, :],
                                    start=True, stop=True)
                close(to, ins)

            for hd in range(M_H):
                products(lambda st: m_x[:, 4 + hd, st * P:(st + 1) * P], m_x[:, hd, T:TC])
                for d in range(2):
                    r = 32 * d + hd
                    spread(to_dve, (row_r, P, r))
                    marks["m_row", 2 * hd + d] = to_dve.n
                    spread(to_act, (row_m, 64, r))
                    if spare:
                        spare.pop(0)()
                    pe.wait_ge(sem("m_w"), c(sem("m_w")))
                    ps = to_dve.fill(pe)
                    for st in range(4):
                        pe.matmul(ps[:, 0:T], m_v[:, st, hd * P:(hd + 1) * P], m_e[:, d, st, :],
                                  start=st == 0, stop=st == 3)
                    for st in range(4):
                        ins = pe.matmul(ps[:, T:TC], ones, m_e[:, d, st, :], start=st == 0, stop=st == 3)
                    close(to_dve, ins)
                norm_sum([m_rc[:, 2, :]], T)

            marks["a_in"] = to_act.n
            spare = [lambda: linear("u", to_act, hb, TC)] * 4 + [lambda: linear("u", to_act, h, T)] * 2
            pe.wait_ge(to_act.taken, to_act.n)
            for j in range(8):
                n = T if j < 4 else TC
                norm_sum([a_t[:, 0:n]], n, blk)
                pe.wait_ge(sem("a_normed"), c(sem("a_normed")))
                src = a_q[:, j, :] if j < 4 else a_k[:, j - 4, T:TC]
                ps = to_dve.fill(pe)
                close(to_dve, pe.matmul(ps[:, 0:T], rot, src, start=True, stop=True))
            pe.wait_ge(sem("a_rotated"), 8)
            for hd in range(A_H):
                for t in range(TT):
                    for sub in range(2):
                        rows = slice(SUB * sub, SUB * sub + SUB)
                        ps = to_dve.fill(pe)
                        close(to_dve, pe.matmul(ps[:, :], a_q[rows, hd, t * P:(t + 1) * P], a_k[rows, hd, :],
                                                start=True, stop=True))
                        marks["a_score", 4 * hd + 2 * t + sub] = to_dve.n
                    if spare:
                        spare.pop(0)()
                    pe.wait_ge(sem("a_p"), c(sem("a_p")))
                    ps = to_act.fill(pe)
                    for st in range(4):
                        ins = pe.transpose(ps[:, st * P:(st + 1) * P], a_p0[:, st * P:(st + 1) * P], ident)
                    close(to_act, ins)
                    marks["a_pt", 2 * hd + t] = to_act.n
                pe.wait_ge(to_act.taken, to_act.n)
                ps = to_dve.fill(pe)
                for st in range(4):
                    ins = pe.matmul(ps[:, 0:T], a_v[:, st, hd * P:(hd + 1) * P], a_pt[:, hd % 2, st, :],
                                    start=st == 0, stop=st == 3)
                close(to_dve, ins)
                norm_sum([a_t[:, 0:T]], T)

            marks["s_in"] = to_act.n
            spare = [lambda: linear("u", to_act, h, T)] * 12
            for _ in range(4):
                spare.pop(0)()
            pe.wait_ge(sem("s_xbc"), 8)
            for t in range(4):
                ps = to_act.fill(pe)
                for j in range(4):
                    ins = pe.transpose(ps[:, j * P:(j + 1) * P], s_x[:, j, t * P:(t + 1) * P], ident)
                close(to_act, ins)
            for hd in range(S_H):
                if hd % 4 == 0:
                    g = hd // 4
                    products(lambda st: s_x[:, 4 + g, st * P:(st + 1) * P], s_x[:, 6 + g, T:TC])
                if hd == 0:
                    pe.wait_ge(to_act.taken, to_act.n)
                rows = slice(64 * (hd % 2), 64 * (hd % 2) + 64)
                for d in range(2):
                    spread(to_dve, (row_r, P, 64 + 32 * d + hd))
                    marks["s_row", 2 * hd + d] = to_dve.n
                for d in range(2):
                    if spare and hd:
                        spare.pop(0)()
                    pe.wait_ge(sem("s_w"), c(sem("s_w")))
                    if d == 0:
                        ps = to_dve.fill(pe)
                    for st in range(4):
                        ins = pe.matmul(ps[rows, 0:T], s_xt[:, st, hd * 64:(hd + 1) * 64], s_e[:, st, :],
                                        start=st == 0 and d == 0, stop=st == 3 and d == 1)
                    if d == 0:
                        ins.then_inc(sem("s_w_used"), 1)
                close(to_dve, ins)
            for g in range(2):
                norm_sum([sq_s[:, 2 * g, :], sq_s[:, 2 * g + 1, :]], T)

            pe.wait_ge(sem("branches"), 1)
            marks["merge"] = to_act.n
            for half in range(2):
                for y in (y_m, y_a, y_s):
                    linear("branch", to_dve, lambda k: y[:, k, :], T, kt=4, tiles=4)
            pe.wait_ge(sem("merged"), 8)
            for j in range(4):
                linear("w_out", to_dve, lambda k: g_acc[:, k, :], T)

            norm_sum([f_sq[:, k, 0:T] for k in range(KT)], T)
            pe.wait_ge(s["normed"], c(s["normed"]))
            pe.wait_ge(to_dve.taken, to_dve.n)
            for b in range(4):
                pe.matmul(banks[4 + b][:, :], f_zero[:, 0:P], f_zero[:, :], start=True, stop=False,
                          skip_group_check=True)

            marks["ff"] = to_act.n
            waiting = []

            def down(i, w, g):
                pe.wait_ge(sem("ff_hidden"), 2 * i + 2)
                for q in range(2):
                    for m in range(KT):
                        ins = pe.matmul(banks[4 + m // 2][:, (m % 2) * T:(m % 2 + 1) * T], w[:, q, m * P:(m + 1) * P],
                                        f_he[:, i % 2, q, :], start=False, stop=False, skip_group_check=True)
                ins.then_inc(sem("ff_down_used"), 1)
                freed[g] = (sem("ff_down_used"), i + 1)

            for i in range(FF_PAIRS):
                linear("ff_a", to_act, h, T)
                linear("ff_g", to_act, h, T)
                if waiting:
                    down(*waiting.pop())
                g = slot[0]
                waiting.append((i, weights("ff_down", 2), g))
            down(*waiting.pop())
            for b in range(4):
                ins = pe.matmul(banks[4 + b][:, :], f_zero[:, 0:P], f_zero[:, :], start=False, stop=True,
                                skip_group_check=True)
            ins.then_inc(sem("ff_done"), 1)

            pe.wait_ge(sem("x_final"), 1)
            for t in range(TT):
                for half in range(2):
                    ps = to_act.fill(pe)
                    for k in range(4):
                        ins = pe.transpose(ps[:, k * P:(k + 1) * P], x[:, 4 * half + k, t * P:(t + 1) * P], ident)
                    close(to_act, ins)
                marks["out", t] = to_act.n
            assert slot[0] == len(SLOTS)

        @block.sync
        def _(sp):
            def reuse(g):
                if g >= RING:
                    sm, value = freed[g - RING]
                    sp.wait_ge(sm, value)

            def load(g, src, kt, n):
                sp.dma_start(ring[:, g % RING, :].rearrange("p (k n) -> p k n", k=kt), src).then_inc(landed[g % RING], 16)

            def expert(layer, g0, e, j, sl):
                if j < 4:
                    w = A["moe_w_gate"] if j % 2 == 0 else A["moe_w_up"]
                    c0 = 256 * (j // 2)
                    src = w[layer, sl, :, c0:c0 + 256].rearrange("o (k p) n -> p (o k) n", p=P)
                    load(g0 + j, src, KT, 256)
                else:
                    r0 = 256 * (j - 4)
                    src = A["moe_w_down"][layer, sl, r0:r0 + 256, :].rearrange("o (k p) n -> p (o k) n", p=P)
                    load(g0 + j, src, 2, D)

            g = 0
            while g < len(SLOTS):
                what, arg = SLOTS[g]
                if what != "moe":
                    reuse(g)
                    load(g, *arg)
                    g += 1
                    continue
                for j in range(6):
                    reuse(g + j)
                    expert(arg, g, 0, j, slice(0, 1))
                first = arg * EXPERTS
                with sp.Fori(1, EXPERTS) as e:
                    for j, (sm, per, at) in enumerate((("gate_used", 2, 1), ("gate_up_ready", 4, 2),
                                                       ("gate_used", 2, 2), ("gate_up_ready", 4, 4),
                                                       ("down_used", 2, 1), ("down_used", 2, 2))):
                        sp.wait_ge(sem(sm), per * e + (per * (first - 1) + at))
                        expert(arg, g, e, j, bass.ds(e, 1))
                g += 6 * EXPERTS
            for t in range(TT):
                sp.wait_ge(sem("act_tile_taken"), marks["out", t])
                sp.dma_start(out[0, t * P:(t + 1) * P, :], o_tok[:, t, :]).then_inc(sem("stored"), 16)
            sp.wait_ge(sem("stored"), 16 * TT)

        @block.gpsimd
        def _(pool):
            def load(i, cols_):
                w = (ada[1], w_mod)[i]
                pool.dma_start(side[:, i], w[:, cols_].rearrange(f_rows, p=P)).then_inc(sem(f"side_landed{i}"), 16)

            pool.wait_ge(sem("combine"), 1)
            for i in range(2):
                load(i, slice(0, 384))
            with pool.Fori(1, EXPERTS) as e:
                for i in range(2):
                    pool.wait_ge(sem(f"side_used{i}"), e)
                    load(i, bass.ds(e * 384, 384))

        @block.scalar
        def _(act):
            c = Count()
            tiles = act_banks()

            def a(ins, done=s["act_step"]):
                ins.then_inc(done, 1)
                act.wait_ge(done, c(done))

            def take(dst, src=None, func=ACT.Identity, n=T, parts=P, done=None, **kw):
                ps = tiles.read(act)
                view = ps[0:parts, 0:n] if src is None else src(ps)
                act.activation(dst, view, func, **kw).then_inc(tiles.taken, 1)
                tiles.step()
                if done is not None:
                    act.wait_ge(tiles.taken, tiles.n)

            inv_n = [0]

            def inverse(count, n=T, at=0):
                ps = tiles.read(act)
                ins = act.activation(lnt[:, 0:n], ps[:, 0:n], ACT.Ln, bias=eps, scale=1.0 / count)
                ins.then_inc(tiles.taken, 1)
                tiles.step()
                act.wait_ge(tiles.taken, tiles.n)
                a(act.activation(inv[:, inv_n[0] % 4, at:at + n], lnt[:, 0:n], ACT.Exp, scale=-0.5), s["norm_inv"])
                inv_n[0] += 1

            for dst, src in early:
                act.dma_start(dst, src).then_inc(sem("conditions"), 16)
            for dst, src in loads:
                act.dma_start(dst, src, allow_slow_non_contiguous=True).then_inc(s["params"], 16)
            act.wait_ge(sem("cleared"), 1)
            for dst, src in later:
                act.dma_start(dst, src, allow_slow_non_contiguous=True).then_inc(s["params"], 16)
            act.wait_ge(sem("dve_tile_taken"), 1)
            a(act.activation(cond_t[:, :], cols[:, 0:24], ACT.Tanh, scale=0.5), sem("cond_tanh"))
            act.wait_ge(s["params"], n_params)

            inverse(D)
            for j in range(4):
                take(g_q[:, j, :], scale=float(P) ** -0.5)
            for j in range(4):
                take(g_k[:, j, :])
            for j in range(4):
                for t in range(TT):
                    take(g_v[:, t, j * 256:(j + 1) * 256])
            for j in range(8):
                take(g_g[:, j, :])
            take(g_lr[0:16, :], parts=16, done=True)
            act.wait_ge(sem("gla_neg"), 1)
            a(act.activation(g_l, g_l, ACT.Exp))
            a(act.activation(g_l, g_l, ACT.Ln, bias=one), sem("gla_log"))
            act.wait_ge(sem("gla_rest"), 1)
            a(act.activation(g_gam, g_gam, ACT.Exp, scale=1.0 / 16))
            a(act.activation(g_l, g_l, ACT.Exp, scale=-1.0 / 16), sem("gla_decay"))
            a(act.activation(sq[:, :, T:TC], g_g, ACT.Tanh, scale=0.5), sem("gla_tanh"))
            for hd in range(GLA_H):
                inverse(GLA_DV)

            def experts(layer):
                inverse(D)
                take(r_s, n=32, func=ACT.Tanh, scale=0.5, done=True)
                first = layer * EXPERTS
                with act.Fori(0, EXPERTS) as e:
                    for f in range(FT):
                        act.wait_ge(sem("gate_up_ready"), 4 * (e + first) + f + 1)
                        act.wait_ge(sem("gate_up_taken"), 4 * (e + first) + f + 3)
                        act.activation(e_th[:, f % 2, :], banks[f][:, 0:T], ACT.Tanh, scale=0.5)\
                            .then_inc(sem("gate_tanh"), 1)

            experts(0)

            inverse(D)
            for j in range(8):
                take(l_xb[:, j, 3:3 + T])
            for j in range(8):
                take(l_g[:, j, :])
            act.wait_ge(sem("lru_half"), 1)
            a(act.activation(misc[:, 8:16], misc[:, 16:24], ACT.Exp), sem("lru_z"))
            for dst, b in ((l_r, 24), (l_i, 32)):
                for m in range(8):
                    take(dst[:, m, :], func=ACT.Tanh, scale=0.5, bias=misc[:, b + m:b + m + 1])
            act.wait_ge(sem("lru_log"), 1)
            a(act.activation(l_a, l_r, ACT.Exp))
            a(act.activation(l_m, l_r, ACT.Tanh, scale=-1.0), sem("lru_am"))
            act.wait_ge(sem("lru_m2"), 1)
            a(act.activation(l_m, l_m, ACT.Sqrt), sem("lru_mult"))
            act.wait_ge(sem("lru_cubic"), 1)
            a(act.activation(l_r, l_r, ACT.Tanh, scale=0.7978845608028654), sem("lru_gelu"))
            experts(1)
            inverse(D)

            inverse(D)
            inverse(D)
            take(z_i[0:64, :], n=TC, parts=64, bias=bias_i[:, 0:1])
            take(z_f, n=TC, bias=bias_f[:, 0:1], done=True)
            a(act.activation(decay[:, 1:2], decay[:, 0:1], ACT.Exp), sem("gate_z"))
            act.wait_ge(sem("gate_neg"), 1)
            a(act.activation(z_e, z_e, ACT.Exp))
            a(act.activation(z_e, z_e, ACT.Ln, bias=one), sem("gate_log"))

            act.wait_ge(sem("m_pad"), 1)
            for j in range(4):
                take(m_pad[:, j, 1, 1:257])
            for j in range(4):
                take(m_pad[:, 4 + j, :, 1:257], lambda ps: ps.rearrange("p (s t) -> p s t", s=2))
            for j in range(2):
                for t in range(4):
                    take(m_v[:, t, j * 256:(j + 1) * 256])
            for j in range(4):
                take(m_o[:, j, :], func=ACT.Tanh, scale=0.5)

            def slot_of(dsts, **kw):
                return lambda: [take(dst, **kw) for dst in dsts]

            spare = ([slot_of([a_q[:, j, :] for j in (2 * i, 2 * i + 1)]) for i in range(2)]
                     + [slot_of([a_k[:, j, :] for j in (2 * i, 2 * i + 1)], n=TC) for i in range(2)]
                     + [slot_of([a_v[:, t, i * 256:(i + 1) * 256] for t in range(4)]) for i in range(2)])
            for j in range(8):
                act.wait_ge(sem("m_conv"), j + 1)
                if j < 4:
                    a(act.activation(m_pad[:, j, 1, 0:T], m_x[:, j, T:TC], ACT.Tanh, scale=0.5), sem("m_tanh"))
                else:
                    a(act.activation(m_pad[:, j, :, 0:T], m_x[:, j, :].rearrange("p (s t) -> p s t", s=2), ACT.Tanh,
                                     scale=0.5), sem("m_tanh"))
                if j % 2:
                    spare.pop(0)()
            for hd in range(M_H):
                for d in range(2):
                    n = 2 * hd + d
                    if n:
                        act.wait_ge(sem("m_read"), n)
                    take(m_rc[:, 0, :], func=ACT.Exp, scale=-1.0, done=True)
                    act.wait_ge(sem("dve_tile_taken"), marks["m_row", n])
                    a(act.activation(m_e[:, d], m_e[:, d], ACT.Exp), sem("m_exp"))
                    if spare:
                        spare.pop(0)()
                inverse(P)

            halves = lambda ps: ps.rearrange("p (s t) -> p s t", s=2)
            spare = ([slot_of([s_pad[:, j, :, 1:257] for j in (2 * i, 2 * i + 1)], src=halves) for i in range(4)]
                     + [slot_of([s_z[:, j, :] for j in (2 * i, 2 * i + 1)]) for i in range(2)])
            for j in range(8):
                inverse(SUB, T if j < 4 else TC)
            act.wait_ge(sem("a_lam"), 1)
            a(act.activation(misc[:, 42:44], misc[:, 40:42], ACT.Exp), sem("a_lam_exp"))
            n = 0
            for hd in range(A_H):
                for t in range(TT):
                    for sub, dst in enumerate((a_p0, a_p1)):
                        act.wait_ge(sem("dve_tile_taken"), marks["a_score", n])
                        a(act.activation(dst, dst, ACT.Exp, bias=a_st[:, 2 + sub:3 + sub], scale=SUB ** -0.5,
                                         accum_out=a_st[:, 4 + sub:5 + sub]), sem("a_exp"))
                        n += 1
                    if spare:
                        if len(spare) == 6:
                            act.wait_ge(sem("s_pad"), 1)
                        spare.pop(0)()
                    take(a_pt[:, hd % 2, :, t * P:(t + 1) * P], lambda ps: ps.rearrange("p (s t) -> p s t", s=4),
                         done=True)
                inverse(P)

            spare = [slot_of([g_th[:, j, :] for j in (2 * i, 2 * i + 1)], func=ACT.Tanh, scale=0.5)
                     for i in range(12)]
            for j in range(8):
                act.wait_ge(sem("s_conv"), j + 1)
                a(act.activation(s_pad[:, j, :, 0:T], s_x[:, j, :].rearrange("p (s t) -> p s t", s=2), ACT.Tanh,
                                 scale=0.5), sem("s_tanh"))
                if j % 2:
                    spare.pop(0)()
            for t in range(4):
                take(s_xt[:, t, :], n=512, done=True)
            for n in range(2 * S_H):
                act.wait_ge(sem("dve_tile_taken"), marks["s_row", n])
                a(act.activation(s_e, s_e, ACT.Exp), sem("s_exp"))
                if spare and n >= 2:
                    spare.pop(0)()
            act.wait_ge(sem("s_y"), 1)
            a(act.activation(s_qm[:, 0], s_z, ACT.Tanh, scale=0.5), sem("s_ztanh"))
            for g in range(2):
                inverse(256)

            inverse(D)

            for i in range(FF_PAIRS):
                for j in range(4):
                    if i:
                        act.wait_ge(sem("ff_conv"), 4 * (i - 1) + j + 1)
                    take(f_pad[:, j, 1:257])
                for q in range(2):
                    act.wait_ge(sem("ff_conv"), 4 * i + 2 + q + 1)
                    a(act.activation(f_th[:, q, :], f_c[:, 2 + q, :], ACT.Tanh, scale=0.5), sem("ff_tanh"))
            for t in range(TT):
                for half in range(2):
                    take(o_tok[:, t, half * 512:(half + 1) * 512], n=512, done=True)

        @block.vector
        def _(dve):
            c = Count()
            tiles = dve_banks()

            def v(ins, done=s["dve_step"]):
                ins.then_inc(done, 1)
                dve.wait_ge(done, c(done))

            def tt(o, i0, i1, op, done=s["dve_step"]):
                v(dve.tensor_tensor(o, i0, i1, op), done)

            def ts(o, i0, s1, s2, op0, op1=None, done=s["dve_step"]):
                if op1 is None:
                    v(dve.tensor_scalar(o, i0, s1, None, op0), done)
                else:
                    v(dve.tensor_scalar(o, i0, s1, s2, op0, op1), done)

            def stt(o, i0, sc, i1, op0, op1, done=s["dve_step"]):
                v(dve.scalar_tensor_tensor(out=o, in0=i0, scalar=sc, in1=i1, op0=op0, op1=op1), done)

            def take():
                return tiles.read(dve)

            def took(ins):
                ins.then_inc(tiles.taken, 1)
                tiles.step()
                dve.wait_ge(tiles.taken, tiles.n)

            inv_n = [0]

            def inverse():
                dve.wait_ge(s["norm_inv"], inv_n[0] + 1)
                i = inv[:, inv_n[0] % 4, :]
                inv_n[0] += 1
                return i

            mul, add, sub, mx = ALU.mult, ALU.add, ALU.subtract, ALU.max

            for tile in (bias_i[:, :], bias_f[:, :]):
                v(dve.memset(tile, 0.0))
            v(dve.memset(decay[:, :], 0.0), sem("cleared"))
            ps = take()
            took(dve.tensor_copy(cols[:, 0:24], ps[:, 0:24]))
            dve.wait_ge(sem("cond_tanh"), 1)
            stt(cond[:, :], cond_t[:, :], 1.0, cols[:, 0:24], add, mul)
            ts(cond[:, :], cond[:, :], 0.5, None, mul)
            dve.wait_ge(s["params"], n_params)
            ps = take()
            took(dve.tensor_copy(cols[:, 0:N_ROWS], ps[:, 0:N_ROWS]))
            for dst in (x[:, :, :], hh[:, :, 0:T]):
                for pair in range(4):
                    ps = take()
                    took(dve.tensor_copy(dst[:, 2 * pair:2 * pair + 2, :], ps.rearrange("p (k t) -> p k t", k=2)))

            def mod_sum(j):
                ps = take()
                took(dve.tensor_reduce(mods[:, 0, 2 * j:2 * j + 2], ps[:, 0:256].rearrange("p (m q) -> p m q", m=2),
                                       AX, add))

            for j in range(24):
                assert SLOTS[j][0] == "mod"
                dve.wait_ge(landed[j % RING], 16 * (j // RING + 1))
                w = ring[:, j % RING, :].rearrange("p (k n) -> p k n", k=KT)
                acc = mod_acc[:, j % 2].rearrange("p m q -> p (m q)")
                ts(acc, w[:, 0, :], cond[:, 0:1], None, mul)
                for k in range(1, KT):
                    stt(acc, w[:, k, :], cond[:, k:k + 1], acc, mul, add,
                        done=sem("mod_part") if k == KT - 1 else s["dve_step"])
                if j:
                    mod_sum(j - 1)
            mod_sum(23)
            tt(mods[:, 0, :], mods[:, 0, :], col("ada_b", 0, 48), add)

            def all_gains(which):
                for i, (layer, at, g) in enumerate(
                        ((0, 8, col("norm_mix_g", 0, 8)), (0, 32, col("norm_ffn_g", 0, 8)),
                         (1, 8, col("norm_mix_g", 8, 8)), (1, 32, col("norm_ffn_g", 8, 8)),
                         (2, 8, col("norm1_g_2", 0, 8)), (2, 32, col("norm2_g_2", 0, 8)))):
                    if (layer == 0) == (which == 0):
                        stt(gains[:, i, :], mods[:, layer, at:at + 8], 1.0, g, add, mul)

            all_gains(0)

            def norm(gain, shift, sq_=None, src=x, at=T):
                q = sq if sq_ is None else sq_
                tt(q[:, :, 0:T], src[:, :, 0:T], src[:, :, 0:T], mul, done=s["norm_sq"])
                i = inverse()
                for k in range(KT):
                    stt(hh[:, k, at:at + T], src[:, k, 0:T], gain[:, k:k + 1], i[:, 0:T], mul, mul)
                    ts(hh[:, k, at:at + T], hh[:, k, at:at + T], shift[:, k:k + 1], None, add,
                       done=s["normed"] if k == KT - 1 else s["dve_step"])

            def residual(gate):
                for k in range(KT):
                    ps = take()
                    took(dve.scalar_tensor_tensor(out=x[:, k, :], in0=ps[:, 0:T], scalar=gate[:, k:k + 1],
                                                  in1=x[:, k, :], op0=mul, op1=add))

            norm(gains[:, 0, :], mods[:, 0, 0:8])
            for j in range(4):
                ps = take()
                took(dve.tensor_scalar(g_z[:, j, :], ps[:, 0:T], col("gla_b_gate", j), None, add))
            stt(g_l, g_z, -1.0, g_z, mul, ALU.min, done=sem("gla_neg"))
            ts(g_z, g_z, 0.0, None, ALU.min)
            dve.wait_ge(sem("gla_log"), 1)
            tt(g_z, g_z, g_l, sub)
            for j in range(4):
                for n in range(CHUNKS):
                    at = slice(n * 64, (n + 1) * 64)
                    v(dve.tensor_tensor_scan(g_l[:, j, at], ones[:, 0:64], g_z[:, j, at], 0.0, mul, add))
            v(dve.tensor_copy(g_gam, g_l[:, :, 63:T:64]))
            for j in range(4):
                lc = g_l[:, j, :].rearrange("p (n t) -> p n t", n=CHUNKS)
                tt(lc, lc, g_gam[:, j, :].unsqueeze(2).to_broadcast([P, CHUNKS, 64]), sub,
                   done=sem("gla_rest") if j == 3 else s["dve_step"])
            dve.wait_ge(sem("gla_decay"), 1)
            tt(g_z, g_k, g_l, mul, done=sem("gla_kdec"))
            for t in range(TT):
                ps = take()
                took(dve.tensor_copy(g_kt[:, t, :], ps))
            for n in range(CHUNKS):
                for pair in range(2):
                    ps = take()
                    for q in range(2):
                        hd = 2 * pair + q
                        u = ps[:, q * 256:(q + 1) * 256]
                        if n == 0:
                            ins = dve.tensor_copy(g_s[:, n, hd, :], u)
                        else:
                            ins = dve.scalar_tensor_tensor(out=g_s[:, n, hd, :], in0=g_s[:, n - 1, hd, :],
                                                           scalar=g_gam[:, hd, n:n + 1], in1=u, op0=mul, op1=add)
                        if q == 0:
                            v(ins)
                        else:
                            took(ins)
            for hd in range(GLA_H):
                ps = take()
                took(dve.tensor_copy(g_o[:, 2 * hd:2 * hd + 2, :], ps.rearrange("p (j t) -> p j t", j=2)))
                o = g_o[:, 2 * hd:2 * hd + 2, :]
                tt(sq[:, 2 * hd:2 * hd + 2, 0:T], o, o, mul, done=s["norm_sq"])
            dve.wait_ge(sem("gla_tanh"), 1)
            stt(g_g, sq[:, :, T:TC], 1.0, g_g, add, mul)
            for hd in range(GLA_H):
                i = inverse()
                for j in range(2):
                    o = g_o[:, 2 * hd + j, :]
                    stt(o, o, col("gla_norm_g", j), i[:, 0:T], mul, mul)
                    stt(o, o, 0.5, g_g[:, 2 * hd + j, :], mul, mul,
                        done=sem("gla_y") if (hd, j) == (3, 1) else s["dve_step"])
            residual(mods[:, 0, 16:24])

            def side_read(e):
                one_more = e + 1
                dve.wait_ge(sem("side_turned"), one_more)
                for b in range(3):
                    n = (4, 4, 1)[b]
                    src = banks[b][:, 0:n * P].rearrange("p (m q) -> p m q", m=n)
                    if isinstance(e, int):
                        dst = side_raw[:, e, 4 * b:4 * b + n]
                    else:
                        dst = side_raw[:, bass.ds(e, 1), 4 * b:4 * b + n].rearrange("p o m -> p (o m)")
                    dve.tensor_reduce(dst, src, AX, add).then_inc(sem("side_read"), 1)

            def side_products(e):
                accs = [side_acc[:, 3 * i:3 * i + 3, :].rearrange("p m q -> p (m q)") for i in range(3)]
                for i in range(2):
                    dve.wait_ge(sem(f"side_landed{i}"), 16 * (e + 1))
                    for k in range(KT):
                        w = side[:, i, k, :]
                        for q in ((0,) if i == 0 else (1, 2)):
                            cnd = cond[:, 8 * q + k:8 * q + k + 1]
                            if k == 0:
                                ins = dve.tensor_scalar(accs[q], w, cnd, None, mul)
                            else:
                                dve.wait_ge(sem(f"side_step{q}"), (KT - 1) * e + k)
                                ins = dve.scalar_tensor_tensor(out=accs[q], in0=w, scalar=cnd, in1=accs[q], op0=mul,
                                                               op1=add)
                            if k < KT - 1:
                                ins.then_inc(sem(f"side_step{q}"), 1)
                            elif q == 1:
                                ins.then_inc(sem("side_first"), 1)
                            elif q == 0:
                                ins.then_inc(sem("side_used0"), 1)
                            else:
                                ins.then_inc(sem("side_used1"), 1)
                dve.wait_ge(sem("side_first"), e + 1)
                dve.wait_ge(sem("side_used0"), e + 1)
                dve.wait_ge(sem("side_used1"), e + 1)
                dve.sem_inc(sem("side_part"), 1)

            def experts(layer):
                norm(gains[:, 2 * layer + 1, :], mods[:, layer, 24:32])
                v(dve.memset(e_zero, 0.0))
                dve.wait_ge(sem("act_tile_taken"), marks["logits", layer])
                ts(r_s, r_s, 1.0, 0.5, add, mul)
                grp = r_sel.rearrange("p (g i) -> p g i", i=4)
                tt(r_sel.rearrange("p (t e) -> p t e", t=2), r_s.rearrange("p (t e) -> p t e", t=2),
                   router_b[:, :].unsqueeze(1).to_broadcast([P, 2, 16]), add)
                tt(r_pair[:, :, 0:3], grp[:, :, 0:3], grp[:, :, 1:4], add)
                tt(r_pair[:, :, 3:5], grp[:, :, 0:2], grp[:, :, 2:4], add)
                tt(r_pair[:, :, 5:6], grp[:, :, 0:1], grp[:, :, 3:4], add)
                v(dve.tensor_reduce(r_gs, r_pair, AX, mx))
                gs2 = r_gs.rearrange("p (t g) -> p t g", t=2)
                key2 = r_key.rearrange("p (t g) -> p t g", t=2)
                v(dve.tensor_reduce(r_gm, gs2, AX, mx))
                tt(key2, gs2, r_gm.unsqueeze(2).to_broadcast([P, 2, 4]), ALU.is_ge)
                tt(key2, key2, con[:, C_IOTA:C_IOTA + 4].unsqueeze(1).to_broadcast([P, 2, 4]), mul)
                v(dve.tensor_reduce(r_km, key2, AX, mx))
                tt(r_oh.rearrange("p (t g) -> p t g", t=2), key2, r_km.unsqueeze(2).to_broadcast([P, 2, 4]), ALU.is_equal)
                a4 = r_a.rearrange("p g (i j) -> p g i j", i=4)
                b4 = r_b.rearrange("p g (i j) -> p g i j", i=4)
                other = grp.unsqueeze(2).to_broadcast([P, 8, 4, 4])
                own = grp.unsqueeze(3).to_broadcast([P, 8, 4, 4])
                tt(a4, other, own, ALU.is_gt)
                tt(b4, other, own, ALU.is_equal)
                tt(r_b, r_b, con[:, C_TRI:C_TRI + 16].unsqueeze(1).to_broadcast([P, 8, 16]), mul)
                tt(r_a, r_a, r_b, add)
                v(dve.tensor_reduce(r_rank, a4, AX, add))
                rank = r_rank.rearrange("p (g i) -> p g i", i=4)
                stt(rank, rank, 1.5, r_oh.unsqueeze(2).to_broadcast([P, 8, 4]), ALU.is_lt, mul)
                tt(r_w, r_rank, r_s, mul)
                w2 = r_w.rearrange("p (t e) -> p t e", t=2)
                v(dve.tensor_reduce(r_den, w2, AX, add))
                v(dve.reciprocal(r_den, r_den))
                tt(r_comb.rearrange("p (t e) -> p t e", t=2), w2, r_den.unsqueeze(2).to_broadcast([P, 2, 16]), mul,
                   done=sem("combine"))
                ps = take()
                took(dve.tensor_copy(e_ct[0:16, :], ps[0:16, 0:T]))
                for e in range(0, EXPERTS, 2):
                    ps = take()
                    took(dve.tensor_copy(e_cb[:, e:e + 2, :], ps.rearrange("p (e t) -> p e t", e=2)))
                first = layer * EXPERTS
                if layer == 0:
                    v(dve.memset(side_acc, 0.0), sem("side_part"))
                    for f in range(3):
                        dve.sem_inc(sem("side_read"), 1)
                if layer == 0:
                    for f in range(FT):
                        dve.sem_inc(sem("gate_up_taken"), 1)
                with dve.Fori(0, EXPERTS) as e:
                    n = 4 * (e + first)
                    for f in range(FT):
                        dve.wait_ge(sem("gate_tanh"), n + (f + 1))
                        dve.scalar_tensor_tensor(out=e_t1, in0=e_th[:, f % 2, :], scalar=1.0, in1=banks[f][:, 0:T],
                                                 op0=add, op1=mul).then_inc(sem("silu2"), 1)
                        dve.wait_ge(sem("silu2"), n + (f + 1))
                        dve.scalar_tensor_tensor(out=e_t1, in0=e_t1, scalar=0.5, in1=banks[f][:, T:TC], op0=mul,
                                                 op1=mul).then_inc(sem("gate_up_taken"), 1)
                        dve.wait_ge(sem("gate_up_taken"), n + (f + 5))
                        dve.tensor_tensor(e_he[:, f, :], e_t1, e_cb[:, bass.ds(e, 1), :].rearrange("p o t -> p (o t)"),
                                          mul).then_inc(sem("hidden_ready"), 1)
                        dve.wait_ge(sem("hidden_ready"), n + (f + 1))
                    if layer == 0:
                        side_read(e)
                        side_products(e)
                if layer == 0:
                    side_read(EXPERTS)
                    dve.wait_ge(sem("side_read"), 3 * EXPERTS + 6)
                    raw = side_raw[:, 1:, :]
                    for which in range(3):
                        b = col("b_mod_2", 0, 48) if which else col("ada_b", 48, 48)
                        tt(mods[:, 1 + which, :].rearrange("p (e m) -> p e m", m=3),
                           raw[:, :, 3 * which:3 * which + 3], b.rearrange("p (e m) -> p e m", m=3), add)
                    all_gains(1)
                    stt(misc[:, 48:56], mods[:, 3, 8:16], 1.0, col("norm1_g_2", 0, 8), add, mul)
                dve.wait_ge(sem("experts_done"), layer + 1)
                for k in range(KT):
                    stt(x[:, k, :], banks[4 + k // 2][:, (k % 2) * T:(k % 2 + 1) * T],
                        mods[:, layer, 40 + k:41 + k], x[:, k, :], mul, add)

            experts(0)

            norm(gains[:, 2, :], mods[:, 1, 0:8])
            v(dve.memset(l_xb[:, :, 0:3], 0.0))
            lam8, z8 = col("lru_lambda", 0, 8), misc[:, 8:16]
            ts(misc[:, 24:32], col("lru_b_r", 0, 8), 0.5, None, mul)
            ts(misc[:, 32:40], col("lru_b_i", 0, 8), 0.5, None, mul)
            stt(misc[:, 16:24], lam8, -1.0, lam8, mul, ALU.min, done=sem("lru_half"))
            dve.wait_ge(sem("lru_z"), 1)
            s8, q8 = misc[:, 56:64], misc[:, 16:24]
            ts(s8, z8, 2.0, None, add)
            v(dve.reciprocal(s8, s8))
            tt(s8, s8, z8, mul)
            tt(q8, s8, s8, mul)
            ts(z8, q8, 1.0 / 17, None, mul)
            for k in range(7, 0, -1):
                stt(z8, z8, 1.0 / (2 * k + 1), q8, add, mul)
            stt(z8, z8, 1.0, s8, add, mul)
            ts(s8, lam8, -1.0, 0.0, mul, mx)
            stt(s8, z8, 2.0, s8, mul, add)
            ts(s8, s8, -4.0, None, mul)
            for j in range(8):
                dve.wait_ge(sem("act_tile_taken"), marks["lru_xb"] + j + 1)
                ts(l_x[:, j, :], l_xb[:, j, 0:T], col("lru_conv_w", j), col("lru_conv_b", j), mul, add)
                for tap in range(1, 4):
                    stt(l_x[:, j, :], l_xb[:, j, tap:tap + T], col("lru_conv_w", 8 * tap + j), l_x[:, j, :], mul, add,
                        done=sem("lru_conv") if tap == 3 else s["dve_step"])
            dve.wait_ge(sem("act_tile_taken"), marks["lru_gates"])
            for j in range(8):
                ts(l_r[:, j, :], l_r[:, j, :], 1.0, s8[:, j:j + 1], add, mul,
                   done=sem("lru_log") if j == 7 else s["dve_step"])
            stt(l_x, l_i, 1.0, l_x, add, mul)
            dve.wait_ge(sem("lru_am"), 1)
            tt(l_i, l_a, l_a, mul)
            stt(l_m, l_i, 1.0, l_m, add, mul, done=sem("lru_m2"))
            tt(l_i, l_g, l_g, mul)
            ts(l_i, l_i, 0.044715, 1.0, mul, add)
            tt(l_r, l_i, l_g, mul, done=sem("lru_cubic"))
            dve.wait_ge(sem("lru_mult"), 1)
            stt(l_x, l_x, 0.5, l_m, mul, mul)
            for j in range(8):
                v(dve.tensor_tensor_scan(l_h[:, j, :], l_a[:, j, :], l_x[:, j, :], 0.0, mul, add))
            dve.wait_ge(sem("lru_gelu"), 1)
            stt(l_g, l_r, 1.0, l_g, add, mul)
            stt(l_h, l_h, 0.5, l_g, mul, mul, done=sem("lru_y"))
            residual(mods[:, 1, 16:24])
            experts(1)

            tt(sq[:, :, 0:T], x[:, :, :], x[:, :, :], mul, done=s["norm_sq"])
            i = inverse()
            for k in range(KT):
                stt(x[:, k, :], x[:, k, :], col("final_norm_g", k), i[:, 0:T], mul, mul)

            tt(sq2[:, :, 0:T], hh[:, :, 0:T], hh[:, :, 0:T], mul, done=s["norm_sq"])
            tt(sq2[:, :, T:TC], x[:, :, :], x[:, :, :], mul, done=s["norm_sq"])
            for src, at, gain, shift in ((hh, 0, misc[:, 48:56], mods[:, 3, 0:8]), (x, T, gains[:, 4, :], mods[:, 2, 0:8])):
                i = inverse()
                for k in range(KT):
                    stt(hh[:, k, at:at + T], src[:, k, 0:T], gain[:, k:k + 1], i[:, 0:T], mul, mul)
                    ts(hh[:, k, at:at + T], hh[:, k, at:at + T], shift[:, k:k + 1], None, add,
                       done=s["normed"] if k == KT - 1 and at else s["dve_step"])
            v(dve.memset(m_pad[:, :, :, 0:1], 0.0))
            v(dve.memset(m_pad[:, :, :, 257:258], 0.0), sem("m_pad"))
            v(dve.memset(wp_i, 0.0))
            v(dve.memset(wp_f, 0.0))
            for d in range(2):
                v(dve.tensor_copy(wp_i[:, :, 32 * d:32 * d + 4], w_small[:, 0, :, 8 * d:8 * d + 4]))
                v(dve.tensor_copy(wp_f[:, :, 32 * d:32 * d + 4], w_small[:, 0, :, 8 * d + 4:8 * d + 8]))
                v(dve.tensor_copy(wp_f[:, :, 64 + 32 * d:64 + 32 * d + 8], w_small[:, 1, :, 8 * d:8 * d + 8]),
                  sem("small_w") if d else s["dve_step"])
            dve.wait_ge(sem("gate_z"), 1)
            ts(z_f, z_f, sgn, None, mul)
            stt(z_e, z_f, -1.0, z_f, mul, ALU.min, done=sem("gate_neg"))
            ts(z_f, z_f, 0.0, None, mx)
            ts(decay[:, 1:2], decay[:, 1:2], -1.0, None, mul)
            v(dve.memset(z_one, 1.0))
            dve.wait_ge(sem("gate_log"), 1)
            tt(z_sp, z_f, z_e, add)
            ts(z_e, z_sp, decay[:, 1:2], None, mul)

            def turn(dst, src, parts):
                for q in range(parts):
                    r = slice(32 * q, 32 * q + 32)
                    if q % 2 == 0:
                        v(dve.tensor_copy(dst[r, :], src[r, :]))
                    else:
                        v(dve.tensor_copy(dst[r, 0:T], src[r, 0:T][:, ::-1]))
                        v(dve.tensor_copy(dst[r, T:TC], src[r, T:TC][:, ::-1]))

            turn(z_inc, z_e, 4)
            turn(z_ir, z_i, 2)
            v(dve.tensor_tensor_scan(z_fs, z_one, z_inc, 0.0, mul, add))
            v(dve.tensor_tensor_scan(z_ms[0:64, :], z_inc[0:64, :], z_ir[0:64, :], 0.0, add, mx))
            turn(z_e, z_fs, 4)
            turn(z_f, z_ms, 2)
            tt(row_r[0:64, :], z_e[0:64, T:TC], z_f[0:64, T:TC], sub)
            v(dve.tensor_copy(row_r[64:P, :], z_e[64:P, T:TC]))
            v(dve.tensor_copy(row_m[0:64, :], z_f[0:64, T:TC]))
            tt(z_inc[0:64, :], z_i[0:64, :], z_e[0:64, :], sub)
            ts(z_inc[64:P, :], z_e[64:P, :], -1.0, None, mul, done=sem("gate_rows"))
            for dst in (col_c, col_dt):
                ps = take()
                took(dve.tensor_copy(dst, ps.rearrange("p (a b) -> p a b", a=4)))

            def mask(qm, half, ps):
                pv = ps.rearrange("p (a t) -> p a t", a=2)
                if half == 0:
                    v(dve.tensor_copy(qm[:, 0, 0:2, :], pv))
                    took(dve.tensor_copy(qm[:, 1, 0:2, :], pv))
                    return
                tt(qm[:, 0, 2, 0:P], pv[:, 0, 0:P], fwd, mul)
                v(dve.tensor_copy(qm[:, 0, 2, P:T], pv[:, 0, P:T]))
                v(dve.memset(qm[:, 0, 3, 0:P], 0.0))
                tt(qm[:, 0, 3, P:T], pv[:, 1, P:T], fwd, mul)
                tt(qm[:, 1, 2, 0:P], pv[:, 0, 0:P], bwd, mul)
                v(dve.memset(qm[:, 1, 2, P:T], 0.0))
                v(dve.tensor_copy(qm[:, 1, 3, 0:P], pv[:, 1, 0:P]))
                took(dve.tensor_tensor(qm[:, 1, 3, P:T], pv[:, 1, P:T], bwd, mul))

            def conv3(dst, pad, w, b, j, lat_only, done):
                if lat_only:
                    d_, p_ = dst[:, j, T:TC], lambda tap: pad[:, j, 1, tap:tap + T]
                else:
                    d_ = dst[:, j, :].rearrange("p (s t) -> p s t", s=2)
                    p_ = lambda tap: pad[:, j, :, tap:tap + T]
                ts(d_, p_(0), col(w, j), col(b, j), mul, add)
                stt(d_, p_(1), col(w, 8 + j), d_, mul, add)
                stt(d_, p_(2), col(w, 16 + j), d_, mul, add, done=done)

            for j in range(8):
                dve.wait_ge(sem("act_tile_taken"), marks["m_qk_in"] - 7 + j)
                conv3(m_x, m_pad, "m_conv_w_2", "m_conv_b_2", j, j < 4, sem("m_conv"))
            for j in range(8):
                dve.wait_ge(sem("m_tanh"), j + 1)
                if j < 4:
                    stt(m_x[:, j, T:TC], m_pad[:, j, 1, 0:T], 1.0, m_x[:, j, T:TC], add, mul, done=sem("m_qk"))
                else:
                    xs = m_x[:, j, :].rearrange("p (s t) -> p s t", s=2)
                    stt(xs, m_pad[:, j, :, 0:T], 1.0, xs, add, mul, done=sem("m_qk"))
            for hd in range(M_H):
                for half in range(2):
                    mask(m_qm, half, take())
                for d in range(2):
                    r = 32 * d + hd
                    ps = take()
                    for st in range(4):
                        ins = dve.tensor_scalar(m_e[:, d, st, :], ps[:, 0:T], col_c[:, st, r:r + 1], 0.0, add, ALU.min)
                        if st < 3:
                            v(ins)
                        else:
                            took(ins)
                    dve.wait_ge(sem("m_exp"), 2 * hd + d + 1)
                    stt(m_e[:, d], m_e[:, d], 0.25 * float(P) ** -0.5, m_qm[:, d], mul, mul, done=sem("m_w"))
                    ps = take()
                    tt(m_rc[:, 1, :], ps[:, T:TC], m_rc[:, 0, :], mx, done=sem("m_read"))
                    stt(m_rc[:, 1, :], ps[:, T:TC], -1.0, m_rc[:, 1, :], mul, mx)
                    v(dve.reciprocal(m_rc[:, 1, :], m_rc[:, 1, :]))
                    if d == 0:
                        took(dve.tensor_tensor(m_h[:, hd, :], ps[:, 0:T], m_rc[:, 1, :], mul))
                    else:
                        took(dve.tensor_tensor(m_rc[:, 1, :], ps[:, 0:T], m_rc[:, 1, :], mul))
                        tt(m_h[:, hd, :], m_h[:, hd, :], m_rc[:, 1, :], add)
                tt(m_rc[:, 2, :], m_h[:, hd, :], m_h[:, hd, :], mul, done=s["norm_sq"])
                i = inverse()
                stt(m_h[:, hd, :], m_h[:, hd, :], col("m_norm_g_2", hd), i[:, 0:T], mul, mul)
                stt(m_rc[:, 1, :], m_o[:, hd, :], 1.0, m_h[:, hd, :], add, mul)
                ts(y_m[:, hd, :], m_rc[:, 1, :], 0.5, None, mul)

            v(dve.memset(s_pad[:, :, :, 0:1], 0.0))
            v(dve.memset(s_pad[:, :, :, 257:258], 0.0), sem("s_pad"))
            l4 = lam_p.rearrange("p (a b) -> p a b", a=4)
            tt(l4[:, 0:4:2, :], l4[:, 0:4:2, :], l4[:, 1:4:2, :], mul)
            v(dve.tensor_reduce(misc[:, 40:42], l4[:, 0:4:2, :], AX, add), sem("a_lam"))
            dve.wait_ge(sem("act_tile_taken"), marks["a_in"])
            for j in range(8):
                n = T if j < 4 else TC
                q = a_q[:, j, :] if j < 4 else a_k[:, j - 4, :]
                tt(a_t[:, 0:n], q, q, mul, done=s["norm_sq"])
                i = inverse()
                stt(q, q, col("a_qnorm_g_2" if j < 4 else "a_knorm_g_2"), i[:, 0:n], mul, mul, done=sem("a_normed"))
                lat = q if j < 4 else q[:, T:TC]
                ps = take()
                took(dve.tensor_tensor(a_u[:, 0:T], ps[:, 0:T], sin, mul))
                tt(a_u[:, T:TC], lat, cos, mul)
                tt(lat, a_u[:, 0:T], a_u[:, T:TC], add, done=sem("a_rotated"))
            dve.wait_ge(sem("a_lam_exp"), 1)
            tt(misc[:, 44:45], misc[:, 43:44], misc[:, 42:43], sub)
            ts(misc[:, 44:45], misc[:, 44:45], -LAM_INIT, None, add)
            n = 0
            for hd in range(A_H):
                for t in range(TT):
                    for sub_, dst in enumerate((a_p0, a_p1)):
                        ps = take()
                        v(dve.tensor_reduce(a_st[:, sub_:sub_ + 1], ps, AX, mx))
                        ts(a_st[:, 2 + sub_:3 + sub_], a_st[:, sub_:sub_ + 1], -(SUB ** -0.5), None, mul)
                        if sub_ == 0 and n:
                            dve.wait_ge(sem("act_tile_taken"), marks["a_pt", n // 2 - 1])
                        took(dve.tensor_copy(dst, ps))
                        n += 1
                    dve.wait_ge(sem("a_exp"), n)
                    v(dve.reciprocal(a_st[:, 4:6], a_st[:, 4:6]))
                    tt(a_st[:, 5:6], a_st[:, 5:6], misc[:, 44:45], mul)
                    ts(a_p0, a_p0, a_st[:, 4:5], None, mul)
                    stt(a_p0, a_p1, a_st[:, 5:6], a_p0, mul, add, done=sem("a_p"))
                ps = take()
                took(dve.tensor_copy(a_o[:, hd, :], ps[:, 0:T]))
                tt(a_t[:, 0:T], a_o[:, hd, :], a_o[:, hd, :], mul, done=s["norm_sq"])
                i = inverse()
                stt(a_o[:, hd, :], a_o[:, hd, :], col("a_subln_g_2"), i[:, 0:T], mul, mul)
                ts(y_a[:, hd, :], a_o[:, hd, :], 1.0 - LAM_INIT, None, mul)

            dve.wait_ge(sem("act_tile_taken"), marks["s_in"])
            for j in range(8):
                conv3(s_x, s_pad, "s_conv_w_2", "s_conv_b_2", j, False, sem("s_conv"))
            for j in range(8):
                dve.wait_ge(sem("s_tanh"), j + 1)
                xs = s_x[:, j, :].rearrange("p (s t) -> p s t", s=2)
                stt(xs, s_pad[:, j, :, 0:T], 1.0, xs, add, mul, done=sem("s_xbc"))
            n = 0
            for hd in range(S_H):
                if hd % 4 == 0:
                    for half in range(2):
                        mask(s_qm, half, take())
                for d in range(2):
                    r = 64 + 32 * d + hd
                    ps = take()
                    if n:
                        if d == 1:
                            dve.wait_ge(sem("s_w_used"), hd + 1)
                    for st in range(4):
                        ins = dve.tensor_scalar(s_e[:, st, :], ps[:, 0:T], col_c[:, st, r:r + 1], 0.0, add, ALU.min)
                        if st < 3:
                            v(ins)
                        else:
                            took(ins)
                    n += 1
                    dve.wait_ge(sem("s_exp"), n)
                    for st in range(4):
                        stt(s_e[:, st, :], s_e[:, st, :], col_dt[:, st, r:r + 1], s_qm[:, d, st, :], mul, mul,
                            done=sem("s_w") if st == 3 else s["dve_step"])
                rows = slice(64 * (hd % 2), 64 * (hd % 2) + 64)
                ps = take()
                took(dve.tensor_scalar(s_y[rows, hd // 2, :], ps[rows, 0:T], 0.125, None, mul))
            ts(misc[:, 56:60], d_skip[:, :], 0.5, None, mul)
            for j in range(4):
                stt(s_y[:, j, :], s_x[:, j, T:TC], misc[:, 56 + j:57 + j], s_y[:, j, :], mul, add,
                    done=sem("s_y") if j == 3 else s["dve_step"])
            dve.wait_ge(sem("s_ztanh"), 1)
            stt(s_z, s_qm[:, 0], 1.0, s_z, add, mul)
            stt(s_y, s_y, 0.5, s_z, mul, mul)
            for g in range(2):
                pair = s_y[:, 2 * g:2 * g + 2, :]
                tt(sq_s[:, 2 * g:2 * g + 2, :], pair, pair, mul, done=s["norm_sq"])
            for g in range(2):
                i = inverse()
                for j in (2 * g, 2 * g + 1):
                    stt(y_s[:, j, :], s_y[:, j, :], col("s_norm_g_2", j), i[:, 0:T], mul, mul,
                        done=sem("branches") if j == 3 else s["dve_step"])

            for half in range(2):
                for br in range(3):
                    for j in range(4):
                        ps = take()
                        if (half, br, j) == (0, 0, 0):
                            dve.wait_ge(sem("act_tile_taken"), marks["merge"])
                        dst = g_acc[:, 4 * half + j, :]
                        o = dst if br == 0 else g_tmp
                        ins = dve.scalar_tensor_tensor(out=o, in0=g_th[:, 8 * br + 4 * half + j, :], scalar=1.0, in1=ps[:, 0:T], op0=add,
                                                       op1=mul)
                        took(ins)
                        if br == 1:
                            tt(dst, dst, g_tmp, add)
                        if br == 2:
                            tt(dst, dst, g_tmp, add)
                            ts(dst, dst, 0.5, None, mul, done=sem("merged"))
            residual(mods[:, 2, 16:24])

            v(dve.memset(f_pad[:, :, 0:1], 0.0))
            v(dve.memset(f_pad[:, :, 257:258], 0.0))
            v(dve.memset(f_zero, 0.0))
            norm(gains[:, 5, :], mods[:, 2, 24:32], sq_=f_sq)
            for i in range(FF_PAIRS):
                for j in range(4):
                    f = 2 * i + j % 2 + (22 if j >= 2 else 0)
                    dve.wait_ge(sem("act_tile_taken"), marks["ff"] + 4 * i + j + 1)
                    ts(f_c[:, j, :], f_pad[:, j, 0:T], col("ffn_conv_w_2", f), None, mul)
                    stt(f_c[:, j, :], f_pad[:, j, 1:1 + T], col("ffn_conv_w_2", 44 + f), f_c[:, j, :], mul, add)
                    stt(f_c[:, j, :], f_pad[:, j, 2:2 + T], col("ffn_conv_w_2", 88 + f), f_c[:, j, :], mul, add,
                        done=sem("ff_conv"))
                for q in range(2):
                    dve.wait_ge(sem("ff_tanh"), 2 * i + q + 1)
                    stt(f_c[:, 2 + q, :], f_th[:, q, :], 1.0, f_c[:, 2 + q, :], add, mul)
                    if i >= 2:
                        dve.wait_ge(sem("ff_down_used"), i - 1)
                    stt(f_he[:, i % 2, q, :], f_c[:, 2 + q, :], 0.5, f_c[:, q, :], mul, mul, done=sem("ff_hidden"))
            dve.wait_ge(sem("ff_done"), 1)
            for k in range(KT):
                stt(x[:, k, :], banks[4 + k // 2][:, (k % 2) * T:(k % 2 + 1) * T], mods[:, 2, 40 + k:41 + k],
                    x[:, k, :], mul, add, done=sem("x_final") if k == KT - 1 else s["dve_step"])


_INS = ['x', 'c', 'gla_w_in', 'gla_w_gate_up', 'gla_b_gate', 'gla_norm_g', 'gla_w_out', 'lru_w_in', 'lru_conv_w',
        'lru_conv_b', 'lru_w_r', 'lru_b_r', 'lru_w_i', 'lru_b_i', 'lru_lambda', 'lru_w_out', 'router_w',
        'router_bias', 'moe_w_gate', 'moe_w_up', 'moe_w_down', 'norm_mix_g', 'norm_ffn_g', 'ada_w', 'ada_b',
        'final_norm_g', 'c_2', 'ctx_2', 'c_ctx_2', 'w_mod_2', 'b_mod_2', 'norm1_g_2', 'norm2_g_2', 'w_in_2',
        'm_conv_w_2', 'm_conv_b_2', 'm_igate_b_2', 'm_fgate_b_2', 'm_norm_g_2', 'a_qnorm_g_2', 'a_knorm_g_2',
        'a_lambda_2', 'a_subln_g_2', 's_conv_w_2', 's_conv_b_2', 's_dt_bias_2', 's_a_log_2', 's_d_2', 's_norm_g_2',
        'w_branch_m_2', 'w_branch_a_2', 'w_branch_s_2', 'w_out_2', 'w_up_2', 'ffn_conv_w_2', 'w_down_2']


def kernel(**inputs):
    import numpy as _np
    import concourse.bacc as _bacc
    from concourse import mybir as _mybir
    from concourse.bass_utils import run_bass_kernel_spmd as _run

    nc = _bacc.Bacc("TRN2", target_bir_lowering=False, num_devices=1)
    arrays, args = {}, {}
    inputs = dict(inputs, consts=constants())
    for name in _INS + ["consts"]:
        a = _np.ascontiguousarray(inputs[name])
        arrays[f"in_{name}_dram"] = a
        args[name] = nc.dram_tensor(f"in_{name}_dram", a.shape, _mybir.dt.from_np(a.dtype), kind="ExternalInput").ap()
    out = nc.dram_tensor("out_0_dram", (1, T, D), F32, kind="ExternalOutput").ap()
    build(nc, args, out)
    r = _run(nc, [arrays], core_ids=[0])
    return r.results[0]["out_0_dram"]
```

```python
import math
from contextlib import ExitStack

import numpy as np

import concourse.bass as bass
from concourse import mybir

F32 = mybir.dt.float32
F32R = mybir.dt.float32r
ALU = mybir.AluOpType
ACT = mybir.ActivationFunctionType
AX = mybir.AxisListType.X

P = 128
D = 1024
KT = D // P
T = 256
TT = T // P
TC = 512
EPS = 1e-6
EXPERTS, GROUPS, D_EXPERT = 16, 4, 512
FT = D_EXPERT // P
GLA_H, GLA_CHUNK, GLA_DV = 4, 64, 256
CHUNKS = T // GLA_CHUNK
M_H, A_H, S_H, SUB = 4, 4, 8, 64
D_FF = 2816
FF_PAIRS = D_FF // 256
LAM_INIT = 0.8 - 0.6 * math.exp(0.0)
U_QK, U_V, U_O, U_G, U_AQ, U_AK, U_AV, U_Z, U_XBC, U_DT, U_MERGE = np.cumsum(
    [0, 1024, 512, 512, 16, 512, 512, 512, 512, 1024, 16]).tolist()

PASSES = ((0, 0), (0, 1), (1, 0))
MOD_FIRST = 9
RING = 6
SLOT = 2048

C_ID, C_ONE, C_BLK, C_ROT, C_COS, C_SIN, C_FWD, C_BWD, C_SGN, C_EPS, C_IOTA, C_TRI, C_END = np.cumsum(
    [0, 128, 128, 128, 128, 256, 256, 128, 128, 1, 1, 4, 16]).tolist()


def constants():
    c = np.zeros((P, C_END), np.float32)
    c[:, C_ID:C_ID + P] = np.eye(P)
    c[:, C_ONE:C_ONE + P] = 1.0
    half = np.arange(P) // SUB
    c[:, C_BLK:C_BLK + P] = half[:, None] == half[None, :]
    inv_freq = np.float32(10000.0) ** (-np.arange(16, dtype=np.float32) / np.float32(16))
    t = np.arange(T)
    for p in range(P):
        f = p % SUB
        pos = (t // 64 if f < 32 else t % 64).astype(np.float32)
        ang = pos * inv_freq[f % 16]
        c[p, C_COS:C_COS + T] = np.cos(ang)
        c[p, C_SIN:C_SIN + T] = np.sin(ang)
        if f % 32 < 16:
            c[p + 16, C_ROT + p] = -1.0
        else:
            c[p - 16, C_ROT + p] = 1.0
    s = np.arange(P)
    c[:, C_FWD:C_FWD + P] = s[:, None] <= s[None, :]
    c[:, C_BWD:C_BWD + P] = s[:, None] >= s[None, :]
    c[:, C_SGN] = np.where(s < 64, -1.0, 1.0)
    c[:, C_EPS] = EPS
    c[:, C_IOTA:C_IOTA + 4] = [4, 3, 2, 1]
    c[:, C_TRI:C_TRI + 16] = (np.arange(4)[None, :] < np.arange(4)[:, None]).reshape(-1)
    return c


VECTORS = [("c", 8), ("c_2", 8), ("c_ctx_2", 8), ("ada_b", 96), ("b_mod_2", 48), ("norm_mix_g", 16),
           ("norm_ffn_g", 16), ("final_norm_g", 8), ("gla_b_gate", 4), ("gla_norm_g", 2), ("lru_conv_w", 32),
           ("lru_conv_b", 8), ("lru_b_r", 8), ("lru_b_i", 8), ("lru_lambda", 8), ("norm1_g_2", 8),
           ("norm2_g_2", 8), ("m_conv_w_2", 24), ("m_conv_b_2", 8), ("m_norm_g_2", 4), ("a_qnorm_g_2", 1),
           ("a_knorm_g_2", 1), ("a_subln_g_2", 1), ("s_conv_w_2", 24), ("s_conv_b_2", 8), ("s_norm_g_2", 4),
           ("ffn_conv_w_2", 132)]
COL, N_ROWS = {}, 0
for _name, _rows in VECTORS:
    COL[_name] = N_ROWS
    N_ROWS += _rows
ROW_TILES = -(-N_ROWS // P)


class Count:

    def __init__(self):
        self.at = {}

    def __call__(self, sem, by=1):
        self.at[sem.name] = self.at.get(sem.name, 0) + by
        return self.at[sem.name]

    def now(self, sem):
        return self.at.get(sem.name, 0)


class Banks:

    def __init__(self, banks, ready, taken):
        self.banks, self.ready, self.taken, self.n = banks, ready, taken, 0

    def fill(self, pe):
        if self.n >= len(self.banks):
            pe.wait_ge(self.taken, self.n - len(self.banks) + 1)
        return self.banks[self.n % len(self.banks)]

    def read(self, eng):
        eng.wait_ge(self.ready, self.n + 1)
        return self.banks[self.n % len(self.banks)]

    def step(self):
        self.n += 1


def build(nc, A, out):
    f_rows = "(k p) n -> p k n"

    def wide(w, col, kt=KT):
        n = SLOT // kt
        return w[:, col:col + n].rearrange(f_rows, p=P), kt, n

    def tall(w, row):
        return w[row:row + 256, :].rearrange(f_rows, p=P), 2, D

    ada, w_mod, gin, lin_w = A["ada_w"], A["w_mod_2"][0], A["gla_w_in"][0], A["lru_w_in"][0]
    win, w_up, w_down = A["w_in_2"][0], A["w_up_2"][0], A["w_down_2"][0]

    def plan():
        for j in range(24):
            yield "mod", wide(ada[0], 256 * j)
        for j in range(12):
            yield "gla_in", wide(gin, 256 * j)
        for j in range(4):
            yield "gla_out", wide(A["gla_w_out"][0], 256 * j)
        yield "moe", 0
        for j in (4, 5, 6, 7, 0, 1, 2, 3):
            yield "lru_in", wide(lin_w, 256 * j)
        for w in ("lru_w_r", "lru_w_i"):
            yield "lru_gate", (A[w][0].rearrange("b (k p) j -> p (b k) j", p=P), 8, 256)
        for j in range(4):
            yield "lru_out", wide(A["lru_w_out"][0], 256 * j)
        yield "moe", 1
        for col, n in ((U_QK, 4), (U_V, 2), (U_O, 2), (U_AQ, 2), (U_AK, 2), (U_AV, 2), (U_XBC, 4), (U_Z, 2),
                       (U_MERGE, 12)):
            for j in range(n):
                yield "u", wide(win, col + 256 * j)
        for half in range(2):
            for w in ("w_branch_m_2", "w_branch_a_2", "w_branch_s_2"):
                yield "branch", wide(A[w][0], 512 * half, 4)
        for j in range(4):
            yield "w_out", wide(A["w_out_2"][0], 256 * j)
        for j in range(FF_PAIRS):
            yield "ff_a", wide(w_up, 256 * j)
            yield "ff_g", wide(w_up, D_FF + 256 * j)
            if j:
                yield "ff_down", tall(w_down, 256 * (j - 1))
        yield "ff_down", tall(w_down, 256 * (FF_PAIRS - 1))

    SLOTS = []
    for what, load in plan():
        SLOTS += [(what, load)] if what != "moe" else [("moe", load)] * (6 * EXPERTS)
    freed = {}

    with ExitStack() as ctx:
        def sb(name, shape):
            return ctx.enter_context(nc.sbuf_tensor(name, shape, F32))

        sems = {}

        def sem(name):
            if name not in sems:
                sems[name] = ctx.enter_context(nc.semaphore(name))
            return sems[name]

        ring = sb("ring", [P, RING, SLOT])
        con = sb("con", [P, C_END])
        cols = sb("cols", [P, ROW_TILES * P])
        x = sb("x", [P, KT, T])
        hh = sb("hh", [P, KT, TC])
        mods = sb("mods", [P, 4, 48])
        gains = sb("gains", [P, 6, KT])
        cond = sb("cond", [P, 24])
        cond_t = sb("cond_t", [P, 24])
        lnt = sb("lnt", [P, TC])
        inv = sb("inv", [P, 4, TC])
        w_lr = sb("w_lr", [P, KT, 16])
        w_gate_up = sb("w_gate_up", [16, 512])
        w_router = sb("w_router", [P, KT, 16])
        router_b = sb("router_b", [P, 16])
        w_small = sb("w_small", [P, 2, KT, 16])
        bias_i = sb("bias_i", [64, 1])
        bias_f = sb("bias_f", [P, 1])
        decay = sb("decay", [P, 2])
        lam_p = sb("lam_p", [P, 256])
        d_skip = sb("d_skip", [P, 4])
        misc = sb("misc", [P, 64])
        ROOM = 28200
        PARTS = (2 * KT + 2 * FT) * T + 4 * SLOT
        FF_PARTS = PARTS + 2 * SLOT
        with nc.sbuf_tensor("parts", [P, FF_PARTS], F32R) as parts:
            h_parts = parts[:, 0:2 * KT * T].rearrange("p (o k t) -> p o k t", o=2, k=KT)
            he_parts = parts[:, 2 * KT * T:(2 * KT + 2 * FT) * T].rearrange("p (o f t) -> p o f t", o=2, f=FT)
            w_parts = parts[:, PARTS - 4 * SLOT:].rearrange("p (b o n) -> p b o n", b=3, o=2)
        work = sb("work", [P, ROOM])

        used = [0, 0]

        def room(*shape):
            n = int(np.prod(shape))
            a = work[:, used[0]:used[0] + n]
            used[0] += n
            assert used[0] <= ROOM, (used, shape)
            if len(shape) == 1:
                return a
            names = "abcd"[:len(shape)]
            return a.rearrange(f"p ({' '.join(names)}) -> p {' '.join(names)}",
                               **{k: v for k, v in zip(names, shape)})

        def again(at=0):
            used[0] = at

        ident, ones = con[:, C_ID:C_ID + P], con[:, C_ONE:C_ONE + P]
        blk, rot = con[:, C_BLK:C_BLK + P], con[:, C_ROT:C_ROT + P]
        cos, sin = con[:, C_COS:C_COS + T], con[:, C_SIN:C_SIN + T]
        fwd, bwd = con[:, C_FWD:C_FWD + P], con[:, C_BWD:C_BWD + P]
        one = con[:, C_ONE:C_ONE + 1]
        sgn, eps = con[:, C_SGN:C_SGN + 1], con[:, C_EPS:C_EPS + 1]

        def col(name, j=0, n=1):
            return cols[:, COL[name] + j:COL[name] + j + n]

        banks = [ctx.enter_context(nc.psum_tensor(f"bank{i}", [P, 512], F32))[:, :] for i in range(8)]

        def act_banks():
            return Banks(banks[:4], sem("act_tile_ready"), sem("act_tile_taken"))

        def dve_banks():
            return Banks(banks[4:], sem("dve_tile_ready"), sem("dve_tile_taken"))

        again()
        prow, x_in, c_in = room(ROW_TILES, P), room(TT, D), room(TT, D)
        again()
        sq = room(KT, TC)
        base = used[0]
        g_q, g_k, g_v, g_g = room(4, T), room(4, T), room(TT, D), room(8, T)
        g_z, g_l, g_kt, g_lr = room(4, T), room(4, T), room(TT, 512), room(T)
        g_s, g_o = room(CHUNKS, GLA_H, GLA_DV), room(8, T)
        g_gam = room(4, CHUNKS)
        again(PARTS)
        e_cb, e_th, e_t1, e_ct = room(EXPERTS, T), room(2, T), room(2, T), room(T)
        e_zero = room(512)
        r_s, r_sel, r_pair, r_gs, r_gm, r_key, r_km, r_oh = (room(32), room(32), room(8, 6), room(8), room(2), room(8),
                                                             room(2), room(8))
        r_a, r_b, r_rank, r_w, r_den, r_comb = room(8, 16), room(8, 16), room(32), room(32), room(2), room(32)
        side, side_acc, side_raw = room(2, KT, 384), room(9, P), room(EXPERTS, 9)
        side_tmp = lnt[:, 0:384]
        again(ROW_TILES * P + 2 * TT * D)
        mod_acc, mod_row = room(2, 2, P), room(12 * 256)
        again(0)
        l_g, l_xb, l_x, l_r, l_i, l_a, l_m, l_h = (room(8, T), room(8, T + 3), room(8, T), room(8, T), room(8, T),
                                                   room(8, T), room(8, T), room(8, T))
        again(0)
        y_m, y_a, y_s = room(4, T), room(4, T), room(4, T)
        row_r, row_m, col_c, col_dt = room(T), room(T), room(4, P), room(4, P)
        base2 = used[0]
        sq2 = room(KT, TC)
        again(base2)
        m_pad, m_x, m_v, m_o, m_h = room(8, 2, 258), room(8, TC), room(4, 512), room(4, T), room(4, T)
        m_qm, m_e, m_rc = room(2, 4, T), room(2, 4, T), room(4, T)
        upper = used[0]
        z_i, z_f, z_sp, z_e, z_inc, z_ir, z_fs, z_ms, z_one = [room(TC) for _ in range(9)]
        wp_i, wp_f = room(KT, 64), room(KT, P)
        again(upper)
        a_q, a_k, a_v = room(4, T), room(4, TC), room(4, 512)
        again(base2)
        a_t, a_u, a_p0, a_p1, a_pt, a_o, a_st = (room(TC), room(TC), room(TC), room(TC), room(2, 4, T), room(4, T),
                                                 room(8))
        s_pad, s_z, s_x, s_xt = room(8, 2, 258), room(4, T), room(8, TC), room(4, 512)
        assert used[0] <= upper
        again(base2)
        s_y, s_qm, s_e = room(4, T), room(2, 4, T), room(4, T)
        sq_s = s_qm[:, 1]
        again(base2)
        g_acc, g_tmp = room(8, T), room(T)
        again(upper)
        g_th = room(24, T)
        again(FF_PARTS)
        f_pad, f_c, f_th, f_he, f_zero = room(4, 258), room(4, T), room(2, T), room(2, 2, T), room(512)
        o_tok = room(TT, D)
        f_sq = room(KT, T)
        f_parts = he_parts.rearrange("p o (b q) t -> p o b q t", b=2)

        s = {n: sem(n) for n in (
            "params", "dve_step", "act_step", "pool_step", "columns", "cond", "norm_sq", "norm_inv", "normed",
            "mod_used", "x_in")}
        landed = [sem(f"slot_landed{i}") for i in range(RING)]
        ff_used = []
        SPLIT_AT = [(3, 4, None)] + [(3 * i + 2, 3 * i + 3, 3 * i + 4) for i in range(1, FF_PAIRS)]
        LOWS = 2 * 6 * EXPERTS
        marks = {}

        loads = [(con[:, :], A["consts"])]
        for name, rows in VECTORS:
            v = A[name]
            dims = len(v.shape)
            flat = v if dims == 1 else v.rearrange(" ".join("abcd"[:dims]) + " -> (" + " ".join("abcd"[:dims]) + ")")
            if name in ("a_qnorm_g_2", "a_knorm_g_2"):
                r = COL[name]
                for half in range(2):
                    loads.append((prow[r % P:r % P + 1, r // P, half * SUB:(half + 1) * SUB],
                                  flat.rearrange("(o n) -> o n", o=1)))
                continue
            m = flat.rearrange("(r n) -> r n", n=P)
            r, done = COL[name], 0
            while done < rows:
                k = min(rows - done, P - (r + done) % P)
                at = (r + done) % P
                loads.append((prow[at:at + k, (r + done) // P, :], m[done:done + k, :]))
                done += k
        loads.append((x_in, A["x"][0].rearrange("(t p) n -> p t n", p=P)))
        loads.append((c_in, A["ctx_2"][0].rearrange("(t p) n -> p t n", p=P)))
        loads.append((w_lr[:, :, :], gin[:, 3072:3088].rearrange(f_rows, p=P)))
        loads.append((w_gate_up[:, :], A["gla_w_gate_up"][0]))
        loads.append((w_router[:, :, :], A["router_w"].rearrange(f_rows, p=P)))
        loads.append((router_b[:, :], A["router_bias"].rearrange("(o n) -> o n", o=1).to_broadcast([P, 16])))
        loads.append((w_small[:, 0, :, :], win[:, U_G:U_G + 16].rearrange(f_rows, p=P)))
        loads.append((w_small[:, 1, :, :], win[:, U_DT:U_DT + 16].rearrange(f_rows, p=P)))
        loads.append((lam_p[:, :], A["a_lambda_2"][0].rearrange("(o a) b -> o (a b)", o=1).to_broadcast([P, 256])))
        column = lambda v, n: v.rearrange("(n o) -> n o", o=1)
        later = []
        for d in range(2):
            later.append((bias_i[32 * d:32 * d + 4, :], column(A["m_igate_b_2"][0, d], 4)))
            later.append((bias_f[32 * d:32 * d + 4, :], column(A["m_fgate_b_2"][0, d], 4)))
            later.append((bias_f[64 + 32 * d:64 + 32 * d + 8, :], column(A["s_dt_bias_2"][0, d], 8)))
            later.append((decay[64 + 32 * d:64 + 32 * d + 8, 0:1], column(A["s_a_log_2"][0, d], 8)))
        for hd in range(S_H):
            loads.append((d_skip[64 * (hd % 2):64 * (hd % 2) + 64, hd // 2:hd // 2 + 1],
                          A["s_d_2"][0, hd:hd + 1].rearrange("(n o) -> n o", o=1).to_broadcast([64, 1])))
        early, loads = loads[:4], loads[4:]
        n_params = 16 * (len(loads) + len(later))

        block = ctx.enter_context(nc.Block())

        @block.tensor
        def _(pe):
            c = Count()
            to_act, to_dve = act_banks(), dve_banks()
            slot = [0]

            def weights(what, kt):
                g = slot[0]
                assert SLOTS[g][0] == what, (g, SLOTS[g][0], what)
                pe.wait_ge(landed[g % RING], 16 * (g // RING + 1))
                slot[0] += 1
                return ring[:, g % RING, :].rearrange("p (k n) -> p k n", k=kt)

            def free_slot(sem_, value, back=1):
                freed[slot[0] - back] = (sem_, value)

            def close(banks_, ins):
                ins.then_inc(banks_.ready, 1)
                banks_.step()

            def linear(what, to, rhs, n, kt=KT, tiles=2, width=None):
                w = weights(what, kt)
                for m in range(tiles):
                    ps = to.fill(pe)
                    for k in range(kt):
                        ins = pe.matmul(ps[:, 0:n], w[:, k, m * P:(m + 1) * P], rhs(k), start=k == 0, stop=k == kt - 1)
                    close(to, ins)
                free_slot(to.ready, to.n)

            def by_token(what, to, src, tiles):
                w = weights(what, KT)
                for t in range(tiles):
                    ps = to.fill(pe)
                    for k in range(KT):
                        ins = pe.matmul(ps[:, 0:256], src(k, t), w[:, k, :], start=k == 0, stop=k == KT - 1)
                    close(to, ins)
                free_slot(to.ready, to.n)

            def norm_sum(parts, n, lhs=ones):
                pe.wait_ge(s["norm_sq"], c(s["norm_sq"]))
                ps = to_act.fill(pe)
                for k, part in enumerate(parts):
                    ins = pe.matmul(ps[:, 0:n], lhs, part, start=k == 0, stop=k == len(parts) - 1)
                close(to_act, ins)

            pe.wait_ge(sem("conditions"), 16 * len(early))
            ps = to_dve.fill(pe)
            close(to_dve, pe.transpose(ps[:, 0:24], prow[0:24, 0, :], ident[0:24, 0:24]))

            def inputs_turned():
                pe.wait_ge(s["params"], n_params)
                ps = to_dve.fill(pe)
                for i in range(ROW_TILES):
                    n = min(P, N_ROWS - i * P)
                    ins = pe.transpose(ps[:, i * P:i * P + n], prow[0:n, i, :], ident[0:n, 0:n])
                close(to_dve, ins)
                for src in (x_in, c_in):
                    for pair in range(4):
                        ps = to_dve.fill(pe)
                        for k in range(2):
                            for t in range(TT):
                                ins = pe.transpose(ps[:, (2 * k + t) * P:(2 * k + t + 1) * P],
                                                   src[:, t, (2 * pair + k) * P:(2 * pair + k + 1) * P], ident)
                        close(to_dve, ins)

            pe.wait_ge(sem("cond_ready"), 1)
            for i in range(12):
                slot[0] += 1
                w = weights("mod", KT)
                ps = to_act.fill(pe)
                for k in range(KT):
                    ins = pe.matmul(ps[0:1, 0:256], cond[:, k:k + 1], w[:, k, :], start=k == 0, stop=k == KT - 1)
                close(to_act, ins)
                free_slot(to_act.ready, to_act.n)
                pe.wait_ge(sem("mod_part"), i + 1)
                ps = to_dve.fill(pe)
                for m in range(2):
                    ins = pe.transpose(ps[:, m * P:(m + 1) * P], mod_acc[:, i % 2, m, :], ident)
                close(to_dve, ins)
                free_slot(sem("mod_part"), i + 1, back=2)
                if i == MOD_FIRST - 1:
                    inputs_turned()
            pe.wait_ge(to_act.taken, to_act.n)
            ps = to_dve.fill(pe)
            for m in range(24):
                ins = pe.transpose(ps[:, m:m + 1], mod_row[0:1, m * P:(m + 1) * P], ident[0:1, 0:1])
            close(to_dve, ins)

            h = lambda k: hh[:, k, T:TC]
            token = lambda k, t: hh[:, k, t * P:(t + 1) * P]
            hb = lambda k: hh[:, k, :]

            def norm(n=T):
                norm_sum([sq[:, k, 0:n] for k in range(KT)], n)
                pe.wait_ge(s["normed"], c(s["normed"]))

            norm()
            for j in range(4):
                linear("gla_in", to_act, h, T)
            for j in range(4):
                by_token("gla_in", to_act, lambda k, t: hh[:, k, T + t * P:T + (t + 1) * P], TT)
            for j in range(4):
                linear("gla_in", to_act, h, T)
            ps = to_act.fill(pe)
            for k in range(KT):
                ins = pe.matmul(ps[0:16, 0:T], w_lr[:, k, :], h(k), start=k == 0, stop=k == KT - 1)
            close(to_act, ins)
            pe.wait_ge(to_act.taken, to_act.n)
            for j in range(4):
                ps = to_dve.fill(pe)
                close(to_dve, pe.matmul(ps[:, 0:T], w_gate_up[:, j * P:(j + 1) * P], g_lr[0:16, :],
                                        start=True, stop=True))
            pe.wait_ge(sem("gla_kdec"), 1)
            for t in range(TT):
                ps = to_dve.fill(pe)
                for hd in range(GLA_H):
                    ins = pe.transpose(ps[:, hd * P:(hd + 1) * P], g_z[:, hd, t * P:(t + 1) * P], ident)
                close(to_dve, ins)
            pe.wait_ge(to_dve.taken, to_dve.n)
            for n in range(CHUNKS):
                rows = slice(64 * (n % 2), 64 * (n % 2) + 64)
                for pair in range(2):
                    ps = to_dve.fill(pe)
                    for q in range(2):
                        hd = 2 * pair + q
                        ins = pe.matmul(ps[:, q * 256:(q + 1) * 256], g_kt[rows, n // 2, hd * P:(hd + 1) * P],
                                        g_v[rows, n // 2, hd * 256:(hd + 1) * 256], start=True, stop=True)
                    close(to_dve, ins)
            pe.wait_ge(to_dve.taken, to_dve.n)
            for hd in range(GLA_H):
                ps = to_dve.fill(pe)
                for j in range(2):
                    for n in range(CHUNKS):
                        ins = pe.matmul(ps[:, j * T + n * 64:j * T + (n + 1) * 64], g_s[:, n, hd, j * P:(j + 1) * P],
                                        g_q[:, hd, n * 64:(n + 1) * 64], start=True, stop=True)
                close(to_dve, ins)
            for hd in range(GLA_H):
                norm_sum([sq[:, j, 0:T] for j in (2 * hd, 2 * hd + 1)], T)
            pe.wait_ge(sem("gla_y"), 1)
            for j in range(4):
                linear("gla_out", to_dve, lambda k: g_o[:, k, :], T)

            def side_sums(e):
                pe.wait_ge(sem("side_part"), e + 1)
                pe.wait_ge(sem("side_first"), e + 1)
                pe.wait_ge(sem("hidden_ready"), 4 * e + 3)
                for b in range(3):
                    for i in range(4 * b, min(4 * b + 4, 9)):
                        ins = pe.transpose(banks[b][:, (i - 4 * b) * P:(i - 4 * b + 1) * P], side_acc[:, i, :], ident)
                ins.then_inc(sem("side_turned"), 1)

            def experts(layer):
                norm()
                ps = to_act.fill(pe)
                for t in range(TT):
                    for k in range(KT):
                        ins = pe.matmul(ps[:, t * 16:(t + 1) * 16], hh[:, k, T + t * P:T + (t + 1) * P],
                                        w_router[:, k, :], start=k == 0, stop=k == KT - 1)
                close(to_act, ins)
                marks["logits", layer] = to_act.n
                pe.wait_ge(sem("combine"), layer + 1)
                ps = to_dve.fill(pe)
                for t in range(TT):
                    ins = pe.matmul(ps[0:16, t * P:(t + 1) * P], r_comb[:, t * 16:(t + 1) * 16], ident,
                                    start=True, stop=True)
                close(to_dve, ins)
                pe.wait_ge(to_dve.taken, to_dve.n)
                for e in range(0, EXPERTS, 2):
                    ps = to_dve.fill(pe)
                    for q in range(2):
                        ins = pe.matmul(ps[:, q * T:(q + 1) * T],
                                        ident[0:16, e + q:e + q + 1].to_broadcast([16, P]), e_ct[0:16, :],
                                        start=True, stop=True)
                    close(to_dve, ins)
                pe.wait_ge(to_dve.taken, to_dve.n)
                pe.wait_ge(to_act.taken, to_act.n)
                for b in range(4):
                    pe.matmul(banks[4 + b][:, :], e_zero[:, 0:P], e_zero[:, :], start=True, stop=False,
                              skip_group_check=True)
                pe.wait_ge(sem("h_split"), layer + 1)
                g0, first = slot[0], layer * EXPERTS
                gate_used, gu_ready, down_used = sem("gate_used"), sem("gate_up_ready"), sem("down_used")
                gu_taken, he_ready = sem("gate_up_taken"), sem("hidden_ready")

                def split_at(j, e, kt):
                    assert SLOTS[g0 + j][0] == "moe"
                    pe.wait_ge(sem("low_ready"), 6 * (e + first) + j + 1)
                    return [w_parts[:, j % 2, o].rearrange("p (k n) -> p k n", k=kt) for o in range(2)]

                with pe.Fori(0, EXPERTS // 2) as half_e:
                    for e in (2 * half_e, 2 * half_e + 1):
                        for pair in range(2):
                            for up in range(2):
                                w = split_at(2 * pair + up, e, KT)
                                for q in range(2):
                                    f = 2 * pair + q
                                    if not up:
                                        pe.wait_ge(gu_taken, 4 * (e + first) + f + 1)
                                        if layer == 0 and f < 3:
                                            pe.wait_ge(sem("side_read"), 3 * e + f + 1)
                                    for k in range(KT):
                                        for i, (a_, b_) in enumerate(PASSES):
                                            ins = pe.matmul(banks[f][:, up * T:(up + 1) * T],
                                                            w[a_][:, k, q * P:(q + 1) * P], h_parts[:, b_, k, :],
                                                            start=k == 0 and i == 0, stop=k == KT - 1 and i == 2)
                                    if up:
                                        ins.then_inc(gu_ready, 1)
                                if not up:
                                    ins.then_inc(gate_used, 1)
                        for pair in range(2):
                            w = split_at(4 + pair, e, 2)
                            for q in range(2):
                                f = 2 * pair + q
                                pe.wait_ge(he_ready, 4 * (e + first) + f + 1)
                                for m in range(KT):
                                    for a_, b_ in PASSES:
                                        ins = pe.matmul(banks[4 + m // 2][:, (m % 2) * T:(m % 2 + 1) * T],
                                                        w[a_][:, q, m * P:(m + 1) * P], he_parts[:, b_, f, :],
                                                        start=False, stop=False, skip_group_check=True)
                            ins.then_inc(down_used, 1)
                            if layer == 0 and pair == 0:
                                side_sums(e)
                for b in range(4):
                    ins = pe.matmul(banks[4 + b][:, :], e_zero[:, 0:P], e_zero[:, :], start=False, stop=True,
                                    skip_group_check=True)
                ins.then_inc(sem("experts_done"), 1)
                slot[0] += 6 * EXPERTS
                for j in range(6):
                    freed[slot[0] - 6 + j] = (sem("low_ready"), 6 * (first + EXPERTS - 1) + j + 1)

            experts(0)

            norm()
            for j in range(8):
                if j == 0:
                    marks["lru_xb"] = to_act.n
                linear("lru_in", to_act, h, T)
            pe.wait_ge(sem("lru_conv"), 8)
            for gate in range(2):
                w = weights("lru_gate", 8)
                for m in range(8):
                    ps = to_act.fill(pe)
                    for k in range(2):
                        b = m // 2
                        ins = pe.matmul(ps[:, 0:T], w[:, 2 * b + k, (m % 2) * P:(m % 2 + 1) * P],
                                        l_x[:, 2 * b + k, :], start=k == 0, stop=k == 1)
                    close(to_act, ins)
                free_slot(to_act.ready, to_act.n)
            marks["lru_gates"] = to_act.n
            pe.wait_ge(sem("lru_y"), 1)
            for j in range(4):
                linear("lru_out", to_dve, lambda k: l_h[:, k, :], T)
            experts(1)
            norm_sum([sq[:, k, 0:T] for k in range(KT)], T)

            norm_sum([sq2[:, k, 0:T] for k in range(KT)], T)
            norm_sum([sq2[:, k, T:TC] for k in range(KT)], T)
            pe.wait_ge(s["normed"], c(s["normed"]))
            pe.wait_ge(sem("small_w"), 1)
            for w, n in ((wp_i, 64), (wp_f, P)):
                ps = to_act.fill(pe)
                for k in range(KT):
                    ins = pe.matmul(ps[0:n, :], w[:, k, :], hb(k), start=k == 0, stop=k == KT - 1)
                close(to_act, ins)
            for j in range(2):
                linear("u", to_act, h, T)
            for j in range(2):
                linear("u", to_act, hb, TC)
            marks["m_qk_in"] = to_act.n
            pe.wait_ge(sem("gate_rows"), 1)
            for src in (z_inc, z_sp):
                ps = to_dve.fill(pe)
                for t in range(4):
                    ins = pe.transpose(ps[:, t * P:(t + 1) * P], src[:, t * P:(t + 1) * P], ident)
                close(to_dve, ins)
            for j in range(2):
                by_token("u", to_act, token, 4)
            for j in range(2):
                linear("u", to_act, h, T)
            values_in = to_act.n
            spare = ([lambda: linear("u", to_act, h, T)] * 2 + [lambda: linear("u", to_act, hb, TC)] * 2
                     + [lambda: by_token("u", to_act, token, 4)] * 2)
            for _ in range(4):
                spare.pop(0)()
            pe.wait_ge(to_act.taken, values_in)
            pe.wait_ge(sem("m_qk"), 8)

            def products(k_of, q_of):
                for half in range(2):
                    ps = to_dve.fill(pe)
                    for q in range(2):
                        ins = pe.matmul(ps[:, q * T:(q + 1) * T], k_of(2 * half + q), q_of, start=True, stop=True)
                    close(to_dve, ins)

            def spread(to, *rows):
                ps = to.fill(pe)
                for i, (tile, n, r) in enumerate(rows):
                    ins = pe.matmul(ps[:, i * T:(i + 1) * T], ident[0:n, r:r + 1].to_broadcast([n, P]), tile[0:n, :],
                                    start=True, stop=True)
                close(to, ins)

            def m_rows(n):
                hd, d = n // 2, n % 2
                if d == 0:
                    products(lambda st: m_x[:, 4 + hd, st * P:(st + 1) * P], m_x[:, hd, T:TC])
                spread(to_dve, (row_r, P, 32 * d + hd))
                marks["m_row", n] = to_dve.n
                spread(to_act, (row_m, 64, 32 * d + hd))

            m_rows(0)
            for hd in range(M_H):
                for d in range(2):
                    if 2 * hd + d + 1 < 2 * M_H:
                        m_rows(2 * hd + d + 1)
                    if spare:
                        spare.pop(0)()
                    pe.wait_ge(sem("m_w"), c(sem("m_w")))
                    ps = to_dve.fill(pe)
                    for st in range(4):
                        pe.matmul(ps[:, 0:T], m_v[:, st, hd * P:(hd + 1) * P], m_e[:, d, st, :],
                                  start=st == 0, stop=st == 3)
                    for st in range(4):
                        ins = pe.matmul(ps[:, T:TC], ones, m_e[:, d, st, :], start=st == 0, stop=st == 3)
                    close(to_dve, ins)
                norm_sum([m_rc[:, 2, :]], T)

            marks["a_in"] = to_act.n
            spare = [lambda: linear("u", to_act, hb, TC)] * 4 + [lambda: linear("u", to_act, h, T)] * 2
            pe.wait_ge(to_act.taken, to_act.n)
            for j in range(8):
                n = T if j < 4 else TC
                norm_sum([a_t[:, 0:n]], n, blk)
                pe.wait_ge(sem("a_normed"), c(sem("a_normed")))
                src = a_q[:, j, :] if j < 4 else a_k[:, j - 4, T:TC]
                ps = to_dve.fill(pe)
                close(to_dve, pe.matmul(ps[:, 0:T], rot, src, start=True, stop=True))
            pe.wait_ge(sem("a_rotated"), 8)
            for hd in range(A_H):
                for t in range(TT):
                    for sub in range(2):
                        rows = slice(SUB * sub, SUB * sub + SUB)
                        ps = to_dve.fill(pe)
                        close(to_dve, pe.matmul(ps[:, :], a_q[rows, hd, t * P:(t + 1) * P], a_k[rows, hd, :],
                                                start=True, stop=True))
                        marks["a_score", 4 * hd + 2 * t + sub] = to_dve.n
                    if spare:
                        spare.pop(0)()
                    pe.wait_ge(sem("a_p"), c(sem("a_p")))
                    ps = to_act.fill(pe)
                    for st in range(4):
                        ins = pe.transpose(ps[:, st * P:(st + 1) * P], a_p0[:, st * P:(st + 1) * P], ident)
                    close(to_act, ins)
                    marks["a_pt", 2 * hd + t] = to_act.n
                pe.wait_ge(to_act.taken, to_act.n)
                ps = to_dve.fill(pe)
                for st in range(4):
                    ins = pe.matmul(ps[:, 0:T], a_v[:, st, hd * P:(hd + 1) * P], a_pt[:, hd % 2, st, :],
                                    start=st == 0, stop=st == 3)
                close(to_dve, ins)
                norm_sum([a_t[:, 0:T]], T)

            marks["s_in"] = to_act.n
            spare = [lambda: linear("u", to_act, h, T)] * 12
            for _ in range(4):
                spare.pop(0)()
            pe.wait_ge(sem("s_xbc"), 8)
            for t in range(4):
                ps = to_act.fill(pe)
                for j in range(4):
                    ins = pe.transpose(ps[:, j * P:(j + 1) * P], s_x[:, j, t * P:(t + 1) * P], ident)
                close(to_act, ins)
            for hd in range(S_H):
                if hd % 4 == 0:
                    g = hd // 4
                    products(lambda st: s_x[:, 4 + g, st * P:(st + 1) * P], s_x[:, 6 + g, T:TC])
                if hd == 0:
                    pe.wait_ge(to_act.taken, to_act.n)
                rows = slice(64 * (hd % 2), 64 * (hd % 2) + 64)
                for d in range(2):
                    spread(to_dve, (row_r, P, 64 + 32 * d + hd))
                    marks["s_row", 2 * hd + d] = to_dve.n
                for d in range(2):
                    if spare and hd:
                        spare.pop(0)()
                    pe.wait_ge(sem("s_w"), c(sem("s_w")))
                    if d == 0:
                        ps = to_dve.fill(pe)
                    for st in range(4):
                        ins = pe.matmul(ps[rows, 0:T], s_xt[:, st, hd * 64:(hd + 1) * 64], s_e[:, st, :],
                                        start=st == 0 and d == 0, stop=st == 3 and d == 1)
                    if d == 0:
                        ins.then_inc(sem("s_w_used"), 1)
                close(to_dve, ins)
            for g in range(2):
                norm_sum([sq_s[:, 2 * g, :], sq_s[:, 2 * g + 1, :]], T)

            pe.wait_ge(sem("branches"), 1)
            marks["merge"] = to_act.n
            for half in range(2):
                for y in (y_m, y_a, y_s):
                    linear("branch", to_dve, lambda k: y[:, k, :], T, kt=4, tiles=4)
            pe.wait_ge(sem("merged"), 8)
            for j in range(4):
                linear("w_out", to_dve, lambda k: g_acc[:, k, :], T)

            norm_sum([f_sq[:, k, 0:T] for k in range(KT)], T)
            pe.wait_ge(s["normed"], c(s["normed"]))
            pe.wait_ge(to_dve.taken, to_dve.n)
            for b in range(4):
                pe.matmul(banks[4 + b][:, :], f_zero[:, 0:P], f_zero[:, :], start=True, stop=False,
                          skip_group_check=True)

            marks["ff"] = to_act.n
            ff_used.clear()
            pe.wait_ge(sem("h_split"), 3)

            def split(what, kt):
                g, n = slot[0], len(ff_used)
                assert SLOTS[g][0] == what
                pe.wait_ge(sem("low_ready"), LOWS + n + 1)
                freed[g] = (sem("low_ready"), LOWS + n + 1)
                slot[0] += 1
                return [w_parts[:, n % 3, o].rearrange("p (k n) -> p k n", k=kt) for o in range(2)]

            def up(what):
                w = split(what, KT)
                for m in range(2):
                    ps = to_act.fill(pe)
                    for k in range(KT):
                        for i, (a_, b_) in enumerate(PASSES):
                            ins = pe.matmul(ps[:, 0:T], w[a_][:, k, m * P:(m + 1) * P], h_parts[:, b_, k, :],
                                            start=k == 0 and i == 0, stop=k == KT - 1 and i == 2)
                    close(to_act, ins)
                ff_used.append((to_act.ready, to_act.n))

            def down(i):
                w = split("ff_down", 2)
                pe.wait_ge(sem("ff_hidden"), 2 * i + 2)
                for q in range(2):
                    for m in range(KT):
                        for a_, b_ in PASSES:
                            ins = pe.matmul(banks[4 + m // 2][:, (m % 2) * T:(m % 2 + 1) * T],
                                            w[a_][:, q, m * P:(m + 1) * P], f_parts[:, b_, i % 2, q, :],
                                            start=False, stop=False, skip_group_check=True)
                ins.then_inc(sem("ff_down_used"), 1)
                ff_used.append((sem("ff_down_used"), i + 1))

            for i in range(FF_PAIRS):
                up("ff_a")
                up("ff_g")
                if i:
                    down(i - 1)
            down(FF_PAIRS - 1)
            for b in range(4):
                ins = pe.matmul(banks[4 + b][:, :], f_zero[:, 0:P], f_zero[:, :], start=False, stop=True,
                                skip_group_check=True)
            ins.then_inc(sem("ff_done"), 1)

            pe.wait_ge(sem("x_final"), 1)
            for t in range(TT):
                for half in range(2):
                    ps = to_act.fill(pe)
                    for k in range(4):
                        ins = pe.transpose(ps[:, k * P:(k + 1) * P], x[:, 4 * half + k, t * P:(t + 1) * P], ident)
                    close(to_act, ins)
                marks["out", t] = to_act.n
            assert slot[0] == len(SLOTS)

        @block.sync
        def _(sp):
            def reuse(g):
                if g >= RING:
                    sm, value = freed[g - RING]
                    sp.wait_ge(sm, value)

            def load(g, src, kt, n):
                sp.dma_start(ring[:, g % RING, :].rearrange("p (k n) -> p k n", k=kt), src).then_inc(landed[g % RING], 16)

            def expert(layer, g0, e, j, sl):
                if j < 4:
                    w = A["moe_w_gate"] if j % 2 == 0 else A["moe_w_up"]
                    c0 = 256 * (j // 2)
                    src = w[layer, sl, :, c0:c0 + 256].rearrange("o (k p) n -> p (o k) n", p=P)
                    load(g0 + j, src, KT, 256)
                else:
                    r0 = 256 * (j - 4)
                    src = A["moe_w_down"][layer, sl, r0:r0 + 256, :].rearrange("o (k p) n -> p (o k) n", p=P)
                    load(g0 + j, src, 2, D)

            g = 0
            while g < len(SLOTS):
                what, arg = SLOTS[g]
                if what != "moe":
                    reuse(g)
                    load(g, *arg)
                    g += 1
                    continue
                for j in range(6):
                    reuse(g + j)
                    expert(arg, g, 0, j, slice(0, 1))
                first = arg * EXPERTS
                with sp.Fori(1, EXPERTS) as e:
                    for j in range(6):
                        sp.wait_ge(sem("low_ready"), 6 * e + (6 * (first - 1) + j + 1))
                        expert(arg, g, e, j, bass.ds(e, 1))
                g += 6 * EXPERTS
            for t in range(TT):
                sp.wait_ge(sem("act_tile_taken"), marks["out", t])
                sp.dma_start(out[0, t * P:(t + 1) * P, :], o_tok[:, t, :]).then_inc(sem("stored"), 16)
            sp.wait_ge(sem("stored"), 16 * TT)

        @block.gpsimd
        def _(pool):
            def load(i, cols_):
                w = (ada[1], w_mod)[i]
                pool.dma_start(side[:, i], w[:, cols_].rearrange(f_rows, p=P)).then_inc(sem(f"side_landed{i}"), 16)

            def products(i, n):
                q, cnd = 2 * i, 16 * i
                acc = side_acc[:, 3 * q:3 * q + 3, :].rearrange("p m q -> p (m q)")
                pool.wait_ge(sem(f"side_landed{i}"), 16 * n)
                for k in range(KT):
                    scaled = acc if k == 0 else side_tmp
                    if k > 1:
                        pool.wait_ge(sem(f"side_sum{i}"), (KT - 1) * n + (k - KT))
                    pool.tensor_tensor(scaled, side[:, i, k, :],
                                       cond[:, cnd + k:cnd + k + 1].to_broadcast([P, 384]), ALU.mult)\
                        .then_inc(sem(f"side_scaled{i}"), 1)
                    pool.wait_ge(sem(f"side_scaled{i}"), KT * n + (k + 1 - KT))
                    if k:
                        pool.tensor_tensor(acc, acc, side_tmp, ALU.add).then_inc(sem(f"side_sum{i}"), 1)
                pool.wait_ge(sem(f"side_sum{i}"), (KT - 1) * n)

            pool.wait_ge(sem("combine"), 1)
            for i in range(2):
                load(i, slice(0, 384))
            products(0, 1)
            load(0, slice(384, 768))
            products(1, 1)
            pool.sem_inc(sem("side_part"), 1)
            pool.wait_ge(sem("side_first"), 1)
            load(1, slice(384, 768))
            with pool.Fori(1, EXPERTS - 1) as e:
                pool.wait_ge(sem("side_turned"), e)
                products(0, e + 1)
                load(0, bass.ds(e * 384 + 384, 384))
                products(1, e + 1)
                pool.sem_inc(sem("side_part"), 1)
                pool.wait_ge(sem("side_first"), e + 1)
                load(1, bass.ds(e * 384 + 384, 384))
            pool.wait_ge(sem("side_turned"), EXPERTS - 1)
            for i in range(2):
                products(i, EXPERTS)
            pool.sem_inc(sem("side_part"), 1)

        @block.scalar
        def _(act):
            c = Count()
            tiles = act_banks()

            def a(ins, done=s["act_step"]):
                ins.then_inc(done, 1)
                act.wait_ge(done, c(done))

            def take(dst, src=None, func=ACT.Identity, n=T, parts=P, done=None, **kw):
                ps = tiles.read(act)
                view = ps[0:parts, 0:n] if src is None else src(ps)
                act.activation(dst, view, func, **kw).then_inc(tiles.taken, 1)
                tiles.step()
                if done is not None:
                    act.wait_ge(tiles.taken, tiles.n)

            inv_n = [0]

            def inverse(count, n=T, at=0):
                ps = tiles.read(act)
                ins = act.activation(lnt[:, 0:n], ps[:, 0:n], ACT.Ln, bias=eps, scale=1.0 / count)
                ins.then_inc(tiles.taken, 1)
                tiles.step()
                act.wait_ge(tiles.taken, tiles.n)
                a(act.activation(inv[:, inv_n[0] % 4, at:at + n], lnt[:, 0:n], ACT.Exp, scale=-0.5), s["norm_inv"])
                inv_n[0] += 1

            for dst, src in early:
                act.dma_start(dst, src).then_inc(sem("conditions"), 16)
            act.wait_ge(sem("dve_tile_taken"), 1)
            a(act.activation(cond_t[:, :], cols[:, 0:24], ACT.Tanh, scale=0.5), sem("cond_tanh"))
            for dst, src in loads:
                act.dma_start(dst, src, allow_slow_non_contiguous=True).then_inc(s["params"], 16)
            act.wait_ge(sem("cleared"), 1)
            for dst, src in later:
                act.dma_start(dst, src, allow_slow_non_contiguous=True).then_inc(s["params"], 16)
            for i in range(12):
                take(mod_row[0:1, 256 * i:256 * (i + 1)], n=256, parts=1)
            act.wait_ge(s["params"], n_params)

            inverse(D)
            for j in range(4):
                take(g_q[:, j, :], scale=float(P) ** -0.5)
            for j in range(4):
                take(g_k[:, j, :])
            for j in range(4):
                for t in range(TT):
                    take(g_v[:, t, j * 256:(j + 1) * 256])
            for j in range(8):
                take(g_g[:, j, :])
            take(g_lr[0:16, :], parts=16, done=True)
            act.wait_ge(sem("gla_neg"), 1)
            a(act.activation(g_l, g_l, ACT.Exp))
            a(act.activation(g_l, g_l, ACT.Ln, bias=one), sem("gla_log"))
            act.wait_ge(sem("gla_rest"), 1)
            a(act.activation(g_gam, g_gam, ACT.Exp, scale=1.0 / 16))
            a(act.activation(g_l, g_l, ACT.Exp, scale=-1.0 / 16), sem("gla_decay"))
            a(act.activation(sq[:, :, T:TC], g_g, ACT.Tanh, scale=0.5), sem("gla_tanh"))
            for hd in range(GLA_H):
                inverse(GLA_DV)

            def experts(layer):
                inverse(D)
                take(r_s, n=32, func=ACT.Tanh, scale=0.5, done=True)
                first = layer * EXPERTS
                g0 = [i for i, sl in enumerate(SLOTS) if sl[0] == "moe"][layer * 6 * EXPERTS]
                gate_used, gu_ready, down_used = sem("gate_used"), sem("gate_up_ready"), sem("down_used")

                def high(j, e):
                    g = g0 + j
                    act.wait_ge(landed[g % RING], 16 * (g // RING + 1) + 16 * e)
                    n = e + first
                    if j == 0:
                        act.wait_ge(down_used, 2 * n + 1)
                    elif j == 1:
                        act.wait_ge(down_used, 2 * n + 2)
                    elif j % 2 == 0:
                        act.wait_ge(gate_used, 2 * n + j // 2)
                    else:
                        act.wait_ge(gu_ready, 4 * n + j - 1)
                    act.activation(w_parts[:, j % 2, 0, :], ring[:, g % RING, :], ACT.Identity)\
                        .then_inc(sem("high_ready"), 1)

                with act.Fori(0, EXPERTS // 2) as half_e:
                    for e in (2 * half_e, 2 * half_e + 1):
                        for j in range(6):
                            if j in (3, 5):
                                for f in (j - 3, j - 2):
                                    act.wait_ge(gu_ready, 4 * (e + first) + f + 1)
                                    act.wait_ge(sem("gate_up_taken"), 4 * (e + first) + f + 3)
                                    act.activation(e_th[:, f % 2, :], banks[f][:, 0:T], ACT.Tanh, scale=0.5)\
                                        .then_inc(sem("gate_tanh"), 1)
                            high(j, e)
                            if j in (3, 5):
                                for f in (j - 3, j - 2):
                                    act.wait_ge(sem("hidden_whole"), 4 * (e + first) + f + 1)
                                    act.activation(he_parts[:, 0, f, :], e_t1[:, f % 2, :], ACT.Identity)\
                                        .then_inc(sem("hidden_high"), 1)

            experts(0)

            inverse(D)
            for j in range(8):
                take(l_xb[:, j, 3:3 + T])
            for j in range(8):
                take(l_g[:, j, :])
            act.wait_ge(sem("lru_half"), 1)
            a(act.activation(misc[:, 8:16], misc[:, 16:24], ACT.Exp), sem("lru_z"))
            for dst, b in ((l_r, 24), (l_i, 32)):
                for m in range(8):
                    take(dst[:, m, :], func=ACT.Tanh, scale=0.5, bias=misc[:, b + m:b + m + 1])
            act.wait_ge(sem("lru_log"), 1)
            a(act.activation(l_a, l_r, ACT.Exp))
            a(act.activation(l_m, l_r, ACT.Tanh, scale=-1.0), sem("lru_am"))
            act.wait_ge(sem("lru_m2"), 1)
            a(act.activation(l_m, l_m, ACT.Sqrt), sem("lru_mult"))
            act.wait_ge(sem("lru_cubic"), 1)
            a(act.activation(l_r, l_r, ACT.Tanh, scale=0.7978845608028654), sem("lru_gelu"))
            experts(1)
            inverse(D)

            inverse(D)
            inverse(D)
            take(z_i[0:64, :], n=TC, parts=64, bias=bias_i[:, 0:1])
            take(z_f, n=TC, bias=bias_f[:, 0:1], done=True)
            a(act.activation(decay[:, 1:2], decay[:, 0:1], ACT.Exp), sem("gate_z"))
            act.wait_ge(sem("gate_neg"), 1)
            a(act.activation(z_e, z_e, ACT.Exp))
            a(act.activation(z_e, z_e, ACT.Ln, bias=one), sem("gate_log"))

            act.wait_ge(sem("m_pad"), 1)
            for j in range(4):
                take(m_pad[:, j, 1, 1:257])
            for j in range(4):
                take(m_pad[:, 4 + j, :, 1:257], lambda ps: ps.rearrange("p (s t) -> p s t", s=2))
            for j in range(2):
                for t in range(4):
                    take(m_v[:, t, j * 256:(j + 1) * 256])
            for j in range(4):
                take(m_o[:, j, :], func=ACT.Tanh, scale=0.5)

            def slot_of(dsts, **kw):
                return lambda: [take(dst, **kw) for dst in dsts]

            spare = ([slot_of([a_q[:, j, :] for j in (2 * i, 2 * i + 1)]) for i in range(2)]
                     + [slot_of([a_k[:, j, :] for j in (2 * i, 2 * i + 1)], n=TC) for i in range(2)]
                     + [slot_of([a_v[:, t, i * 256:(i + 1) * 256] for t in range(4)]) for i in range(2)])
            for j in range(8):
                act.wait_ge(sem("m_conv"), j + 1)
                if j < 4:
                    a(act.activation(m_pad[:, j, 1, 0:T], m_x[:, j, T:TC], ACT.Tanh, scale=0.5), sem("m_tanh"))
                else:
                    a(act.activation(m_pad[:, j, :, 0:T], m_x[:, j, :].rearrange("p (s t) -> p s t", s=2), ACT.Tanh,
                                     scale=0.5), sem("m_tanh"))
                if j % 2:
                    spare.pop(0)()
            def m_exps(n):
                if n >= 2:
                    act.wait_ge(sem("m_read"), n - 1)
                take(m_rc[:, 3 * (n % 2), :], func=ACT.Exp, scale=-1.0, done=True)
                act.wait_ge(sem("dve_tile_taken"), marks["m_row", n])
                a(act.activation(m_e[:, n % 2], m_e[:, n % 2], ACT.Exp), sem("m_exp"))

            m_exps(0)
            for hd in range(M_H):
                for d in range(2):
                    if 2 * hd + d + 1 < 2 * M_H:
                        m_exps(2 * hd + d + 1)
                    if spare:
                        spare.pop(0)()
                inverse(P)

            halves = lambda ps: ps.rearrange("p (s t) -> p s t", s=2)
            spare = ([slot_of([s_pad[:, j, :, 1:257] for j in (2 * i, 2 * i + 1)], src=halves) for i in range(4)]
                     + [slot_of([s_z[:, j, :] for j in (2 * i, 2 * i + 1)]) for i in range(2)])
            for j in range(8):
                inverse(SUB, T if j < 4 else TC)
            act.wait_ge(sem("a_lam"), 1)
            a(act.activation(misc[:, 42:44], misc[:, 40:42], ACT.Exp), sem("a_lam_exp"))
            n = 0
            for hd in range(A_H):
                for t in range(TT):
                    for sub, dst in enumerate((a_p0, a_p1)):
                        act.wait_ge(sem("dve_tile_taken"), marks["a_score", n])
                        a(act.activation(dst, dst, ACT.Exp, bias=a_st[:, 2 + sub:3 + sub], scale=SUB ** -0.5,
                                         accum_out=a_st[:, 4 + sub:5 + sub]), sem("a_exp"))
                        n += 1
                    if spare:
                        if len(spare) == 6:
                            act.wait_ge(sem("s_pad"), 1)
                        spare.pop(0)()
                    take(a_pt[:, hd % 2, :, t * P:(t + 1) * P], lambda ps: ps.rearrange("p (s t) -> p s t", s=4),
                         done=True)
                inverse(P)

            spare = [slot_of([g_th[:, j, :] for j in (2 * i, 2 * i + 1)], func=ACT.Tanh, scale=0.5)
                     for i in range(12)]
            for j in range(8):
                act.wait_ge(sem("s_conv"), j + 1)
                a(act.activation(s_pad[:, j, :, 0:T], s_x[:, j, :].rearrange("p (s t) -> p s t", s=2), ACT.Tanh,
                                 scale=0.5), sem("s_tanh"))
                if j % 2:
                    spare.pop(0)()
            for t in range(4):
                take(s_xt[:, t, :], n=512, done=True)
            for n in range(2 * S_H):
                act.wait_ge(sem("dve_tile_taken"), marks["s_row", n])
                a(act.activation(s_e, s_e, ACT.Exp), sem("s_exp"))
                if spare and n >= 2:
                    spare.pop(0)()
            act.wait_ge(sem("s_y"), 1)
            a(act.activation(s_qm[:, 0], s_z, ACT.Tanh, scale=0.5), sem("s_ztanh"))
            for g in range(2):
                inverse(256)

            inverse(D)

            ff0 = len(SLOTS) - 3 * FF_PAIRS

            def high(n):
                if n is None or n >= 3 * FF_PAIRS:
                    return
                g = ff0 + n
                act.wait_ge(landed[g % RING], 16 * (g // RING + 1))
                if n >= 3:
                    act.wait_ge(*ff_used[n - 3])
                act.activation(w_parts[:, n % 3, 0, :], ring[:, g % RING, :], ACT.Identity)\
                    .then_inc(sem("high_ready"), 1)

            for n in range(3):
                high(n)
            for i in range(FF_PAIRS):
                for j in range(4):
                    if i:
                        act.wait_ge(sem("ff_conv"), 4 * (i - 1) + j + 1)
                    take(f_pad[:, j, 1:257])
                    if j % 2:
                        high(SPLIT_AT[i][j // 2])
                for q in range(2):
                    act.wait_ge(sem("ff_conv"), 4 * i + 2 + q + 1)
                    a(act.activation(f_th[:, q, :], f_c[:, 2 + q, :], ACT.Tanh, scale=0.5), sem("ff_tanh"))
                high(SPLIT_AT[i][2])
            for t in range(TT):
                for half in range(2):
                    take(o_tok[:, t, half * 512:(half + 1) * 512], n=512, done=True)

        @block.vector
        def _(dve):
            c = Count()
            tiles = dve_banks()

            def v(ins, done=s["dve_step"]):
                ins.then_inc(done, 1)
                dve.wait_ge(done, c(done))

            def tt(o, i0, i1, op, done=s["dve_step"]):
                v(dve.tensor_tensor(o, i0, i1, op), done)

            def ts(o, i0, s1, s2, op0, op1=None, done=s["dve_step"]):
                if op1 is None:
                    v(dve.tensor_scalar(o, i0, s1, None, op0), done)
                else:
                    v(dve.tensor_scalar(o, i0, s1, s2, op0, op1), done)

            def stt(o, i0, sc, i1, op0, op1, done=s["dve_step"]):
                v(dve.scalar_tensor_tensor(out=o, in0=i0, scalar=sc, in1=i1, op0=op0, op1=op1), done)

            def take():
                return tiles.read(dve)

            def took(ins):
                ins.then_inc(tiles.taken, 1)
                tiles.step()
                dve.wait_ge(tiles.taken, tiles.n)

            inv_n = [0]

            def inverse():
                dve.wait_ge(s["norm_inv"], inv_n[0] + 1)
                i = inv[:, inv_n[0] % 4, :]
                inv_n[0] += 1
                return i

            mul, add, sub, mx = ALU.mult, ALU.add, ALU.subtract, ALU.max

            for tile in (bias_i[:, :], bias_f[:, :]):
                v(dve.memset(tile, 0.0))
            v(dve.memset(decay[:, :], 0.0), sem("cleared"))
            ps = take()
            took(dve.tensor_copy(cols[:, 0:24], ps[:, 0:24]))
            dve.wait_ge(sem("cond_tanh"), 1)
            stt(cond[:, :], cond_t[:, :], 1.0, cols[:, 0:24], add, mul)
            ts(cond[:, :], cond[:, :], 0.5, None, mul, done=sem("cond_ready"))

            def inputs_turned():
                dve.wait_ge(s["params"], n_params)
                ps = take()
                took(dve.tensor_copy(cols[:, 0:N_ROWS], ps[:, 0:N_ROWS]))
                for dst in (x[:, :, :], hh[:, :, 0:T]):
                    for pair in range(4):
                        ps = take()
                        took(dve.tensor_copy(dst[:, 2 * pair:2 * pair + 2, :], ps.rearrange("p (k t) -> p k t", k=2)))

            def mod_sum(i):
                ps = take()
                took(dve.tensor_reduce(mods[:, 0, 4 * i:4 * i + 2], ps[:, 0:256].rearrange("p (m q) -> p m q", m=2),
                                       AX, add))

            for i in range(12):
                j = 2 * i
                assert SLOTS[j][0] == "mod"
                dve.wait_ge(landed[j % RING], 16 * (j // RING + 1))
                w = ring[:, j % RING, :].rearrange("p (k n) -> p k n", k=KT)
                acc = mod_acc[:, i % 2].rearrange("p m q -> p (m q)")
                ts(acc, w[:, 0, :], cond[:, 0:1], None, mul)
                for k in range(1, KT):
                    stt(acc, w[:, k, :], cond[:, k:k + 1], acc, mul, add,
                        done=sem("mod_part") if k == KT - 1 else s["dve_step"])
                if i and i != MOD_FIRST:
                    mod_sum(i - 1)
                if i == MOD_FIRST - 1:
                    mod_sum(i)
                    inputs_turned()
            mod_sum(11)
            ps = take()
            took(dve.tensor_copy(mods[:, 0, :].rearrange("p (i b m) -> p i b m", b=2, m=2)[:, :, 1, :],
                                 ps[:, 0:24].rearrange("p (i m) -> p i m", m=2)))
            tt(mods[:, 0, :], mods[:, 0, :], col("ada_b", 0, 48), add)

            def all_gains(which):
                for i, (layer, at, g) in enumerate(
                        ((0, 8, col("norm_mix_g", 0, 8)), (0, 32, col("norm_ffn_g", 0, 8)),
                         (1, 8, col("norm_mix_g", 8, 8)), (1, 32, col("norm_ffn_g", 8, 8)),
                         (2, 8, col("norm1_g_2", 0, 8)), (2, 32, col("norm2_g_2", 0, 8)))):
                    if (layer == 0) == (which == 0):
                        stt(gains[:, i, :], mods[:, layer, at:at + 8], 1.0, g, add, mul)

            all_gains(0)

            def norm(gain, shift, sq_=None, src=x, at=T):
                q = sq if sq_ is None else sq_
                tt(q[:, :, 0:T], src[:, :, 0:T], src[:, :, 0:T], mul, done=s["norm_sq"])
                i = inverse()
                for k in range(KT):
                    stt(hh[:, k, at:at + T], src[:, k, 0:T], gain[:, k:k + 1], i[:, 0:T], mul, mul)
                    ts(hh[:, k, at:at + T], hh[:, k, at:at + T], shift[:, k:k + 1], None, add,
                       done=s["normed"] if k == KT - 1 else s["dve_step"])

            def residual(gate):
                for k in range(KT):
                    ps = take()
                    took(dve.scalar_tensor_tensor(out=x[:, k, :], in0=ps[:, 0:T], scalar=gate[:, k:k + 1],
                                                  in1=x[:, k, :], op0=mul, op1=add))

            norm(gains[:, 0, :], mods[:, 0, 0:8])
            for j in range(4):
                ps = take()
                took(dve.tensor_scalar(g_z[:, j, :], ps[:, 0:T], col("gla_b_gate", j), None, add))
            stt(g_l, g_z, -1.0, g_z, mul, ALU.min, done=sem("gla_neg"))
            ts(g_z, g_z, 0.0, None, ALU.min)
            dve.wait_ge(sem("gla_log"), 1)
            tt(g_z, g_z, g_l, sub)
            for j in range(4):
                for n in range(CHUNKS):
                    at = slice(n * 64, (n + 1) * 64)
                    v(dve.tensor_tensor_scan(g_l[:, j, at], ones[:, 0:64], g_z[:, j, at], 0.0, mul, add))
            v(dve.tensor_copy(g_gam, g_l[:, :, 63:T:64]))
            for j in range(4):
                lc = g_l[:, j, :].rearrange("p (n t) -> p n t", n=CHUNKS)
                tt(lc, lc, g_gam[:, j, :].unsqueeze(2).to_broadcast([P, CHUNKS, 64]), sub,
                   done=sem("gla_rest") if j == 3 else s["dve_step"])
            dve.wait_ge(sem("gla_decay"), 1)
            tt(g_z, g_k, g_l, mul, done=sem("gla_kdec"))
            for t in range(TT):
                ps = take()
                took(dve.tensor_copy(g_kt[:, t, :], ps))
            for n in range(CHUNKS):
                for pair in range(2):
                    ps = take()
                    for q in range(2):
                        hd = 2 * pair + q
                        u = ps[:, q * 256:(q + 1) * 256]
                        if n == 0:
                            ins = dve.tensor_copy(g_s[:, n, hd, :], u)
                        else:
                            ins = dve.scalar_tensor_tensor(out=g_s[:, n, hd, :], in0=g_s[:, n - 1, hd, :],
                                                           scalar=g_gam[:, hd, n:n + 1], in1=u, op0=mul, op1=add)
                        if q == 0:
                            v(ins)
                        else:
                            took(ins)
            for hd in range(GLA_H):
                ps = take()
                took(dve.tensor_copy(g_o[:, 2 * hd:2 * hd + 2, :], ps.rearrange("p (j t) -> p j t", j=2)))
                o = g_o[:, 2 * hd:2 * hd + 2, :]
                tt(sq[:, 2 * hd:2 * hd + 2, 0:T], o, o, mul, done=s["norm_sq"])
            dve.wait_ge(sem("gla_tanh"), 1)
            stt(g_g, sq[:, :, T:TC], 1.0, g_g, add, mul)
            for hd in range(GLA_H):
                i = inverse()
                for j in range(2):
                    o = g_o[:, 2 * hd + j, :]
                    stt(o, o, col("gla_norm_g", j), i[:, 0:T], mul, mul)
                    stt(o, o, 0.5, g_g[:, 2 * hd + j, :], mul, mul,
                        done=sem("gla_y") if (hd, j) == (3, 1) else s["dve_step"])
            residual(mods[:, 0, 16:24])

            def side_read(e):
                dve.wait_ge(sem("side_turned"), e + 1)
                for b in range(3):
                    n = (4, 4, 1)[b]
                    src = banks[b][:, 0:n * P].rearrange("p (m q) -> p m q", m=n)
                    dst = side_raw[:, bass.ds(e, 1), 4 * b:4 * b + n].rearrange("p o m -> p (o m)")
                    dve.tensor_reduce(dst, src, AX, add).then_inc(sem("side_read"), 1)

            def experts(layer):
                norm(gains[:, 2 * layer + 1, :], mods[:, layer, 24:32])
                v(dve.memset(e_zero, 0.0))
                v(dve.tensor_copy(h_parts[:, 0], hh[:, :, T:TC]))
                tt(h_parts[:, 1], hh[:, :, T:TC], h_parts[:, 0].bitcast(F32), sub, done=sem("h_split"))
                dve.wait_ge(sem("act_tile_taken"), marks["logits", layer])
                ts(r_s, r_s, 1.0, 0.5, add, mul)
                grp = r_sel.rearrange("p (g i) -> p g i", i=4)
                tt(r_sel.rearrange("p (t e) -> p t e", t=2), r_s.rearrange("p (t e) -> p t e", t=2),
                   router_b[:, :].unsqueeze(1).to_broadcast([P, 2, 16]), add)
                tt(r_pair[:, :, 0:3], grp[:, :, 0:3], grp[:, :, 1:4], add)
                tt(r_pair[:, :, 3:5], grp[:, :, 0:2], grp[:, :, 2:4], add)
                tt(r_pair[:, :, 5:6], grp[:, :, 0:1], grp[:, :, 3:4], add)
                v(dve.tensor_reduce(r_gs, r_pair, AX, mx))
                gs2 = r_gs.rearrange("p (t g) -> p t g", t=2)
                key2 = r_key.rearrange("p (t g) -> p t g", t=2)
                v(dve.tensor_reduce(r_gm, gs2, AX, mx))
                tt(key2, gs2, r_gm.unsqueeze(2).to_broadcast([P, 2, 4]), ALU.is_ge)
                tt(key2, key2, con[:, C_IOTA:C_IOTA + 4].unsqueeze(1).to_broadcast([P, 2, 4]), mul)
                v(dve.tensor_reduce(r_km, key2, AX, mx))
                tt(r_oh.rearrange("p (t g) -> p t g", t=2), key2, r_km.unsqueeze(2).to_broadcast([P, 2, 4]), ALU.is_equal)
                a4 = r_a.rearrange("p g (i j) -> p g i j", i=4)
                b4 = r_b.rearrange("p g (i j) -> p g i j", i=4)
                other = grp.unsqueeze(2).to_broadcast([P, 8, 4, 4])
                own = grp.unsqueeze(3).to_broadcast([P, 8, 4, 4])
                tt(a4, other, own, ALU.is_gt)
                tt(b4, other, own, ALU.is_equal)
                tt(r_b, r_b, con[:, C_TRI:C_TRI + 16].unsqueeze(1).to_broadcast([P, 8, 16]), mul)
                tt(r_a, r_a, r_b, add)
                v(dve.tensor_reduce(r_rank, a4, AX, add))
                rank = r_rank.rearrange("p (g i) -> p g i", i=4)
                stt(rank, rank, 1.5, r_oh.unsqueeze(2).to_broadcast([P, 8, 4]), ALU.is_lt, mul)
                tt(r_w, r_rank, r_s, mul)
                w2 = r_w.rearrange("p (t e) -> p t e", t=2)
                v(dve.tensor_reduce(r_den, w2, AX, add))
                v(dve.reciprocal(r_den, r_den))
                tt(r_comb.rearrange("p (t e) -> p t e", t=2), w2, r_den.unsqueeze(2).to_broadcast([P, 2, 16]), mul,
                   done=sem("combine"))
                ps = take()
                took(dve.tensor_copy(e_ct[0:16, :], ps[0:16, 0:T]))
                for e in range(0, EXPERTS, 2):
                    ps = take()
                    took(dve.tensor_copy(e_cb[:, e:e + 2, :], ps.rearrange("p (e t) -> p e t", e=2)))
                first = layer * EXPERTS
                if layer == 0:
                    for f in range(3):
                        dve.sem_inc(sem("side_read"), 1)
                if layer == 0:
                    for f in range(FT):
                        dve.sem_inc(sem("gate_up_taken"), 1)
                    for _ in range(2):
                        dve.sem_inc(sem("down_used"), 1)

                def low(j, e):
                    dve.wait_ge(sem("high_ready"), 6 * (e + first) + j + 1)
                    dve.tensor_tensor(w_parts[:, j % 2, 1, :], ring[:, (g0 + j) % RING, :],
                                      w_parts[:, j % 2, 0, :].bitcast(F32), sub).then_inc(sem("low_ready"), 1)

                def side_products(e, k0, k1):
                    acc = side_acc[:, 3:6, :].rearrange("p m q -> p (m q)")
                    if k0 == 0:
                        dve.wait_ge(sem("side_landed1"), 16 * (e + 1))
                    for k in range(k0, k1):
                        w, cnd = side[:, 1, k, :], cond[:, 8 + k:9 + k]
                        if k == 0:
                            ins = dve.tensor_scalar(acc, w, cnd, None, mul)
                        else:
                            dve.wait_ge(sem("side_step"), (KT - 1) * e + k)
                            ins = dve.scalar_tensor_tensor(out=acc, in0=w, scalar=cnd, in1=acc, op0=mul, op1=add)
                        ins.then_inc(sem("side_step" if k < KT - 1 else "side_first"), 1)

                def hidden(f, e):
                    n = 4 * (e + first)
                    dve.wait_ge(sem("gate_tanh"), n + (f + 1))
                    t1 = e_t1[:, f % 2, :]
                    dve.scalar_tensor_tensor(out=t1, in0=e_th[:, f % 2, :], scalar=1.0, in1=banks[f][:, 0:T],
                                             op0=add, op1=mul).then_inc(sem("silu2"), 1)
                    dve.wait_ge(sem("silu2"), n + (f + 1))
                    dve.scalar_tensor_tensor(out=t1, in0=t1, scalar=0.5, in1=banks[f][:, T:TC], op0=mul,
                                             op1=mul).then_inc(sem("gate_up_taken"), 1)
                    dve.wait_ge(sem("gate_up_taken"), n + (f + 5))
                    dve.tensor_tensor(t1, t1, e_cb[:, bass.ds(e, 1), :].rearrange("p o t -> p (o t)"),
                                      mul).then_inc(sem("hidden_whole"), 1)

                def hidden_low(f, e):
                    dve.wait_ge(sem("hidden_high"), 4 * (e + first) + f + 1)
                    dve.tensor_tensor(he_parts[:, 1, f, :], e_t1[:, f % 2, :], he_parts[:, 0, f, :].bitcast(F32),
                                      sub).then_inc(sem("hidden_ready"), 1)
                    if f % 2:
                        dve.wait_ge(sem("hidden_ready"), 4 * (e + first) + f + 1)

                g0 = [i for i, sl in enumerate(SLOTS) if sl[0] == "moe"][layer * 6 * EXPERTS]
                with dve.Fori(0, EXPERTS // 2) as half_e:
                    for e in (2 * half_e, 2 * half_e + 1):
                        for j in range(6):
                            if j in (3, 5):
                                for f in (j - 3, j - 2):
                                    hidden(f, e)
                            low(j, e)
                            if j in (3, 5):
                                for f in (j - 3, j - 2):
                                    hidden_low(f, e)
                            if layer == 0 and j in (1, 2, 3):
                                side_products(e, *((), (0, 3), (3, 6), (6, 8))[j])
                        if layer == 0:
                            side_read(e)
                if layer == 0:
                    dve.wait_ge(sem("side_read"), 3 * EXPERTS + 3)
                    raw = side_raw
                    for which in range(3):
                        b = col("b_mod_2", 0, 48) if which else col("ada_b", 48, 48)
                        tt(mods[:, 1 + which, :].rearrange("p (e m) -> p e m", m=3),
                           raw[:, :, 3 * which:3 * which + 3], b.rearrange("p (e m) -> p e m", m=3), add)
                    all_gains(1)
                    stt(misc[:, 48:56], mods[:, 3, 8:16], 1.0, col("norm1_g_2", 0, 8), add, mul)
                dve.wait_ge(sem("experts_done"), layer + 1)
                for k in range(KT):
                    stt(x[:, k, :], banks[4 + k // 2][:, (k % 2) * T:(k % 2 + 1) * T],
                        mods[:, layer, 40 + k:41 + k], x[:, k, :], mul, add)

            experts(0)

            norm(gains[:, 2, :], mods[:, 1, 0:8])
            v(dve.memset(l_xb[:, :, 0:3], 0.0))
            lam8, z8 = col("lru_lambda", 0, 8), misc[:, 8:16]
            ts(misc[:, 24:32], col("lru_b_r", 0, 8), 0.5, None, mul)
            ts(misc[:, 32:40], col("lru_b_i", 0, 8), 0.5, None, mul)
            stt(misc[:, 16:24], lam8, -1.0, lam8, mul, ALU.min, done=sem("lru_half"))
            dve.wait_ge(sem("lru_z"), 1)
            s8, q8 = misc[:, 56:64], misc[:, 16:24]
            ts(s8, z8, 2.0, None, add)
            v(dve.reciprocal(s8, s8))
            tt(s8, s8, z8, mul)
            tt(q8, s8, s8, mul)
            ts(z8, q8, 1.0 / 17, None, mul)
            for k in range(7, 0, -1):
                stt(z8, z8, 1.0 / (2 * k + 1), q8, add, mul)
            stt(z8, z8, 1.0, s8, add, mul)
            ts(s8, lam8, -1.0, 0.0, mul, mx)
            stt(s8, z8, 2.0, s8, mul, add)
            ts(s8, s8, -4.0, None, mul)
            for j in range(8):
                dve.wait_ge(sem("act_tile_taken"), marks["lru_xb"] + j + 1)
                ts(l_x[:, j, :], l_xb[:, j, 0:T], col("lru_conv_w", j), col("lru_conv_b", j), mul, add)
                for tap in range(1, 4):
                    stt(l_x[:, j, :], l_xb[:, j, tap:tap + T], col("lru_conv_w", 8 * tap + j), l_x[:, j, :], mul, add,
                        done=sem("lru_conv") if tap == 3 else s["dve_step"])
            dve.wait_ge(sem("act_tile_taken"), marks["lru_gates"])
            for j in range(8):
                ts(l_r[:, j, :], l_r[:, j, :], 1.0, s8[:, j:j + 1], add, mul,
                   done=sem("lru_log") if j == 7 else s["dve_step"])
            stt(l_x, l_i, 1.0, l_x, add, mul)
            dve.wait_ge(sem("lru_am"), 1)
            tt(l_i, l_a, l_a, mul)
            stt(l_m, l_i, 1.0, l_m, add, mul, done=sem("lru_m2"))
            tt(l_i, l_g, l_g, mul)
            ts(l_i, l_i, 0.044715, 1.0, mul, add)
            tt(l_r, l_i, l_g, mul, done=sem("lru_cubic"))
            dve.wait_ge(sem("lru_mult"), 1)
            stt(l_x, l_x, 0.5, l_m, mul, mul)
            for j in range(8):
                v(dve.tensor_tensor_scan(l_h[:, j, :], l_a[:, j, :], l_x[:, j, :], 0.0, mul, add))
            dve.wait_ge(sem("lru_gelu"), 1)
            stt(l_g, l_r, 1.0, l_g, add, mul)
            stt(l_h, l_h, 0.5, l_g, mul, mul, done=sem("lru_y"))
            residual(mods[:, 1, 16:24])
            experts(1)

            tt(sq[:, :, 0:T], x[:, :, :], x[:, :, :], mul, done=s["norm_sq"])
            i = inverse()
            for k in range(KT):
                stt(x[:, k, :], x[:, k, :], col("final_norm_g", k), i[:, 0:T], mul, mul)

            tt(sq2[:, :, 0:T], hh[:, :, 0:T], hh[:, :, 0:T], mul, done=s["norm_sq"])
            tt(sq2[:, :, T:TC], x[:, :, :], x[:, :, :], mul, done=s["norm_sq"])
            for src, at, gain, shift in ((hh, 0, misc[:, 48:56], mods[:, 3, 0:8]), (x, T, gains[:, 4, :], mods[:, 2, 0:8])):
                i = inverse()
                for k in range(KT):
                    stt(hh[:, k, at:at + T], src[:, k, 0:T], gain[:, k:k + 1], i[:, 0:T], mul, mul)
                    ts(hh[:, k, at:at + T], hh[:, k, at:at + T], shift[:, k:k + 1], None, add,
                       done=s["normed"] if k == KT - 1 and at else s["dve_step"])
            v(dve.memset(m_pad[:, :, :, 0:1], 0.0))
            v(dve.memset(m_pad[:, :, :, 257:258], 0.0), sem("m_pad"))
            v(dve.memset(wp_i, 0.0))
            v(dve.memset(wp_f, 0.0))
            for d in range(2):
                v(dve.tensor_copy(wp_i[:, :, 32 * d:32 * d + 4], w_small[:, 0, :, 8 * d:8 * d + 4]))
                v(dve.tensor_copy(wp_f[:, :, 32 * d:32 * d + 4], w_small[:, 0, :, 8 * d + 4:8 * d + 8]))
                v(dve.tensor_copy(wp_f[:, :, 64 + 32 * d:64 + 32 * d + 8], w_small[:, 1, :, 8 * d:8 * d + 8]),
                  sem("small_w") if d else s["dve_step"])
            dve.wait_ge(sem("gate_z"), 1)
            ts(z_f, z_f, sgn, None, mul)
            stt(z_e, z_f, -1.0, z_f, mul, ALU.min, done=sem("gate_neg"))
            ts(z_f, z_f, 0.0, None, mx)
            ts(decay[:, 1:2], decay[:, 1:2], -1.0, None, mul)
            v(dve.memset(z_one, 1.0))
            dve.wait_ge(sem("gate_log"), 1)
            tt(z_sp, z_f, z_e, add)
            ts(z_e, z_sp, decay[:, 1:2], None, mul)

            def turn(dst, src, parts):
                for q in range(parts):
                    r = slice(32 * q, 32 * q + 32)
                    if q % 2 == 0:
                        v(dve.tensor_copy(dst[r, :], src[r, :]))
                    else:
                        v(dve.tensor_copy(dst[r, 0:T], src[r, 0:T][:, ::-1]))
                        v(dve.tensor_copy(dst[r, T:TC], src[r, T:TC][:, ::-1]))

            turn(z_inc, z_e, 4)
            turn(z_ir, z_i, 2)
            v(dve.tensor_tensor_scan(z_fs, z_one, z_inc, 0.0, mul, add))
            v(dve.tensor_tensor_scan(z_ms[0:64, :], z_inc[0:64, :], z_ir[0:64, :], 0.0, add, mx))
            turn(z_e, z_fs, 4)
            turn(z_f, z_ms, 2)
            tt(row_r[0:64, :], z_e[0:64, T:TC], z_f[0:64, T:TC], sub)
            v(dve.tensor_copy(row_r[64:P, :], z_e[64:P, T:TC]))
            v(dve.tensor_copy(row_m[0:64, :], z_f[0:64, T:TC]))
            tt(z_inc[0:64, :], z_i[0:64, :], z_e[0:64, :], sub)
            ts(z_inc[64:P, :], z_e[64:P, :], -1.0, None, mul, done=sem("gate_rows"))
            for dst in (col_c, col_dt):
                ps = take()
                took(dve.tensor_copy(dst, ps.rearrange("p (a b) -> p a b", a=4)))

            def mask(qm, half, ps):
                pv = ps.rearrange("p (a t) -> p a t", a=2)
                if half == 0:
                    v(dve.tensor_copy(qm[:, 0, 0:2, :], pv))
                    took(dve.tensor_copy(qm[:, 1, 0:2, :], pv))
                    return
                tt(qm[:, 0, 2, 0:P], pv[:, 0, 0:P], fwd, mul)
                v(dve.tensor_copy(qm[:, 0, 2, P:T], pv[:, 0, P:T]))
                v(dve.memset(qm[:, 0, 3, 0:P], 0.0))
                tt(qm[:, 0, 3, P:T], pv[:, 1, P:T], fwd, mul)
                tt(qm[:, 1, 2, 0:P], pv[:, 0, 0:P], bwd, mul)
                v(dve.memset(qm[:, 1, 2, P:T], 0.0))
                v(dve.tensor_copy(qm[:, 1, 3, 0:P], pv[:, 1, 0:P]))
                took(dve.tensor_tensor(qm[:, 1, 3, P:T], pv[:, 1, P:T], bwd, mul))

            def conv3(dst, pad, w, b, j, lat_only, done):
                if lat_only:
                    d_, p_ = dst[:, j, T:TC], lambda tap: pad[:, j, 1, tap:tap + T]
                else:
                    d_ = dst[:, j, :].rearrange("p (s t) -> p s t", s=2)
                    p_ = lambda tap: pad[:, j, :, tap:tap + T]
                ts(d_, p_(0), col(w, j), col(b, j), mul, add)
                stt(d_, p_(1), col(w, 8 + j), d_, mul, add)
                stt(d_, p_(2), col(w, 16 + j), d_, mul, add, done=done)

            for j in range(8):
                dve.wait_ge(sem("act_tile_taken"), marks["m_qk_in"] - 7 + j)
                conv3(m_x, m_pad, "m_conv_w_2", "m_conv_b_2", j, j < 4, sem("m_conv"))
            for j in range(8):
                dve.wait_ge(sem("m_tanh"), j + 1)
                if j < 4:
                    stt(m_x[:, j, T:TC], m_pad[:, j, 1, 0:T], 1.0, m_x[:, j, T:TC], add, mul, done=sem("m_qk"))
                else:
                    xs = m_x[:, j, :].rearrange("p (s t) -> p s t", s=2)
                    stt(xs, m_pad[:, j, :, 0:T], 1.0, xs, add, mul, done=sem("m_qk"))
            def m_exponents(n):
                hd, d = n // 2, n % 2
                if d == 0:
                    for half in range(2):
                        mask(m_qm, half, take())
                r = 32 * d + hd
                ps = take()
                for st in range(4):
                    ins = dve.tensor_scalar(m_e[:, d, st, :], ps[:, 0:T], col_c[:, st, r:r + 1], 0.0, add, ALU.min)
                    if st < 3:
                        v(ins)
                    else:
                        took(ins)

            m_exponents(0)
            for hd in range(M_H):
                for d in range(2):
                    if d == 0:
                        m_exponents(2 * hd + 1)
                    dve.wait_ge(sem("m_exp"), 2 * hd + d + 1)
                    stt(m_e[:, d], m_e[:, d], 0.25 * float(P) ** -0.5, m_qm[:, d], mul, mul, done=sem("m_w"))
                    if d == 1 and hd + 1 < M_H:
                        m_exponents(2 * hd + 2)
                    ps = take()
                    tt(m_rc[:, 1, :], ps[:, T:TC], m_rc[:, 3 * d, :], mx, done=sem("m_read"))
                    stt(m_rc[:, 1, :], ps[:, T:TC], -1.0, m_rc[:, 1, :], mul, mx)
                    v(dve.reciprocal(m_rc[:, 1, :], m_rc[:, 1, :]))
                    if d == 0:
                        took(dve.tensor_tensor(m_h[:, hd, :], ps[:, 0:T], m_rc[:, 1, :], mul))
                    else:
                        took(dve.tensor_tensor(m_rc[:, 1, :], ps[:, 0:T], m_rc[:, 1, :], mul))
                        tt(m_h[:, hd, :], m_h[:, hd, :], m_rc[:, 1, :], add)
                tt(m_rc[:, 2, :], m_h[:, hd, :], m_h[:, hd, :], mul, done=s["norm_sq"])
                i = inverse()
                stt(m_h[:, hd, :], m_h[:, hd, :], col("m_norm_g_2", hd), i[:, 0:T], mul, mul)
                stt(m_rc[:, 1, :], m_o[:, hd, :], 1.0, m_h[:, hd, :], add, mul)
                ts(y_m[:, hd, :], m_rc[:, 1, :], 0.5, None, mul)

            v(dve.memset(s_pad[:, :, :, 0:1], 0.0))
            v(dve.memset(s_pad[:, :, :, 257:258], 0.0), sem("s_pad"))
            l4 = lam_p.rearrange("p (a b) -> p a b", a=4)
            tt(l4[:, 0:4:2, :], l4[:, 0:4:2, :], l4[:, 1:4:2, :], mul)
            v(dve.tensor_reduce(misc[:, 40:42], l4[:, 0:4:2, :], AX, add), sem("a_lam"))
            dve.wait_ge(sem("act_tile_taken"), marks["a_in"])
            for j in range(8):
                n = T if j < 4 else TC
                q = a_q[:, j, :] if j < 4 else a_k[:, j - 4, :]
                tt(a_t[:, 0:n], q, q, mul, done=s["norm_sq"])
                i = inverse()
                stt(q, q, col("a_qnorm_g_2" if j < 4 else "a_knorm_g_2"), i[:, 0:n], mul, mul, done=sem("a_normed"))
                lat = q if j < 4 else q[:, T:TC]
                ps = take()
                took(dve.tensor_tensor(a_u[:, 0:T], ps[:, 0:T], sin, mul))
                tt(a_u[:, T:TC], lat, cos, mul)
                tt(lat, a_u[:, 0:T], a_u[:, T:TC], add, done=sem("a_rotated"))
            dve.wait_ge(sem("a_lam_exp"), 1)
            tt(misc[:, 44:45], misc[:, 43:44], misc[:, 42:43], sub)
            ts(misc[:, 44:45], misc[:, 44:45], -LAM_INIT, None, add)
            n = 0
            for hd in range(A_H):
                for t in range(TT):
                    for sub_, dst in enumerate((a_p0, a_p1)):
                        ps = take()
                        v(dve.tensor_reduce(a_st[:, sub_:sub_ + 1], ps, AX, mx))
                        ts(a_st[:, 2 + sub_:3 + sub_], a_st[:, sub_:sub_ + 1], -(SUB ** -0.5), None, mul)
                        if sub_ == 0 and n:
                            dve.wait_ge(sem("act_tile_taken"), marks["a_pt", n // 2 - 1])
                        took(dve.tensor_copy(dst, ps))
                        n += 1
                    dve.wait_ge(sem("a_exp"), n)
                    v(dve.reciprocal(a_st[:, 4:6], a_st[:, 4:6]))
                    tt(a_st[:, 5:6], a_st[:, 5:6], misc[:, 44:45], mul)
                    ts(a_p0, a_p0, a_st[:, 4:5], None, mul)
                    stt(a_p0, a_p1, a_st[:, 5:6], a_p0, mul, add, done=sem("a_p"))
                ps = take()
                took(dve.tensor_copy(a_o[:, hd, :], ps[:, 0:T]))
                tt(a_t[:, 0:T], a_o[:, hd, :], a_o[:, hd, :], mul, done=s["norm_sq"])
                i = inverse()
                stt(a_o[:, hd, :], a_o[:, hd, :], col("a_subln_g_2"), i[:, 0:T], mul, mul)
                ts(y_a[:, hd, :], a_o[:, hd, :], 1.0 - LAM_INIT, None, mul)

            dve.wait_ge(sem("act_tile_taken"), marks["s_in"])
            for j in range(8):
                conv3(s_x, s_pad, "s_conv_w_2", "s_conv_b_2", j, False, sem("s_conv"))
            for j in range(8):
                dve.wait_ge(sem("s_tanh"), j + 1)
                xs = s_x[:, j, :].rearrange("p (s t) -> p s t", s=2)
                stt(xs, s_pad[:, j, :, 0:T], 1.0, xs, add, mul, done=sem("s_xbc"))
            n = 0
            for hd in range(S_H):
                if hd % 4 == 0:
                    for half in range(2):
                        mask(s_qm, half, take())
                for d in range(2):
                    r = 64 + 32 * d + hd
                    ps = take()
                    if n:
                        if d == 1:
                            dve.wait_ge(sem("s_w_used"), hd + 1)
                    for st in range(4):
                        ins = dve.tensor_scalar(s_e[:, st, :], ps[:, 0:T], col_c[:, st, r:r + 1], 0.0, add, ALU.min)
                        if st < 3:
                            v(ins)
                        else:
                            took(ins)
                    n += 1
                    dve.wait_ge(sem("s_exp"), n)
                    for st in range(4):
                        stt(s_e[:, st, :], s_e[:, st, :], col_dt[:, st, r:r + 1], s_qm[:, d, st, :], mul, mul,
                            done=sem("s_w") if st == 3 else s["dve_step"])
                rows = slice(64 * (hd % 2), 64 * (hd % 2) + 64)
                ps = take()
                took(dve.tensor_scalar(s_y[rows, hd // 2, :], ps[rows, 0:T], 0.125, None, mul))
            ts(misc[:, 56:60], d_skip[:, :], 0.5, None, mul)
            for j in range(4):
                stt(s_y[:, j, :], s_x[:, j, T:TC], misc[:, 56 + j:57 + j], s_y[:, j, :], mul, add,
                    done=sem("s_y") if j == 3 else s["dve_step"])
            dve.wait_ge(sem("s_ztanh"), 1)
            stt(s_z, s_qm[:, 0], 1.0, s_z, add, mul)
            stt(s_y, s_y, 0.5, s_z, mul, mul)
            for g in range(2):
                pair = s_y[:, 2 * g:2 * g + 2, :]
                tt(sq_s[:, 2 * g:2 * g + 2, :], pair, pair, mul, done=s["norm_sq"])
            for g in range(2):
                i = inverse()
                for j in (2 * g, 2 * g + 1):
                    stt(y_s[:, j, :], s_y[:, j, :], col("s_norm_g_2", j), i[:, 0:T], mul, mul,
                        done=sem("branches") if j == 3 else s["dve_step"])

            for half in range(2):
                for br in range(3):
                    for j in range(4):
                        ps = take()
                        if (half, br, j) == (0, 0, 0):
                            dve.wait_ge(sem("act_tile_taken"), marks["merge"])
                        dst = g_acc[:, 4 * half + j, :]
                        o = dst if br == 0 else g_tmp
                        ins = dve.scalar_tensor_tensor(out=o, in0=g_th[:, 8 * br + 4 * half + j, :], scalar=1.0, in1=ps[:, 0:T], op0=add,
                                                       op1=mul)
                        took(ins)
                        if br == 1:
                            tt(dst, dst, g_tmp, add)
                        if br == 2:
                            tt(dst, dst, g_tmp, add)
                            ts(dst, dst, 0.5, None, mul, done=sem("merged"))
            residual(mods[:, 2, 16:24])

            v(dve.memset(f_pad[:, :, 0:1], 0.0))
            v(dve.memset(f_pad[:, :, 257:258], 0.0))
            v(dve.memset(f_zero, 0.0))
            norm(gains[:, 5, :], mods[:, 2, 24:32], sq_=f_sq)
            v(dve.tensor_copy(h_parts[:, 0], hh[:, :, T:TC]))
            tt(h_parts[:, 1], hh[:, :, T:TC], h_parts[:, 0].bitcast(F32), sub, done=sem("h_split"))
            ff0 = len(SLOTS) - 3 * FF_PAIRS

            def low(n):
                if n is None or n >= 3 * FF_PAIRS:
                    return
                dve.wait_ge(sem("high_ready"), LOWS + n + 1)
                dve.tensor_tensor(w_parts[:, n % 3, 1, :], ring[:, (ff0 + n) % RING, :],
                                  w_parts[:, n % 3, 0, :].bitcast(F32), sub).then_inc(sem("low_ready"), 1)

            for n in range(3):
                low(n)
            for i in range(FF_PAIRS):
                for j in range(4):
                    f = 2 * i + j % 2 + (22 if j >= 2 else 0)
                    dve.wait_ge(sem("act_tile_taken"), marks["ff"] + 4 * i + j + 1)
                    ts(f_c[:, j, :], f_pad[:, j, 0:T], col("ffn_conv_w_2", f), None, mul)
                    stt(f_c[:, j, :], f_pad[:, j, 1:1 + T], col("ffn_conv_w_2", 44 + f), f_c[:, j, :], mul, add)
                    stt(f_c[:, j, :], f_pad[:, j, 2:2 + T], col("ffn_conv_w_2", 88 + f), f_c[:, j, :], mul, add,
                        done=sem("ff_conv"))
                    if j % 2:
                        low(SPLIT_AT[i][j // 2])
                for q in range(2):
                    dve.wait_ge(sem("ff_tanh"), 2 * i + q + 1)
                    stt(f_c[:, 2 + q, :], f_th[:, q, :], 1.0, f_c[:, 2 + q, :], add, mul)
                    if i >= 2:
                        dve.wait_ge(sem("ff_down_used"), i - 1)
                    stt(f_he[:, i % 2, q, :], f_c[:, 2 + q, :], 0.5, f_c[:, q, :], mul, mul)
                    v(dve.tensor_copy(f_parts[:, 0, i % 2, q, :], f_he[:, i % 2, q, :]))
                    tt(f_parts[:, 1, i % 2, q, :], f_he[:, i % 2, q, :], f_parts[:, 0, i % 2, q, :].bitcast(F32), sub,
                       done=sem("ff_hidden"))
                low(SPLIT_AT[i][2])
            dve.wait_ge(sem("ff_done"), 1)
            for k in range(KT):
                stt(x[:, k, :], banks[4 + k // 2][:, (k % 2) * T:(k % 2 + 1) * T], mods[:, 2, 40 + k:41 + k],
                    x[:, k, :], mul, add, done=sem("x_final") if k == KT - 1 else s["dve_step"])


_INS = ['x', 'c', 'gla_w_in', 'gla_w_gate_up', 'gla_b_gate', 'gla_norm_g', 'gla_w_out', 'lru_w_in', 'lru_conv_w',
        'lru_conv_b', 'lru_w_r', 'lru_b_r', 'lru_w_i', 'lru_b_i', 'lru_lambda', 'lru_w_out', 'router_w',
        'router_bias', 'moe_w_gate', 'moe_w_up', 'moe_w_down', 'norm_mix_g', 'norm_ffn_g', 'ada_w', 'ada_b',
        'final_norm_g', 'c_2', 'ctx_2', 'c_ctx_2', 'w_mod_2', 'b_mod_2', 'norm1_g_2', 'norm2_g_2', 'w_in_2',
        'm_conv_w_2', 'm_conv_b_2', 'm_igate_b_2', 'm_fgate_b_2', 'm_norm_g_2', 'a_qnorm_g_2', 'a_knorm_g_2',
        'a_lambda_2', 'a_subln_g_2', 's_conv_w_2', 's_conv_b_2', 's_dt_bias_2', 's_a_log_2', 's_d_2', 's_norm_g_2',
        'w_branch_m_2', 'w_branch_a_2', 'w_branch_s_2', 'w_out_2', 'w_up_2', 'ffn_conv_w_2', 'w_down_2']


def kernel(**inputs):
    import numpy as _np
    import concourse.bacc as _bacc
    from concourse import mybir as _mybir
    from concourse.bass_utils import run_bass_kernel_spmd as _run

    nc = _bacc.Bacc("TRN2", target_bir_lowering=False, num_devices=1)
    arrays, args = {}, {}
    inputs = dict(inputs, consts=constants())
    for name in _INS + ["consts"]:
        a = _np.ascontiguousarray(inputs[name])
        arrays[f"in_{name}_dram"] = a
        args[name] = nc.dram_tensor(f"in_{name}_dram", a.shape, _mybir.dt.from_np(a.dtype), kind="ExternalInput").ap()
    out = nc.dram_tensor("out_0_dram", (1, T, D), F32, kind="ExternalOutput").ap()
    build(nc, args, out)
    r = _run(nc, [arrays], core_ids=[0])
    return r.results[0]["out_0_dram"]
```
